# Optimizing a Trainium2 kernel written in Bass

```python
import math
import jax, jax.numpy as jnp
from jax import lax
import numpy as np
import jax
import jax.numpy as jnp

D_MODEL = 1024
BATCH = 1
SEQ = 512
DEPTH = 1

D_MIX = D_MODEL
EPS = 1e-6
ROPE_THETA = 10000.0

MLA_HEADS = 8
MLA_QK_NOPE = 64
MLA_QK_ROPE = 32
MLA_QK_DIM = MLA_QK_NOPE + MLA_QK_ROPE
MLA_V_DIM = 64
MLA_Q_RANK = 256
MLA_KV_RANK = 128
MLA_WIDTH = MLA_HEADS * MLA_V_DIM
ATTN_BLOCK = 128

RET_HEADS = 8
RET_HEAD_DIM = 64
RET_WIDTH = RET_HEADS * RET_HEAD_DIM
RET_CHUNK = 128

IN_SPLITS = (
    MLA_Q_RANK,
    MLA_KV_RANK,
    MLA_QK_ROPE,
    RET_WIDTH, RET_WIDTH, RET_WIDTH, RET_WIDTH,
)
IN_COLS = sum(IN_SPLITS)

PEER_HEADS = 8
PEER_N_KEYS = 128
PEER_N_EXPERTS = PEER_N_KEYS * PEER_N_KEYS
PEER_KEY_DIM = 256
PEER_HALF = PEER_KEY_DIM // 2
PEER_TOPK = 16
PEER_TOKEN_BLOCK = 128


def rms_norm(x, g):
    xf = x.astype(jnp.float32)
    y = xf * lax.rsqrt(jnp.mean(xf * xf, axis=-1, keepdims=True) + EPS)
    return (y * g.astype(jnp.float32)).astype(x.dtype)

def rope(x, positions):
    d = x.shape[-1]
    inv = ROPE_THETA ** (-jnp.arange(0, d, 2, dtype=jnp.float32) / d)
    ang = positions.astype(jnp.float32)[:, :, None, None] * inv
    cos, sin = jnp.cos(ang), jnp.sin(ang)
    x1, x2 = jnp.split(x.astype(jnp.float32), 2, axis=-1)
    out = jnp.concatenate([x1 * cos - x2 * sin, x1 * sin + x2 * cos], axis=-1)
    return out.astype(x.dtype)

def mla_group(q_lat, kv_lat, k_rope, positions, g_q_norm, w_uq, g_kv_norm, w_ukv):
    B, S, _ = q_lat.shape
    q = (rms_norm(q_lat, g_q_norm) @ w_uq).reshape(B, S, MLA_HEADS, MLA_QK_DIM)
    q_nope, q_rope = q[..., :MLA_QK_NOPE], q[..., MLA_QK_NOPE:]
    q_rope = rope(q_rope, positions)
    kv = (rms_norm(kv_lat, g_kv_norm) @ w_ukv).reshape(B, S, MLA_HEADS, MLA_QK_NOPE + MLA_V_DIM)
    k_nope, v = kv[..., :MLA_QK_NOPE], kv[..., MLA_QK_NOPE:]
    k_r = rope(k_rope[:, :, None, :], positions)
    k = jnp.concatenate([k_nope, jnp.broadcast_to(k_r, (B, S, MLA_HEADS, MLA_QK_ROPE))], axis=-1)
    qh = jnp.concatenate([q_nope, q_rope], axis=-1) * (MLA_QK_DIM ** -0.5)

    nb = S // ATTN_BLOCK
    q_blocks = qh.reshape(B, nb, ATTN_BLOCK, MLA_HEADS, MLA_QK_DIM).transpose(1, 0, 2, 3, 4)
    key_pos = jnp.arange(S)

    def one_block(args):
        qb, bi = args
        s = jnp.einsum('bqhd,bkhd->bhqk', qb, k).astype(jnp.float32)
        q_pos = bi * ATTN_BLOCK + jnp.arange(ATTN_BLOCK)
        mask = key_pos[None, :] <= q_pos[:, None]
        s = jnp.where(mask[None, None], s, -jnp.inf)
        p = jax.nn.softmax(s, axis=-1).astype(v.dtype)
        return jnp.einsum('bhqk,bkhd->bqhd', p, v)

    out = lax.map(one_block, (q_blocks, jnp.arange(nb)))
    return out.transpose(1, 0, 2, 3, 4).reshape(B, S, MLA_WIDTH)

def retention_group(q, k, v, gate, positions, g_ret_norm):
    B, S, _ = q.shape
    H, d, C = RET_HEADS, RET_HEAD_DIM, RET_CHUNK
    nc = S // C
    q = rope(q.reshape(B, S, H, d), positions)
    k = rope(k.reshape(B, S, H, d), positions) * (d ** -0.5)
    v = v.reshape(B, S, H, d)

    gamma = 1.0 - 2.0 ** (-5.0 - jnp.arange(H, dtype=jnp.float32))
    log_g = jnp.log(gamma)
    idx = jnp.arange(C, dtype=jnp.float32)
    diff = idx[:, None] - idx[None, :]
    dmask = jnp.where(diff >= 0, jnp.exp(log_g[:, None, None] * jnp.maximum(diff, 0.0)), 0.0)

    qc = q.reshape(B, nc, C, H, d).astype(jnp.float32)
    kc = k.reshape(B, nc, C, H, d).astype(jnp.float32)
    vc = v.reshape(B, nc, C, H, d).astype(jnp.float32)

    scores = jnp.einsum('bnihd,bnjhd->bnhij', qc, kc) * dmask
    y_inner = jnp.einsum('bnhij,bnjhd->bnihd', scores, vc)

    zeta = jnp.exp(log_g[:, None] * (C - 1.0 - idx))
    kv_chunk = jnp.einsum('bnjhk,hj,bnjhv->bnhkv', kc, zeta, vc)
    chunk_decay = jnp.exp(log_g * C)

    def step(state, kv_n):
        return state * chunk_decay[None, :, None, None] + kv_n, state

    _, prev = lax.scan(step, jnp.zeros((B, H, d, d), jnp.float32), kv_chunk.transpose(1, 0, 2, 3, 4))
    prev = prev.transpose(1, 0, 2, 3, 4)
    xi = jnp.exp(log_g[:, None] * (idx + 1.0))
    y_cross = jnp.einsum('bnihk,bnhkv,hi->bnihv', qc, prev, xi)

    y = (y_inner + y_cross).reshape(B, S, H, d)
    mu = jnp.mean(y, axis=-1, keepdims=True)
    var = jnp.mean(jnp.square(y - mu), axis=-1, keepdims=True)
    yn = ((y - mu) * lax.rsqrt(var + EPS)).reshape(B, S, RET_WIDTH) * g_ret_norm.astype(jnp.float32)
    return (jax.nn.silu(gate.astype(jnp.float32)) * yn).astype(gate.dtype)

def peer(h, w_query, sub_keys, expert_u, expert_v):
    B, S, D = h.shape
    T = B * S
    K = PEER_TOPK
    xt = h.reshape(T, D)
    q = (xt @ w_query).reshape(T, PEER_HEADS, 2, PEER_HALF)
    s = jnp.einsum('thpd,pkd->thpk', q, sub_keys).astype(jnp.float32)
    s_top, i_top = lax.top_k(s, K)
    cand = (s_top[:, :, 0, :, None] + s_top[:, :, 1, None, :]).reshape(T, PEER_HEADS, K * K)
    cand_idx = (i_top[:, :, 0, :, None] * PEER_N_KEYS + i_top[:, :, 1, None, :]).reshape(T, PEER_HEADS, K * K)
    best, pos = lax.top_k(cand, K)
    eidx = jnp.take_along_axis(cand_idx, pos, axis=-1)
    g = jax.nn.softmax(best, axis=-1)

    nb = T // PEER_TOKEN_BLOCK

    def one_block(args):
        xb, ib, gb = args
        u = expert_u[ib]
        a = jax.nn.gelu(jnp.einsum('thkd,td->thk', u, xb).astype(jnp.float32), approximate=False)
        w = (gb * a).astype(expert_v.dtype)
        return jnp.einsum('thk,thkd->td', w, expert_v[ib])

    out = lax.map(one_block, (xt.reshape(nb, PEER_TOKEN_BLOCK, D),
                              eidx.reshape(nb, PEER_TOKEN_BLOCK, PEER_HEADS, K),
                              g.reshape(nb, PEER_TOKEN_BLOCK, PEER_HEADS, K)))
    return out.reshape(B, S, D)

def first_inputs(seed: int = 0) -> dict:
    key = jax.random.key(seed)
    ks = jax.random.split(key, 20)
    L, D = DEPTH, D_MODEL
    nrm = lambda k, shape, scale: jax.random.normal(k, shape, jnp.float32) * scale
    gain = lambda k, shape: 1.0 + 0.02 * jax.random.normal(k, shape, jnp.float32)
    return {
        "x": nrm(ks[0], (BATCH, SEQ, D), 1.0),
        "c": nrm(ks[1], (BATCH, D), 1.0),
        "positions": jnp.broadcast_to(jnp.arange(SEQ, dtype=jnp.int32), (BATCH, SEQ)),
        "w_ada": nrm(ks[2], (L, D, 6 * D), D ** -0.5),
        "b_ada": nrm(ks[3], (L, 6 * D), 0.01),
        "g_norm1": gain(ks[4], (L, D)),
        "w_in": nrm(ks[5], (L, D, IN_COLS), D ** -0.5),
        "g_q_norm": gain(ks[6], (L, MLA_Q_RANK)),
        "w_uq": nrm(ks[7], (L, MLA_Q_RANK, MLA_HEADS * MLA_QK_DIM), MLA_Q_RANK ** -0.5),
        "g_kv_norm": gain(ks[8], (L, MLA_KV_RANK)),
        "w_ukv": nrm(ks[9], (L, MLA_KV_RANK, MLA_HEADS * (MLA_QK_NOPE + MLA_V_DIM)), MLA_KV_RANK ** -0.5),
        "g_ret_norm": gain(ks[10], (L, RET_WIDTH)),
        "w_out": nrm(ks[11], (L, MLA_WIDTH + RET_WIDTH, D), (MLA_WIDTH + RET_WIDTH) ** -0.5),
        "g_norm2": gain(ks[12], (L, D)),
        "w_query": nrm(ks[13], (L, D, PEER_HEADS * PEER_KEY_DIM), D ** -0.5),
        "sub_keys": nrm(ks[14], (L, 2, PEER_N_KEYS, PEER_HALF), PEER_HALF ** -0.5),
        "expert_u": nrm(ks[15], (L, PEER_N_EXPERTS, D), D ** -0.5),
        "expert_v": nrm(ks[16], (L, PEER_N_EXPERTS, D), 0.5),
        "g_final": gain(ks[17], (D,)),
    }

def first_block(x, c, positions, w_ada, b_ada, g_norm1, w_in, g_q_norm, w_uq, g_kv_norm, w_ukv,
              g_ret_norm, w_out, g_norm2, w_query, sub_keys, expert_u, expert_v, g_final):
    offs = np.cumsum(IN_SPLITS)[:-1].tolist()
    for l in range(DEPTH):
        mod = jax.nn.silu(c) @ w_ada[l] + b_ada[l]
        sh1, sc1, gt1, sh2, sc2, gt2 = [m[:, None, :] for m in jnp.split(mod, 6, axis=-1)]

        h = rms_norm(x, g_norm1[l]) * (1.0 + sc1) + sh1
        proj = h @ w_in[l]
        q_lat, kv_lat, k_rope, rq, rk, rv, rg = jnp.split(proj, offs, axis=-1)
        y_mla = mla_group(q_lat, kv_lat, k_rope, positions, g_q_norm[l], w_uq[l], g_kv_norm[l], w_ukv[l])
        y_ret = retention_group(rq, rk, rv, rg, positions, g_ret_norm[l])
        mixed = jnp.concatenate([y_mla.astype(x.dtype), y_ret.astype(x.dtype)], axis=-1) @ w_out[l]
        x = x + gt1 * mixed

        h2 = rms_norm(x, g_norm2[l]) * (1.0 + sc2) + sh2
        x = x + gt2 * peer(h2, w_query[l], sub_keys[l], expert_u[l], expert_v[l]).astype(x.dtype)
    return rms_norm(x, g_final)


DEPTH_2 = 2

N_MIXERS = 4
NORM_EPS = 1e-6
HEAD_DIM = 64
NEG_INF = -1e30

POOL_WINDOWS = (2, 4, 8, 16)
POOL_GROUP = D_MODEL // len(POOL_WINDOWS)

DIFF_HEADS = D_MODEL // (2 * HEAD_DIM)
DIFF_SUBLN_EPS = 1e-5
Q_BLOCK = 128

LRU_WIDTH = D_MODEL
LRU_BLOCKS = D_MODEL // HEAD_DIM
LRU_BLOCK_DIM = LRU_WIDTH // LRU_BLOCKS
LRU_CONV = 4
LRU_C = 8.0

DIL_GROUPS = ((128, 1), (512, 4), (2048, 16))
DIL_HEADS = D_MODEL // HEAD_DIM
DIL_WIDTH = DIL_HEADS * HEAD_DIM

D_FF = 2816
FFN_CONV = 3


def _n_layers_of(mixer):
    return len(range(mixer, DEPTH_2, N_MIXERS))

def _rms_norm(x, gain, eps=NORM_EPS):
    xf = x.astype(jnp.float32)
    y = xf * lax.rsqrt(jnp.mean(xf * xf, axis=-1, keepdims=True) + eps)
    return (y * gain.astype(jnp.float32)).astype(x.dtype)

def _rope_tables(positions, head_dim):
    inv = ROPE_THETA ** (-jnp.arange(0, head_dim, 2, dtype=jnp.float32) / head_dim)
    ang = positions.astype(jnp.float32)[:, None] * inv[None, :]
    return jnp.cos(ang), jnp.sin(ang)

def _rope(x, cos, sin):
    shape = (cos.shape[0],) + (1,) * (x.ndim - 3) + (cos.shape[1],)
    c, s = cos.reshape(shape), sin.reshape(shape)
    xf = x.astype(jnp.float32)
    x1, x2 = jnp.split(xf, 2, axis=-1)
    return jnp.concatenate([x1 * c - x2 * s, x2 * c + x1 * s], axis=-1).astype(x.dtype)

def _pool_mixer(x, w, scale):
    b, s, d = x.shape
    xf = x.astype(jnp.float32)
    cs = jnp.concatenate([jnp.zeros((b, 1, d), jnp.float32), lax.cumsum(xf, axis=1)], axis=1)
    t = jnp.arange(s)
    parts = []
    for g, win in enumerate(POOL_WINDOWS):
        lo = jnp.clip(t - win // 2, 0, s)
        hi = jnp.clip(t + win - win // 2, 0, s)
        sl = slice(g * POOL_GROUP, (g + 1) * POOL_GROUP)
        csg = cs[:, :, sl]
        mean = (csg[:, hi] - csg[:, lo]) / (hi - lo).astype(jnp.float32)[:, None]
        parts.append(mean - xf[:, :, sl])
    pooled = jnp.stack(parts, axis=2).astype(x.dtype)
    y = jnp.einsum('bsgc,gce->bsge', pooled, w).reshape(b, s, d)
    return y * scale

def _diff_attention(x, w_qkv, lq1, lk1, lq2, lk2, subln, w_o, cos, sin, layer_idx):
    b, s, _ = x.shape
    h, dh = DIFF_HEADS, HEAD_DIM
    q, k, v = jnp.split(x @ w_qkv, 3, axis=-1)
    q = _rope(q.reshape(b, s, 2 * h, dh), cos, sin).reshape(b, s, h, 2, dh) * (dh ** -0.5)
    k = _rope(k.reshape(b, s, 2 * h, dh), cos, sin).reshape(b, s, h, 2, dh)
    v = v.reshape(b, s, h, 2 * dh)
    lam_init = 0.8 - 0.6 * math.exp(-0.3 * layer_idx)
    lam = (jnp.exp(jnp.sum(lq1.astype(jnp.float32) * lk1.astype(jnp.float32)))
           - jnp.exp(jnp.sum(lq2.astype(jnp.float32) * lk2.astype(jnp.float32))) + lam_init)
    nb = s // Q_BLOCK
    q_blocks = q.reshape(b, nb, Q_BLOCK, h, 2, dh).swapaxes(0, 1)

    def one_block(qb):
        sc = jnp.einsum('bqhce,bkhce->bhcqk', qb, k).astype(jnp.float32)
        p = jax.nn.softmax(sc, axis=-1)
        a = p[:, :, 0] - lam * p[:, :, 1]
        return jnp.einsum('bhqk,bkhe->bqhe', a.astype(v.dtype), v)

    o = lax.map(one_block, q_blocks).swapaxes(0, 1).reshape(b, s, h, 2 * dh)
    o = _rms_norm(o, subln, DIFF_SUBLN_EPS) * (1.0 - lam_init)
    return o.reshape(b, s, h * 2 * dh) @ w_o

def _causal_conv(x, w, bias):
    kw = w.shape[0]
    s = x.shape[1]
    xp = jnp.pad(x, ((0, 0), (kw - 1, 0), (0, 0)))
    y = bias
    for j in range(kw):
        y = y + w[j] * xp[:, j:j + s]
    return y

def _rg_lru_direction(u, conv_w, conv_b, w_a, b_a, w_x, b_x, lam):
    b, s, c = u.shape
    xc = _causal_conv(u, conv_w, conv_b)
    xb = xc.reshape(b, s, LRU_BLOCKS, LRU_BLOCK_DIM)
    r = jax.nn.sigmoid((jnp.einsum('bsni,nij->bsnj', xb, w_a).reshape(b, s, c) + b_a).astype(jnp.float32))
    i = jax.nn.sigmoid((jnp.einsum('bsni,nij->bsnj', xb, w_x).reshape(b, s, c) + b_x).astype(jnp.float32))
    log_a = LRU_C * r * jax.nn.log_sigmoid(lam.astype(jnp.float32))
    a = jnp.exp(log_a)
    inp = jnp.sqrt(-jnp.expm1(2.0 * log_a)) * (i * xc.astype(jnp.float32))

    def combine(left, right):
        a_l, b_l = left
        a_r, b_r = right
        return a_l * a_r, a_r * b_l + b_r

    _, h = lax.associative_scan(combine, (a, inp), axis=1)
    return h

def _rglru_mixer(x, w_in, conv_w, conv_b, w_a, b_a, w_x, b_x, lam, w_out):
    gate, u = jnp.split(x @ w_in, 2, axis=-1)
    h_fwd = _rg_lru_direction(u, conv_w[0], conv_b[0], w_a[0], b_a[0], w_x[0], b_x[0], lam[0])
    h_bwd = jnp.flip(_rg_lru_direction(jnp.flip(u, axis=1), conv_w[1], conv_b[1], w_a[1], b_a[1],
                                       w_x[1], b_x[1], lam[1]), axis=1)
    y = jax.nn.gelu(gate.astype(jnp.float32), approximate=True) * (h_fwd + h_bwd)
    return y.astype(x.dtype) @ w_out

def _dilated_chain_attention(q, k, v, dilation, half):
    b, s, h, dh = q.shape
    n = s // dilation
    blk = half
    nb = -(-n // blk)
    pad = nb * blk - n

    def chains(t):
        return t.reshape(b, n, dilation, h, dh).transpose(0, 2, 3, 1, 4)

    qc = jnp.pad(chains(q), ((0, 0), (0, 0), (0, 0), (0, pad), (0, 0))).reshape(b, dilation, h, nb, blk, dh)

    def windows(t):
        tp = jnp.pad(chains(t), ((0, 0), (0, 0), (0, 0), (blk, blk + pad), (0, 0)))
        tp = tp.reshape(b, dilation, h, nb + 2, blk, dh)
        return jnp.concatenate([tp[:, :, :, :-2], tp[:, :, :, 1:-1], tp[:, :, :, 2:]], axis=4)

    kw, vw = windows(k), windows(v)
    qpos = jnp.arange(nb * blk).reshape(nb, blk)
    kpos = jnp.arange(nb)[:, None] * blk + jnp.arange(-blk, 2 * blk)[None, :]
    rel = kpos[:, None, :] - qpos[:, :, None]
    valid = (jnp.abs(rel) <= half) & (kpos[:, None, :] >= 0) & (kpos[:, None, :] < n)
    sc = jnp.einsum('bdhnqe,bdhnke->bdhnqk', qc, kw).astype(jnp.float32)
    sc = jnp.where(valid, sc, NEG_INF)
    lse = jax.nn.logsumexp(sc, axis=-1)
    p = jnp.exp(sc - lse[..., None])
    o = jnp.einsum('bdhnqk,bdhnke->bdhnqe', p.astype(v.dtype), vw)

    def unchain(t):
        t = t.reshape((b, dilation, h, nb * blk) + t.shape[5:])[:, :, :, :n]
        t = jnp.moveaxis(t, 3, 1)
        return t.reshape((b, s, h) + t.shape[4:])

    return unchain(o), unchain(lse)

def _dilated_mixer(x, w_qkv, w_o, cos, sin):
    b, s, _ = x.shape
    n_groups = len(DIL_GROUPS)
    qkv = (x @ w_qkv).reshape(b, s, n_groups, 3, DIL_HEADS, HEAD_DIM)
    q = _rope(qkv[:, :, :, 0], cos, sin) * (HEAD_DIM ** -0.5)
    k = _rope(qkv[:, :, :, 1], cos, sin)
    v = qkv[:, :, :, 2]
    outs, lses = [], []
    for g, (window, dilation) in enumerate(DIL_GROUPS):
        o, l = _dilated_chain_attention(q[:, :, g], k[:, :, g], v[:, :, g], dilation, window // (2 * dilation))
        outs.append(o.astype(jnp.float32))
        lses.append(l)
    wts = jax.nn.softmax(jnp.stack(lses, axis=0), axis=0)
    o = jnp.sum(wts[..., None] * jnp.stack(outs, axis=0), axis=0)
    return o.astype(x.dtype).reshape(b, s, DIL_WIDTH) @ w_o

def _conv_ffn(x, w_up, conv_w, conv_b, w_down):
    s = x.shape[1]
    g, u = jnp.split(x @ w_up, 2, axis=-1)
    half = FFN_CONV // 2
    gp = jnp.pad(g, ((0, 0), (half, half), (0, 0)))
    gc = conv_b
    for j in range(FFN_CONV):
        gc = gc + conv_w[j] * gp[:, j:j + s]
    act = jax.nn.gelu(gc.astype(jnp.float32), approximate=False).astype(x.dtype)
    return (act * u) @ w_down

def second_inputs(seed: int = 0) -> dict:
    key = jax.random.key(seed)
    keys = iter(jax.random.split(key, 48))
    f32 = jnp.float32
    n_a, n_b, n_c, n_d = (_n_layers_of(m) for m in range(N_MIXERS))

    def dense(shape, fan_in):
        return jax.random.normal(next(keys), shape, f32) * fan_in ** -0.5

    def gain(shape):
        return 1.0 + 0.05 * jax.random.normal(next(keys), shape, f32)

    def small(shape, scale=0.02):
        return scale * jax.random.normal(next(keys), shape, f32)

    x = jax.random.normal(next(keys), (BATCH, SEQ, D_MODEL), f32)
    a_c = jax.random.uniform(next(keys), (n_c, 2, LRU_WIDTH), f32, 0.9, 0.999)
    base = a_c ** (1.0 / LRU_C)
    lru_lambda = jnp.log(base) - jnp.log1p(-base)
    return {
        "x": x,
        "positions": jnp.arange(SEQ, dtype=jnp.int32),
        "mix_norm": gain((DEPTH_2, D_MODEL)),
        "pool_w": dense((n_a, len(POOL_WINDOWS), POOL_GROUP, POOL_GROUP), POOL_GROUP),
        "pool_scale": gain((n_a, D_MODEL)),
        "diff_w_qkv": dense((n_b, D_MODEL, 3 * D_MODEL), D_MODEL),
        "diff_lam_q1": small((n_b, HEAD_DIM), 0.1),
        "diff_lam_k1": small((n_b, HEAD_DIM), 0.1),
        "diff_lam_q2": small((n_b, HEAD_DIM), 0.1),
        "diff_lam_k2": small((n_b, HEAD_DIM), 0.1),
        "diff_subln": gain((n_b, 2 * HEAD_DIM)),
        "diff_w_o": dense((n_b, D_MODEL, D_MODEL), D_MODEL),
        "lru_w_in": dense((n_c, D_MODEL, 2 * LRU_WIDTH), D_MODEL),
        "lru_conv_w": dense((n_c, 2, LRU_CONV, LRU_WIDTH), LRU_CONV),
        "lru_conv_b": small((n_c, 2, LRU_WIDTH)),
        "lru_w_a": dense((n_c, 2, LRU_BLOCKS, LRU_BLOCK_DIM, LRU_BLOCK_DIM), LRU_BLOCK_DIM),
        "lru_b_a": small((n_c, 2, LRU_WIDTH)),
        "lru_w_x": dense((n_c, 2, LRU_BLOCKS, LRU_BLOCK_DIM, LRU_BLOCK_DIM), LRU_BLOCK_DIM),
        "lru_b_x": small((n_c, 2, LRU_WIDTH)),
        "lru_lambda": lru_lambda,
        "lru_w_out": dense((n_c, LRU_WIDTH, D_MODEL), LRU_WIDTH),
        "dil_w_qkv": dense((n_d, D_MODEL, len(DIL_GROUPS) * 3 * DIL_WIDTH), D_MODEL),
        "dil_w_o": dense((n_d, DIL_WIDTH, D_MODEL), DIL_WIDTH),
        "ffn_norm": gain((DEPTH_2, D_MODEL)),
        "ffn_w_up": dense((DEPTH_2, D_MODEL, 2 * D_FF), D_MODEL),
        "ffn_conv_w": dense((DEPTH_2, FFN_CONV, D_FF), FFN_CONV),
        "ffn_conv_b": small((DEPTH_2, D_FF)),
        "ffn_w_down": dense((DEPTH_2, D_FF, D_MODEL), D_FF),
        "final_norm": gain((D_MODEL,)),
    }

def second_block(x, positions, mix_norm, pool_w, pool_scale, diff_w_qkv, diff_lam_q1, diff_lam_k1,
              diff_lam_q2, diff_lam_k2, diff_subln, diff_w_o, lru_w_in, lru_conv_w, lru_conv_b,
              lru_w_a, lru_b_a, lru_w_x, lru_b_x, lru_lambda, lru_w_out, dil_w_qkv, dil_w_o,
              ffn_norm, ffn_w_up, ffn_conv_w, ffn_conv_b, ffn_w_down, final_norm):
    cos, sin = _rope_tables(positions, HEAD_DIM)
    h = x
    for i in range(DEPTH_2):
        m, j = i % N_MIXERS, i // N_MIXERS
        hn = _rms_norm(h, mix_norm[i])
        if m == 0:
            y = _pool_mixer(hn, pool_w[j], pool_scale[j])
        elif m == 1:
            y = _diff_attention(hn, diff_w_qkv[j], diff_lam_q1[j], diff_lam_k1[j], diff_lam_q2[j],
                                diff_lam_k2[j], diff_subln[j], diff_w_o[j], cos, sin, i)
        elif m == 2:
            y = _rglru_mixer(hn, lru_w_in[j], lru_conv_w[j], lru_conv_b[j], lru_w_a[j], lru_b_a[j],
                             lru_w_x[j], lru_b_x[j], lru_lambda[j], lru_w_out[j])
        else:
            y = _dilated_mixer(hn, dil_w_qkv[j], dil_w_o[j], cos, sin)
        h = h + y
        h = h + _conv_ffn(_rms_norm(h, ffn_norm[i]), ffn_w_up[i], ffn_conv_w[i], ffn_conv_b[i], ffn_w_down[i])
    return _rms_norm(h, final_norm)


def setup_inputs(seed=0):
    out = dict(first_inputs(seed))
    for name, value in second_inputs(seed + 1).items():
        if name != "x":
            out[name + "_2"] = value
    return out


def reference(
    x, c, positions, w_ada, b_ada, g_norm1, w_in, g_q_norm, w_uq, g_kv_norm, w_ukv, g_ret_norm,
    w_out, g_norm2, w_query, sub_keys, expert_u, expert_v, g_final, positions_2, mix_norm_2,
    pool_w_2, pool_scale_2, diff_w_qkv_2, diff_lam_q1_2, diff_lam_k1_2, diff_lam_q2_2,
    diff_lam_k2_2, diff_subln_2, diff_w_o_2, lru_w_in_2, lru_conv_w_2, lru_conv_b_2, lru_w_a_2,
    lru_b_a_2, lru_w_x_2, lru_b_x_2, lru_lambda_2, lru_w_out_2, dil_w_qkv_2, dil_w_o_2,
    ffn_norm_2, ffn_w_up_2, ffn_conv_w_2, ffn_conv_b_2, ffn_w_down_2, final_norm_2,
):
    x = first_block(
        x, c, positions, w_ada, b_ada, g_norm1, w_in, g_q_norm, w_uq, g_kv_norm, w_ukv,
        g_ret_norm, w_out, g_norm2, w_query, sub_keys, expert_u, expert_v, g_final,
    )
    return second_block(
        x, positions_2, mix_norm_2, pool_w_2, pool_scale_2, diff_w_qkv_2, diff_lam_q1_2,
        diff_lam_k1_2, diff_lam_q2_2, diff_lam_k2_2, diff_subln_2, diff_w_o_2, lru_w_in_2,
        lru_conv_w_2, lru_conv_b_2, lru_w_a_2, lru_b_a_2, lru_w_x_2, lru_b_x_2, lru_lambda_2,
        lru_w_out_2, dil_w_qkv_2, dil_w_o_2, ffn_norm_2, ffn_w_up_2, ffn_conv_w_2, ffn_conv_b_2,
        ffn_w_down_2, final_norm_2,
    )


_drawn_inputs = setup_inputs


def setup_inputs(seed=0):
    import zlib

    import numpy as np

    out = dict(_drawn_inputs(seed))
    spreads = {}
    factors = {'g_q_norm': 8.0,
     'g_kv_norm': 3.652,
     'g_ret_norm': 11.146,
     'diff_lam_q1_2': 3.364,
     'ffn_conv_b_2': 4.471,
     'g_norm2': 4.142,
     'diff_lam_k2_2': 2.808}
    for name, (base, spread) in spreads.items():
        noise = np.random.default_rng([zlib.crc32(name.encode()), seed]).standard_normal(out[name].shape)
        drawn = base * np.exp(spread * noise) if base else spread * noise
        out[name] = jnp.asarray(drawn.astype(out[name].dtype))
    for name, factor in factors.items():
        out[name] = (out[name] * factor).astype(out[name].dtype)
    return out
```

```python
from contextlib import ExitStack

import numpy as np

import concourse.bass as bass
from concourse import mybir

F32 = mybir.dt.float32
F32R = mybir.dt.float32r
I32 = mybir.dt.int32
U32 = mybir.dt.uint32
ACT = mybir.ActivationFunctionType
ALU = mybir.AluOpType
AX = mybir.AxisListType.X

P = 128
D, T = 1024, 512
KT, TT = D // P, T // P
EPS = 1e-6
ROPE_THETA = 10000.0
MLA_H, NOPE, ROPE, MLA_V, Q_RANK = 8, 64, 32, 64, 256
MLA_QK = NOPE + ROPE
RET_H, RET_D = 8, 64
PEER_H, PEER_KEYS, TOPK = 8, 128, 16
N_EXP = PEER_KEYS * PEER_KEYS
DIFF_H, HD = 8, 64
SUBLN_EPS = 1e-5
LAM_INIT = float(0.8 - 0.6 * np.exp(-0.3))
D_FF = 2816
FT = D_FF // P
WINDOWS = (2, 4, 8, 16)
NEG = -1e30
FAR_BELOW = -3.0e38

CHUNK, STAGES, SLOTS = 2048, 2, 4

C_LAT, C_KV, C_RQK, C_RG, C_RV = 0, 1, 2, 6, 8
C_UQ, C_UKV, C_OUT, C_QUERY, C_PEER = 10, 11, 12, 16, 24
PEER_STEPS = N_EXP // 256
C_POOL = C_PEER + 2 * PEER_STEPS
C_FFN1 = C_POOL + 1
C_QKV = C_FFN1 + 2 * FT
C_WO = C_QKV + 12
C_FFN2 = C_WO + 4
C_END = C_FFN2 + 2 * FT

VEC = {}
for _name, _n in (("c", 8), ("b_ada", 48), ("g_norm1", 8), ("g_q", 2), ("g_kv", 1), ("g_ret", 4), ("g_norm2", 8),
                  ("g_final", 8), ("mix0", 8), ("mix1", 8), ("pool_scale", 8), ("subln", 1), ("ffn0", 8),
                  ("ffn1", 8), ("final", 8), ("conv0", 4 * FT), ("conv1", 4 * FT),
                  ("inv64", 1), ("inv96", 1), ("sign64", 1), ("sign96", 1)):
    VEC[_name] = (sum(n for _, n in VEC.values()), _n)
NVEC = sum(n for _, n in VEC.values())
ONES, IDENT, SWAP64, SWAP96, BLOCKMEAN, CAUSAL, IOTA = range(7)
NTAB = 7

TB = 32
NTB = T // TB


class Chain:

    def __init__(self, eng, sem):
        self.eng, self.sem, self.n = eng, sem, 0

    def __call__(self, ins):
        ins.then_inc(self.sem, 1)
        self.n = self.n + 1
        self.eng.wait_ge(self.sem, self.n)


def build(nc, A, O):
    out = O.get("out")
    with ExitStack() as ctx:
        def sb(name, shape, dt=F32, scope=ctx):
            return scope.enter_context(nc.sbuf_tensor("sb_" + name, shape, dt))

        def sem(name):
            return ctx.enter_context(nc.semaphore(name))

        def sems(stage, *names):
            return {n: sem(stage + "_" + n) for n in names}

        xT = sb("xT", [P, KT, T])
        hH = sb("hH", [P, KT, T], F32R)
        hL = sb("hL", [P, KT, T], F32R)
        stage = [sb(f"stage{i}", [P, CHUNK]) for i in range(STAGES)]
        wH = [sb(f"wH{i}", [P, CHUNK], F32R) for i in range(SLOTS)]
        wL = [sb(f"wL{i}", [P, CHUNK], F32R) for i in range(SLOTS)]
        vec = sb("vec", [P, NVEC])
        tab = sb("tab", [P, NTAB, P])
        mod = sb("mod", [P, 48])
        gain1 = sb("gain1", [P, KT])
        gain2 = sb("gain2", [P, KT])
        small = sb("small", [P, 16])
        scr = sb("scr", [P, 9, T])
        posi = sb("posi", [P, T], I32)
        lams = sb("lams", [P, 4, HD])
        sinkv = sb("sinkv", [P, HD])
        stats = sb("stats", [P, 8, 32])
        ps = ctx.enter_context(nc.psum_tensor("ps", [P, 8, T], F32))

        def col(name, i=0, n=1):
            o, m = VEC[name]
            assert i + n <= m
            return vec[:, o + i:o + i + n]

        with ExitStack() as s1:
            ada = [sb(f"ada{i}", [P, CHUNK], scope=s1) for i in range(4)]
            sc = sb("sc", [P, KT], scope=s1)
            sc1 = sb("sc1", [P, KT], scope=s1)
        lat_scope = ExitStack()
        lat = sb("lat", [P, 4, T], scope=lat_scope)
        with ExitStack() as s2:
            qk = sb("qk", [P, 8, T], scope=s2)
            rv = sb("rv", [P, TT, RET_H * RET_D], scope=s2)
            rg = sb("rg", [P, 4, T], scope=s2)
            rope_r = sb("rope_r", [P, 2, T], scope=s2)
            decay = [sb(f"decay{i}", [P, T], scope=s2) for i in range(2)]
        with ExitStack() as s3:
            qnH = sb("qnH", [P, 2, T], F32R, scope=s3)
            qnL = sb("qnL", [P, 2, T], F32R, scope=s3)
            kvH = sb("kvH", [P, 1, T], F32R, scope=s3)
            kvL = sb("kvL", [P, 1, T], F32R, scope=s3)
            qh = sb("qh", [P, MLA_H, T], scope=s3)
            kh = sb("kh", [P, MLA_H, T], scope=s3)
        lat_scope.close()
        with ExitStack() as s4:
            fromsel = sb("fromsel", [P, 3, T], scope=s4)
            with ExitStack() as s5:
                keysT = sb("keysT", [P, 2, P], scope=s5)
                qp = [sb(f"qp{i}", [P, T], scope=s5) for i in range(2)]
                sc_k = [sb(f"sc_k{i}", [P, TT, P], scope=s5) for i in range(2)]
                sc_m = sb("sc_m", [P, TT, P], scope=s5)
                topv = sb("topv", [P, TT, 16, TOPK], scope=s5)
                topi = sb("topi", [P, TT, 16, TOPK], U32, scope=s5)
                topf = sb("topf", [P, TT, 16, TOPK], scope=s5)
                cand = sb("cand", [P, PEER_H, TOPK * TOPK], scope=s5)
                cand2 = sb("cand2", [P, PEER_H, TOPK * TOPK], scope=s5)
                best = sb("best", [P, PEER_H, TOPK], scope=s5)
                pos = sb("pos", [P, PEER_H, TOPK], U32, scope=s5)
                posu = sb("posu", [P, 2, PEER_H, TOPK], U32, scope=s5)
                posf = sb("posf", [P, 2, PEER_H, TOPK], scope=s5)
                chosen = sb("chosen", [P, 3, PEER_H * TOPK], scope=s5)
                gsum = sb("gsum", [P, 2, PEER_H], scope=s5)
            with ExitStack() as s6:
                oneJ = [sb(f"oneJ{i}", [P, 4, P], scope=s6) for i in range(2)]
                oneI = [sb(f"oneI{i}", [P, 4, P], scope=s6) for i in range(2)]
                wst = [sb(f"wst{i}", [P, P, TB], scope=s6) for i in range(2)]
        with ExitStack() as s7:
            wg = [sb(f"wg{i}", [P, NTB, 4, TB], scope=s7) for i in range(2)]
            ga = [sb(f"ga{i}", [P, T], scope=s7) for i in range(2)]
            wa = [sb(f"wa{i}", [P, T], scope=s7) for i in range(2)]
            waH = [[sb(f"waH{i}{m}", [P, T], F32R, scope=s7) for m in range(2)] for i in range(2)]
            waL = [[sb(f"waL{i}{m}", [P, T], F32R, scope=s7) for m in range(2)] for i in range(2)]
        PAD = 8
        with ExitStack() as s8:
            hp = sb("hp", [P, KT, T + 2 * PAD], scope=s8)
            wbuf = [sb(f"wbuf{i}", [P, 2, T + 2 * PAD], scope=s8) for i in range(2)]
            win = [sb(f"win{i}", [P, 2, T], scope=s8) for i in range(2)]
            recips = sb("recips", [P, len(WINDOWS), T], scope=s8)
        with ExitStack() as s9:
            dqk = sb("dqk", [P, 16, T], scope=s9)
            dv = sb("dv", [P, TT, D], scope=s9)
            rope_d = sb("rope_d", [P, 2, T], scope=s9)
        with ExitStack() as s10:
            gcv = [sb(f"gcv{i}", [P, T], scope=s10) for i in range(2)]
            gel = [sb(f"gel{i}", [P, T], scope=s10) for i in range(2)]
            fa = [sb(f"fa{i}", [P, T], scope=s10) for i in range(2)]
            faH = [sb(f"faH{i}", [P, T], F32R, scope=s10) for i in range(2)]
            faL = [sb(f"faL{i}", [P, T], F32R, scope=s10) for i in range(2)]

        wd = A["w_scratch"]

        ld_const = sem("ld_const")
        ld_x = sem("ld_x")
        ld_ada = [sem(f"ld_ada{i}") for i in range(4)]
        ld_stage = [sem(f"ld_stage{i}") for i in range(STAGES)]
        w_hi = sem("w_hi")
        w_split = sem("w_split")
        w_begun = sem("w_begun")
        s_ada = sems("ada", "silu", "exp", "done", "mod")
        s_norm = sems("norm", "sq", "sum", "rec", "root", "xr", "t", "hi", "lo")
        NORMS = (("norm1", KT, 1), ("normq", 2, 1), ("normkv", 1, 1), ("norm2", KT, 1), ("final1", KT, 0),
                 ("mix0", KT, 0), ("ffn0", KT, 1), ("mix1", KT, 1), ("ffn1", KT, 1), ("final2", KT, 0))

        def n_at(name, what):
            at = 0
            for n, tiles, split in NORMS:
                if n == name:
                    return at
                at += 1 if what in ("rec", "root") else tiles * split if what in ("hi", "lo") else tiles

        s_lat = sems("lat", "proj", "copied")
        s_tr = sems("tabr", "arg", "sin")
        s_tm = sems("tabm", "arg", "sin")
        s_td = sems("tabd", "arg", "sin")
        s_rr = sems("rrope", "proj", "copied", "perm", "roped")
        s_rp = sems("rproj", "proj", "gate", "value")
        s_rt = sems("ret", "scores", "decayed", "y", "ycopied", "ld0", "ld1")
        s_rn = sems("retn", "mean", "cent", "sq", "var", "rec", "root", "gexp", "yn", "hi", "lo")
        s_mr = sems("mrope", "proj", "copied", "perm", "roped", "kr")
        s_mk = sems("mkv", "k", "kcopied", "v", "vcopied")
        s_ma = sems("mla", "scores", "negmax", "exp", "probs", "trans", "pt", "o", "hi", "lo")
        s_wo1 = sems("wout", "proj", "added")
        s_q = sems("query", "keys", "proj", "copied", "scores", "scopied", "top", "sel", "negbest", "gexp", "chosen",
                   "trans", "tcopied")
        s_w = sems("wbuild", "ones", "prod", "copied", "st0", "st1")
        s_e = sems("peer", "ld0", "ld1", "a", "gelu", "wa", "hi", "lo", "o", "added")
        s_p = sems("pool", "ld", "filled", "pooled", "hi", "lo", "proj", "added")
        s_f = [sems(f"ffn{i}_l", "proj", "conv", "gelu", "act", "hi", "lo", "o", "added") for i in range(2)]
        s_dr = sems("drope", "proj", "copied", "perm", "roped")
        s_dv = sems("dvals", "v", "copied")
        s_da = sems("diff", "lam", "scores", "negmax", "exp", "probs", "trans", "at", "o", "ycopied")
        s_dn = sems("subln", "sq", "sum", "rec", "root", "yn", "hi", "lo")
        s_wo2 = sems("wo", "proj", "added")
        v_chain = sem("v_chain")
        a_chain = sem("a_chain")
        stored = sem("stored")

        def load(sp, c, src, c0=None):
            k = c if c0 is None else c0
            n = src.shape[-1]
            if k >= STAGES:
                sp.wait_ge(w_split, c - (STAGES - 1))
            sp.dma_start(stage[k % STAGES][:, 0:n], src).then_inc(ld_stage[k % STAGES], 16)

        def landed(k, i=0, per=0):
            return 16 * (k // STAGES + 1) + i * (16 * per // STAGES)

        def split_hi(act, k, n=CHUNK, i=0, per=0):
            act.wait_ge(ld_stage[k % STAGES], landed(k, i, per))
            if k >= SLOTS:
                act.wait_ge(w_begun, k - SLOTS + 2 + i * per)
            act.activation(wH[k % SLOTS][:, 0:n], stage[k % STAGES][:, 0:n], ACT.Copy).then_inc(w_hi, 1)

        def split_lo(dve, k, n=CHUNK, i=0, per=0):
            dve.wait_ge(w_hi, k + 1 + i * per)
            dve.tensor_tensor(wL[k % SLOTS][:, 0:n], stage[k % STAGES][:, 0:n], wH[k % SLOTS][:, 0:n],
                              ALU.subtract).then_inc(w_split, 1)

        def chunk_len(k):
            if k == C_KV:
                return KT * 224
            if k == C_UQ:
                return 2 * MLA_H * MLA_QK
            if k == C_UKV:
                return MLA_H * (NOPE + MLA_V)
            if k > C_FFN1 and k < C_QKV:
                return CHUNK if is_up(k - C_FFN1) else D
            if k > C_FFN2 and k < C_END:
                return CHUNK if is_up(k - C_FFN2) else D
            return CHUNK

        def is_up(r):
            return r == 0 or (r % 2 == 1 and r != 2 * FT - 1)

        def split_hi_at(act, k):
            if k < C_END:
                split_hi(act, k, chunk_len(k))

        def split_lo_at(dve, k):
            if k < C_END:
                split_lo(dve, k, chunk_len(k))

        def three(pe, dst, lh, ll, rh, rl, first, last, begins=False):
            m = pe.matmul(dst, lh, rl, start=first, stop=False)
            if begins:
                m.then_inc(w_begun, 1)
            pe.matmul(dst, ll, rh, start=False, stop=False)
            return pe.matmul(dst, lh, rh, start=False, stop=last)

        def product(pe, k, dst, cols, nkt, width, rH, rL, done, begins):
            wh = wH[k % SLOTS][:, 0:nkt * width].rearrange("p (k n) -> p k n", k=nkt)
            wl = wL[k % SLOTS][:, 0:nkt * width].rearrange("p (k n) -> p k n", k=nkt)
            for q in range(nkt):
                m = three(pe, dst, wh[:, q, cols], wl[:, q, cols], rH[:, q, :], rL[:, q, :], q == 0, q == nkt - 1,
                          begins and q == 0)
            m.then_inc(done, 1)

        block = ctx.enter_context(nc.Block())

        @block.sync
        def _(sp):
            sp.dma_start(vec[:, :], A["vectors"]).then_inc(ld_const, 16)
            sp.dma_start(tab[:, :, :], A["tables"]).then_inc(ld_const, 16)
            sp.dma_start(posi[:, :], A["positions_l"][:, 0:T].broadcast_to([P, T])).then_inc(ld_const, 16)
            sp.dma_start(lams[:, :, :].rearrange("p a b -> p (a b)"),
                         A["lams"].broadcast_to([P, 4 * HD])).then_inc(ld_const, 16)
            for j in range(4):
                sp.dma_start(ada[j][:, :], A["w_ada_l"][j]).then_inc(ld_ada[j], 16)
            with sp.Fori(1, 6) as i:
                for j in range(4):
                    sp.wait_ge(s_ada["done"], i * 4 + j - 3)
                    sp.dma_start(ada[j][:, :], A["w_ada_l"][i * 4 + j]).then_inc(ld_ada[j], 16)
            sp.dma_start(xT[:, :, :], A["x_l"]).then_inc(ld_x, 16)
            for k in range(2):
                load(sp, k, [A["w_lat0"], A["w_lat1"]][k])
            for k in range(8):
                load(sp, 2 + k, A["w_ret_l"][k])
            load(sp, C_UQ, A["w_uq_l"])
            load(sp, C_UKV, A["w_ukv_l"])
            for h in range(RET_H):
                if h < 2:
                    sp.wait_ge(s_norm["lo"], n_at("norm1", "lo") + KT)
                else:
                    sp.wait_ge(s_rt["decayed"], TT * (h - 1))
                sp.dma_start(decay[h % 2][:, :], A["decays"][h]).then_inc(s_rt[f"ld{h % 2}"], 16)
            for k in range(4):
                load(sp, C_OUT + k, A["w_out_l"][k])
            sp.wait_ge(s_tm["arg"], 1)
            sp.dma_start(posi[:, :], A["positions_l"][:, T:2 * T].broadcast_to([P, T])).then_inc(ld_const, 16)
            load(sp, C_QUERY, A["w_query_l"][0])
            load(sp, C_QUERY + 1, A["w_query_l"][1])
            sp.wait_ge(s_wo1["added"], KT)
            sp.dma_start(keysT[:, :, :], A["keys_l"]).then_inc(s_q["keys"], 16)
            for k in range(2, 8):
                load(sp, C_QUERY + k, A["w_query_l"][k])
            load(sp, C_PEER, A["u_l"][0])
            with sp.Fori(0, NTB // 2) as b:
                for par in range(2):
                    sp.wait_ge(s_w["copied"], (TB // 4) * (2 * b + par + 1))
                    sp.dma_start(wd[2 * b + par], wst[par][:, :, :]).then_inc(s_w[f"st{par}"], 16)
            load(sp, C_PEER + 1, A["u_l"][1])
            for par in range(2):
                sp.wait_ge(s_w[f"st{par}"], 16 * (NTB // 2))
            wd_i = wd.rearrange("b j i t -> j b i t")
            for par in range(2):
                sp.dma_start(wg[par][:, :, :, :], wd_i[:, :, 4 * par:4 * par + 4, :]).then_inc(s_e[f"ld{par}"], 16)
            load(sp, C_PEER + 2, A["v_l"][0])
            with sp.Fori(0, PEER_STEPS // 4 - 1) as i:
                for q in range(4):
                    load(sp, C_PEER + 3 + 2 * q + 8 * i, A["u_l"][4 * i + q + 2], C_PEER + 3 + 2 * q)
                    load(sp, C_PEER + 4 + 2 * q + 8 * i, A["v_l"][4 * i + q + 1], C_PEER + 4 + 2 * q)
                    if q % 2 == 1:
                        par = q // 2
                        sp.wait_ge(s_e["wa"], 4 * (2 * i + par) + 4)
                        sp.dma_start(wg[par][:, :, :, :], wd_i[:, :, bass.ds((2 * i + par + 2) * 4, 4), :]
                                     ).then_inc(s_e[f"ld{par}"], 16)
            for s in range(PEER_STEPS - 4, PEER_STEPS + 1):
                c = C_PEER + 2 * s + 3
                if s + 2 < PEER_STEPS:
                    load(sp, c, A["u_l"][s + 2])
                    load(sp, c + 1, A["v_l"][s + 1])
                elif s + 1 < PEER_STEPS:
                    load(sp, c, A["v_l"][s + 1])
            sp.wait_ge(s_norm["t"], n_at("final1", "t") + KT)
            sp.dma_start(recips[:, :, :], A["recips"]).then_inc(s_p["ld"], 16)
            load(sp, C_POOL, A["pool_l"])

            def ffn_loads(l, c):
                load(sp, c, A["up_l"][l, 0])
                load(sp, c + 1, A["up_l"][l, 1])
                load(sp, c + 2, A["down_l"][l, 0])
                with sp.Fori(0, FT // 2 - 1) as i:
                    for q in range(2):
                        load(sp, c + 3 + 2 * q + 4 * i, A["up_l"][l, 2 * i + q + 2], c + 3 + 2 * q)
                        load(sp, c + 4 + 2 * q + 4 * i, A["down_l"][l, 2 * i + q + 1], c + 4 + 2 * q)
                load(sp, c + 2 * FT - 1, A["down_l"][l, FT - 1])

            ffn_loads(0, C_FFN1)
            for k in range(12):
                load(sp, C_QKV + k, A["w_qkv_l"][k])
            for k in range(4):
                load(sp, C_WO + k, A["w_o_l"][k])
            ffn_loads(1, C_FFN2)
            for k in range(KT):
                sp.wait_ge(s_norm["t"], n_at("final2", "t") + k + 1)
                sp.dma_start(out[:, k, :], xT[:, k, :]).then_inc(stored, 16)
            sp.wait_ge(stored, 16 * KT)

        @block.scalar
        def _(act):
            chain = Chain(act, a_chain)

            def norm(name, src, nkt, gains, shifts, dst=None, dstH=None, dstL=None):
                s = s_norm
                for k in range(nkt):
                    if k >= 2:
                        act.wait_ge(s["sum"], n_at(name, "sum") + k - 1)
                    act.activation(scr[:, k % 2, :], src(k), ACT.Square).then_inc(s["sq"], 1)
                act.wait_ge(s["rec"], n_at(name, "rec") + 1)
                act.activation(scr[:, 3, :], scr[:, 4, :], ACT.Sqrt).then_inc(s["root"], 1)
                for k in range(nkt):
                    act.wait_ge(s["xr"], n_at(name, "xr") + k + 1)
                    if dst is None and k >= 2:
                        act.wait_ge(s["lo"], n_at(name, "lo") + k - 1)
                    d = scr[:, 7 + k % 2, :] if dst is None else dst(k)
                    act.activation(d, scr[:, k % 2, :], ACT.Identity, scale=gains(k),
                                   bias=shifts(k) if shifts else 0.0).then_inc(s["t"], 1)
                    if dst is None:
                        act.wait_ge(s["t"], n_at(name, "t") + k + 1)
                        act.activation(dstH[:, k, :], d, ACT.Copy).then_inc(s["hi"], 1)

            def rope_tables(s, tabs):
                for q in range(2):
                    act.wait_ge(s["arg"], q + 1)
                    act.activation(tabs(q), tabs(q), ACT.Sin).then_inc(s["sin"], 1)

            act.wait_ge(ld_const, 64)
            act.activation(sc1[:, :], col("c", 0, 8), ACT.Exp, scale=-1.0).then_inc(s_ada["exp"], 1)
            act.wait_ge(ld_x, 16)
            act.wait_ge(s_ada["mod"], 3)
            norm("norm1", lambda k: xT[:, k, :], KT, lambda k: gain1[:, k:k + 1], lambda k: mod[:, k:k + 1],
                 dstH=hH, dstL=hL)
            split_hi_at(act, 0)
            split_hi_at(act, 1)
            rope_tables(s_tr, lambda q: rope_r[:, q, :])
            for t in range(4):
                if t % 2 == 0:
                    split_hi_at(act, C_LAT + t // 2 + 2)
                n = P if t < 3 else MLA_QK
                act.wait_ge(s_lat["proj"], t + 1)
                act.activation(lat[0:n, t, :], ps[0:n, t % 2, :], ACT.Copy).then_inc(s_lat["copied"], 1)
            for t in range(8):
                if t % 2 == 0:
                    split_hi_at(act, C_RQK + t // 2 + 2)
                act.wait_ge(s_rr["proj"], t + 1)
                act.activation(qk[:, t, :], ps[:, t % 2, :], ACT.Copy).then_inc(s_rr["copied"], 1)
            for t in range(4):
                if t % 2 == 0:
                    split_hi_at(act, C_RG + t // 2 + 2)
                act.wait_ge(s_rp["proj"], t + 1)
                act.activation(rg[:, t, :], ps[:, t % 2, :], ACT.Copy).then_inc(s_rp["gate"], 1)
            split_hi_at(act, C_RV + 2)
            split_hi_at(act, C_RV + 3)
            for m in range(4):
                act.wait_ge(s_rt["y"], 2 * TT * (m + 1))
                act.activation(qk[:, m, :], ps[:, 4 + m % 2, :], ACT.Copy).then_inc(s_rt["ycopied"], 1)
            for m in range(4):
                act.wait_ge(s_rn["cent"], m + 1)
                act.activation(scr[:, 1, :], qk[:, m, :], ACT.Square).then_inc(s_rn["sq"], 1)
                act.wait_ge(s_rn["rec"], m + 1)
                act.activation(scr[:, 3, :], scr[:, 4, :], ACT.Sqrt).then_inc(s_rn["root"], 1)
                act.activation(scr[:, 5, :], rg[:, m, :], ACT.Exp, scale=-1.0).then_inc(s_rn["gexp"], 1)
                act.wait_ge(s_rn["yn"], m + 1)
                act.activation(hH[:, 4 + m, :], qk[:, m, :], ACT.Copy).then_inc(s_rn["hi"], 1)
            act.wait_ge(s_rn["lo"], 4)
            norm("normq", lambda k: lat[:, k, :], 2, lambda k: col("g_q", k), None, dstH=qnH, dstL=qnL)
            act.wait_ge(s_norm["lo"], n_at("normq", "lo") + 2)
            norm("normkv", lambda k: lat[:, 2, :], 1, lambda k: col("g_kv"), None, dstH=kvH, dstL=kvL)
            rope_tables(s_tm, lambda q: scr[:, 7 + q, :])
            for h in range(MLA_H):
                act.wait_ge(s_mr["proj"], h + 1)
                act.activation(qh[0:MLA_QK, h, :], ps[0:MLA_QK, h % 2, :], ACT.Copy).then_inc(s_mr["copied"], 1)
            split_hi_at(act, C_OUT)
            for h in range(MLA_H):
                act.wait_ge(s_mk["k"], h + 1)
                act.activation(kh[0:NOPE, h, :], ps[0:NOPE, h % 2, :], ACT.Copy).then_inc(s_mk["kcopied"], 1)
            split_hi_at(act, C_OUT + 1)

            def mla_pt(u):
                h, qt = u // TT, u % TT
                act.wait_ge(s_ma["trans"], u + 1)
                if qt == 0 and h >= 1:
                    act.wait_ge(s_ma["o"], h)
                act.activation(scr[:, 2:2 + qt + 1, qt * P:(qt + 1) * P],
                               ps[:, 2 + u % 2, 0:(qt + 1) * P].rearrange("p (k n) -> p k n", n=P),
                               ACT.Copy).then_inc(s_ma["pt"], 1)
                if qt == TT - 1 and h % 2 == 1:
                    m = h // 2
                    act.wait_ge(s_ma["o"], h + 1)
                    act.activation(hH[:, m, :], ps[:, 4 + m % 2, :], ACT.Copy).then_inc(s_ma["hi"], 1)

            for u in range(MLA_H * TT):
                n = (u % TT + 1) * P
                act.wait_ge(s_ma["negmax"], u + 1)
                if u >= 2:
                    act.wait_ge(s_ma["trans"], u - 1)
                act.activation(scr[:, u % 2, 0:n], ps[:, u % 2, 0:n], ACT.Exp, bias=stats[:, 1, u:u + 1],
                               scale=MLA_QK ** -0.5, accum_out=stats[:, 2, u:u + 1]).then_inc(s_ma["exp"], 1)
                if u >= 1:
                    mla_pt(u - 1)
            mla_pt(MLA_H * TT - 1)
            for k in range(4):
                split_hi_at(act, C_OUT + k + 2)
            act.wait_ge(s_wo1["added"], KT)
            norm("norm2", lambda k: xT[:, k, :], KT, lambda k: gain2[:, k:k + 1], lambda k: mod[:, 24 + k:25 + k],
                 dstH=hH, dstL=hL)

            def keys_copy(t):
                act.wait_ge(s_q["scores"], t + 1)
                if t >= 2:
                    act.wait_ge(s_q["top"], t - 1)
                act.activation(sc_k[t % 2][:, :, :], ps[:, 2 + t % 2, :].rearrange("p (a n) -> p a n", n=P),
                               ACT.Copy).then_inc(s_q["scopied"], 1)

            for t in range(16):
                if t % 2 == 0 and t // 2 < 7:
                    split_hi_at(act, C_QUERY + t // 2 + 2)
                act.wait_ge(s_q["proj"], t + 1)
                if t >= 2:
                    act.wait_ge(s_q["scores"], t - 1)
                act.activation(qp[t % 2][:, :], ps[:, t % 2, :], ACT.Copy).then_inc(s_q["copied"], 1)
                if t >= 1:
                    keys_copy(t - 1)
            keys_copy(15)
            for tt in range(TT):
                act.wait_ge(s_q["negbest"], tt + 1)
                act.activation(best[:, :, :], best[:, :, :], ACT.Exp).then_inc(s_q["gexp"], 1)
                for r in range(3):
                    act.wait_ge(s_q["trans"], 3 * tt + r + 1)
                    act.activation(fromsel[:, r, tt * P:(tt + 1) * P], ps[:, 4 + r, 0:P],
                                   ACT.Copy).then_inc(s_q["tcopied"], 1)
            with act.Fori(0, NTB // 2) as b:
                for par in range(2):
                    for g in range(TB // 4):
                        if g == 0:
                            act.wait_ge(s_w[f"st{par}"], b * 16)
                        act.wait_ge(s_w["prod"], (2 * b + par) * (TB // 4) + g + 1)
                        act.activation(wst[par][:, :, 4 * g:4 * g + 4],
                                       ps[:, g % 2, :].rearrange("p (t i) -> p i t", t=4),
                                       ACT.Copy).then_inc(s_w["copied"], 1)
            def peer_act(s0, i=0, has_a=True, splits=2):
                for q in range(splits):
                    split_hi(act, C_PEER + 2 * s0 + 1 + q, CHUNK, i, 8)
                if not has_a:
                    return
                for m in range(2):
                    act.wait_ge(s_e["a"], 2 * s0 + m + 1 + 8 * i)
                    if s0 > 0:
                        act.wait_ge(s_e["wa"], 2 * s0 - 2 + m + 1 + 8 * i)
                    act.activation(ga[m][:, :], ps[:, 2 * (s0 % 2) + m, :], ACT.Gelu).then_inc(s_e["gelu"], 1)
                for m in range(2):
                    act.wait_ge(s_e["wa"], 2 * s0 + m + 1 + 8 * i)
                    if s0 >= 2:
                        act.wait_ge(s_e["o"], KT * (s0 - 1) + 8 * KT // 2 * i)
                    act.activation(waH[s0 % 2][m][:, :], wa[m][:, :], ACT.Copy).then_inc(s_e["hi"], 1)

            peer_act(0)
            peer_act(1)
            with act.Fori(0, PEER_STEPS // 4 - 1) as i:
                for q in range(4):
                    peer_act(2 + q, i)
            for s in range(PEER_STEPS - 2, PEER_STEPS):
                peer_act(s, splits=2 if s < PEER_STEPS - 1 else 1)
            act.wait_ge(s_e["added"], KT * PEER_STEPS)
            norm("final1", lambda k: xT[:, k, :], KT, lambda k: col("g_final", k), None, dst=lambda k: xT[:, k, :])
            act.wait_ge(s_norm["t"], n_at("final1", "t") + KT)
            act.wait_ge(s_p["filled"], 1)
            norm("mix0", lambda k: xT[:, k, :], KT, lambda k: col("mix0", k), None,
                 dst=lambda k: hp[:, k, PAD:PAD + T])
            split_hi_at(act, C_POOL)
            for g in range(len(WINDOWS)):
                act.wait_ge(s_p["pooled"], g + 1)
                act.activation(hH[:, 2 * g:2 * g + 2, :], win[g % 2][:, :, 0:T], ACT.Copy).then_inc(s_p["hi"], 1)
            split_hi_at(act, C_POOL + 1)
            split_hi_at(act, C_POOL + 2)

            def ffn_act(l, c, s0, i=0, has_a=True, splits=2):
                s = s_f[l]
                for q in range(splits):
                    k = c + 2 * s0 + 1 + q
                    split_hi(act, k, CHUNK if is_up(k - c) else D, i, 4)
                if not has_a:
                    return
                act.wait_ge(s["conv"], s0 + 1 + 2 * i)
                if s0 >= 1:
                    act.wait_ge(s["act"], s0 + 2 * i)
                act.activation(gel[s0 % 2][:, :], gcv[s0 % 2][:, :], ACT.Gelu).then_inc(s["gelu"], 1)
                act.wait_ge(s["act"], s0 + 1 + 2 * i)
                if s0 >= 2:
                    act.wait_ge(s["o"], KT * (s0 - 1) + 2 * KT * i)
                act.activation(faH[s0 % 2][:, :], fa[s0 % 2][:, :], ACT.Copy).then_inc(s["hi"], 1)

            def ffn_scalar(l, c):
                ffn_act(l, c, 0, splits=0)
                split_hi(act, c + 2, D)
                ffn_act(l, c, 1)
                with act.Fori(0, FT // 2 - 2) as i:
                    for q in range(2):
                        ffn_act(l, c, 2 + q, i)
                ffn_act(l, c, FT - 2)
                ffn_act(l, c, FT - 1, splits=1)

            act.wait_ge(s_p["added"], KT)
            norm("ffn0", lambda k: xT[:, k, :], KT, lambda k: col("ffn0", k), None, dstH=hH, dstL=hL)
            ffn_scalar(0, C_FFN1)
            act.wait_ge(s_f[0]["added"], KT * FT)
            split_hi_at(act, C_QKV)
            split_hi_at(act, C_QKV + 1)
            norm("mix1", lambda k: xT[:, k, :], KT, lambda k: col("mix1", k), None, dstH=hH, dstL=hL)
            rope_tables(s_td, lambda q: rope_d[:, q, :])
            for t in range(16):
                if t % 2 == 0:
                    split_hi_at(act, C_QKV + t // 2 + 2)
                act.wait_ge(s_dr["proj"], t + 1)
                act.activation(dqk[:, t, :], ps[:, t % 2, :], ACT.Copy).then_inc(s_dr["copied"], 1)
            for k in range(4):
                split_hi_at(act, C_QKV + 8 + k + 2)
            act.wait_ge(s_da["lam"], 1)
            act.activation(small[:, 2:4], small[:, 0:2], ACT.Exp).then_inc(s_da["lam"], 1)

            def diff_at(u):
                h, qt = u // TT, u % TT
                act.wait_ge(s_da["trans"], u + 1)
                if qt == 0 and h >= 1:
                    act.wait_ge(s_da["o"], h)
                act.activation(scr[:, 5:9, qt * P:(qt + 1) * P],
                               ps[:, 4 + u % 2, :].rearrange("p (k n) -> p k n", n=P),
                               ACT.Copy).then_inc(s_da["at"], 1)
                if qt == TT - 1:
                    act.wait_ge(s_da["o"], h + 1)
                    act.activation(dqk[:, h, :], ps[:, 6 + h % 2, :], ACT.Copy).then_inc(s_da["ycopied"], 1)

            for u in range(DIFF_H * TT):
                for c in range(2):
                    act.wait_ge(s_da["negmax"], 2 * u + c + 1)
                    if u >= 2:
                        act.wait_ge(s_da["probs"], u - 1)
                    act.activation(scr[:, 2 * (u % 2) + c, :], ps[:, 2 * (u % 2) + c, :], ACT.Exp,
                                   bias=stats[:, 4 * c + 1, u:u + 1], scale=HD ** -0.5,
                                   accum_out=stats[:, 4 * c + 2, u:u + 1]).then_inc(s_da["exp"], 1)
                if u >= 1:
                    diff_at(u - 1)
            diff_at(DIFF_H * TT - 1)
            for h in range(DIFF_H):
                if h >= 1:
                    act.wait_ge(s_dn["sum"], h)
                act.activation(scr[:, 0, :], dqk[:, h, :], ACT.Square).then_inc(s_dn["sq"], 1)
                act.wait_ge(s_dn["rec"], h + 1)
                act.activation(scr[:, 3, :], scr[:, 4, :], ACT.Sqrt).then_inc(s_dn["root"], 1)
                act.wait_ge(s_dn["yn"], h + 1)
                act.activation(hH[:, h, :], dqk[:, h, :], ACT.Copy).then_inc(s_dn["hi"], 1)
            for k in range(4):
                split_hi_at(act, C_WO + k + 2)
            act.wait_ge(s_wo2["added"], KT)
            norm("ffn1", lambda k: xT[:, k, :], KT, lambda k: col("ffn1", k), None, dstH=hH, dstL=hL)
            ffn_scalar(1, C_FFN2)
            act.wait_ge(s_f[1]["added"], KT * FT)
            norm("final2", lambda k: xT[:, k, :], KT, lambda k: col("final", k), None, dst=lambda k: xT[:, k, :])

        @block.vector
        def _(dve):
            chain = Chain(dve, v_chain)

            def rsqrt(var, root, rec_done, root_done, n):
                dve.reciprocal(scr[:, 4, :], var).then_inc(rec_done, 1)
                dve.wait_ge(root_done, n)
                chain(dve.tensor_tensor(scr[:, 5, :], var, scr[:, 3, :], ALU.mult))
                chain(dve.tensor_tensor(scr[:, 5, :], scr[:, 5, :], scr[:, 3, :], ALU.mult))
                chain(dve.tensor_scalar(scr[:, 5, :], scr[:, 5, :], -0.5, 1.5, ALU.mult, ALU.add))
                chain(dve.tensor_tensor(root, scr[:, 5, :], scr[:, 3, :], ALU.mult))

            def norm(name, src, nkt, dst=None, dstL=None, dstH=None):
                s = s_norm
                dve.wait_ge(s["sum"], n_at(name, "sum") + nkt)
                chain(dve.tensor_scalar(scr[:, 2, :], ps[:, 7, :], 1.0 / (nkt * P), EPS, ALU.mult, ALU.add))
                rsqrt(scr[:, 2, :], scr[:, 6, :], s["rec"], s["root"], n_at(name, "root") + 1)

                def low(k):
                    dve.wait_ge(s["hi"], n_at(name, "hi") + k + 1)
                    dve.tensor_tensor(dstL[:, k, :], scr[:, 7 + k % 2, :], dstH[:, k, :],
                                      ALU.subtract).then_inc(s["lo"], 1)

                for k in range(nkt):
                    if k >= 2:
                        dve.wait_ge(s["t"], n_at(name, "t") + k - 1)
                    dve.tensor_tensor(scr[:, k % 2, :], src(k), scr[:, 6, :], ALU.mult).then_inc(s["xr"], 1)
                    if dst is None and k >= 1:
                        low(k - 1)
                if dst is None:
                    low(nkt - 1)

            def rope_tables(s, tabs, positions, inv, sign):
                two_pi = 2.0 * np.pi
                hi = float(np.float32(6.28125))
                mid = float(np.float32(two_pi - hi))
                mid = float((np.float32(mid).view(np.uint32) & np.uint32(0xFFFFF000)).view(np.float32))
                lo = float(np.float32(two_pi - hi - mid))
                ang, turn = scr[:, 5, :], scr[:, 6, :]
                chain(dve.tensor_copy(ang, positions))
                chain(dve.tensor_scalar(ang, ang, inv, None, ALU.mult))
                for q in range(2):
                    chain(dve.tensor_scalar(turn, ang, 1.0 / two_pi, 0.25 if q == 0 else 0.0, ALU.mult, ALU.add))
                    chain(dve.tensor_scalar(turn, turn, 12582912.0, None, ALU.add))
                    chain(dve.tensor_scalar(turn, turn, -12582912.0, None, ALU.add))
                    chain(dve.scalar_tensor_tensor(tabs(q), turn, -hi, ang, ALU.mult, ALU.add))
                    chain(dve.scalar_tensor_tensor(tabs(q), turn, -mid, tabs(q), ALU.mult, ALU.add))
                    chain(dve.scalar_tensor_tensor(tabs(q), turn, -lo, tabs(q), ALU.mult, ALU.add))
                    if q == 0:
                        chain(dve.tensor_scalar(tabs(q), tabs(q), float(np.pi / 2), None, ALU.add))
                    dve.tensor_scalar(tabs(q), tabs(q), 3.1415925, -3.1415925, ALU.min, ALU.max).then_inc(s["arg"], 1)
                dve.wait_ge(s["sin"], 2)
                chain(dve.tensor_scalar(tabs(1), tabs(1), sign, None, ALU.mult))

            def rope(x, swapped, tabs, n, done):
                tmp = scr[0:n, 0, :]
                chain(dve.tensor_tensor(tmp, swapped, tabs(1)[0:n], ALU.mult))
                chain(dve.tensor_tensor(x, x, tabs(0)[0:n], ALU.mult))
                dve.tensor_tensor(x, x, tmp, ALU.add).then_inc(done, 1)

            dve.wait_ge(ld_const, 64)
            dve.wait_ge(s_ada["exp"], 1)
            chain(dve.tensor_scalar(sc1[:, :], sc1[:, :], 1.0, None, ALU.add))
            chain(dve.reciprocal(sc1[:, :], sc1[:, :]))
            dve.tensor_tensor(sc[:, :], sc1[:, :], col("c", 0, 8), ALU.mult).then_inc(s_ada["silu"], 1)
            dve.wait_ge(s_ada["done"], 24)
            dve.tensor_tensor(mod[:, :], ps[:, 0, 0:48], col("b_ada", 0, 48), ALU.add).then_inc(s_ada["mod"], 1)
            dve.wait_ge(s_ada["mod"], 1)
            for q, (g, name) in enumerate(((gain1, "g_norm1"), (gain2, "g_norm2"))):
                chain(dve.tensor_scalar(g[:, :], mod[:, 8 + 24 * q:16 + 24 * q], 1.0, None, ALU.add))
                dve.tensor_tensor(g[:, :], g[:, :], col(name, 0, 8), ALU.mult).then_inc(s_ada["mod"], 1)
            norm("norm1", lambda k: xT[:, k, :], KT, dstL=hL, dstH=hH)
            split_lo_at(dve, 0)
            split_lo_at(dve, 1)
            dve.wait_ge(s_norm["lo"], n_at("norm1", "lo") + KT)
            rope_tables(s_tr, lambda q: rope_r[:, q, :], posi[:, :], col("inv64"), col("sign64"))
            split_lo_at(dve, 2)
            split_lo_at(dve, 3)
            for t in range(8):
                if t % 2 == 0:
                    split_lo_at(dve, C_RQK + t // 2 + 2)
                dve.wait_ge(s_rr["perm"], t + 1)
                rope(qk[:, t, :], ps[:, 2 + t % 2, :], lambda q: rope_r[:, q, :], P, s_rr["roped"])
                dve.wait_ge(s_rr["roped"], t + 1)
            split_lo_at(dve, C_RG + 2)
            split_lo_at(dve, C_RG + 3)
            for j in range(8):
                c, tt = j // TT, j % TT
                dve.wait_ge(s_rp["proj"], 4 + j + 1)
                dve.tensor_copy(rv[:, tt, c * 256:(c + 1) * 256], ps[:, 4 + j % 2, 0:256]).then_inc(s_rp["value"], 1)
            split_lo_at(dve, C_RV + 2)
            split_lo_at(dve, C_RV + 3)
            for u in range(RET_H * TT):
                h, J = u // TT, u % TT
                n = T - P * J
                dve.wait_ge(s_rt["scores"], u + 1)
                dve.wait_ge(s_rt[f"ld{h % 2}"], 16 * (h // 2 + 1))
                if u >= 2:
                    dve.wait_ge(s_rt["y"], u - 1)
                dve.tensor_tensor(scr[:, 1 + u % 2, 0:n], ps[:, u % 2, 0:n], decay[h % 2][:, 0:n],
                                  ALU.mult).then_inc(s_rt["decayed"], 1)
            for m in range(4):
                y = qk[:, m, :]
                dve.wait_ge(s_rn["mean"], m + 1)
                dve.tensor_tensor(y, y, ps[:, 6, :], ALU.subtract).then_inc(s_rn["cent"], 1)
                dve.wait_ge(s_rn["var"], m + 1)
                chain(dve.tensor_scalar(scr[:, 2, :], ps[:, 7, :], EPS, None, ALU.add))
                dve.reciprocal(scr[:, 4, :], scr[:, 2, :]).then_inc(s_rn["rec"], 1)
                dve.wait_ge(s_rn["gexp"], m + 1)
                chain(dve.tensor_scalar(scr[:, 7, :], scr[:, 5, :], 1.0, None, ALU.add))
                chain(dve.reciprocal(scr[:, 8, :], scr[:, 7, :]))
                chain(dve.tensor_tensor(scr[:, 8, :], scr[:, 8, :], rg[:, m, :], ALU.mult))
                chain(dve.tensor_tensor(scr[:, 5, :], scr[:, 2, :], scr[:, 3, :], ALU.mult))
                chain(dve.tensor_tensor(scr[:, 5, :], scr[:, 5, :], scr[:, 3, :], ALU.mult))
                chain(dve.tensor_scalar(scr[:, 5, :], scr[:, 5, :], -0.5, 1.5, ALU.mult, ALU.add))
                chain(dve.tensor_tensor(scr[:, 6, :], scr[:, 5, :], scr[:, 3, :], ALU.mult))
                chain(dve.tensor_tensor(y, y, scr[:, 6, :], ALU.mult))
                dve.scalar_tensor_tensor(y, y, col("g_ret", m), scr[:, 8, :], ALU.mult,
                                         ALU.mult).then_inc(s_rn["yn"], 1)
                dve.wait_ge(s_rn["hi"], m + 1)
                dve.tensor_tensor(hL[:, 4 + m, :], y, hH[:, 4 + m, :], ALU.subtract).then_inc(s_rn["lo"], 1)
            norm("normq", lambda k: lat[:, k, :], 2, dstL=qnL, dstH=qnH)
            norm("normkv", lambda k: lat[:, 2, :], 1, dstL=kvL, dstH=kvH)
            dve.wait_ge(s_norm["lo"], n_at("normkv", "lo") + 1)
            rope_tables(s_tm, lambda q: scr[:, 7 + q, :], posi[:, :], col("inv96"), col("sign96"))
            mla_tabs = lambda q: scr[:, 7 + q, :]
            dve.wait_ge(s_mr["perm"], 1)
            rope(lat[0:MLA_QK, 3, :], ps[0:MLA_QK, 2, :], mla_tabs, MLA_QK, s_mr["kr"])
            dve.wait_ge(s_mr["kr"], 1)
            for h in range(MLA_H):
                dve.tensor_copy(kh[NOPE:MLA_QK, h, :], lat[NOPE:MLA_QK, 3, :]).then_inc(s_mr["kr"], 1)
            for h in range(MLA_H):
                dve.wait_ge(s_mr["perm"], h + 2)
                rope(qh[0:MLA_QK, h, :], ps[0:MLA_QK, 2 + (h + 1) % 2, :], mla_tabs, MLA_QK, s_mr["roped"])
                dve.wait_ge(s_mr["roped"], h + 1)
            split_lo_at(dve, C_OUT)
            for tt in range(TT):
                dve.wait_ge(s_mk["v"], tt + 1)
                dve.wait_ge(s_mr["kr"], MLA_H + 1)
                dve.tensor_copy(lat[:, tt, :], ps[:, 4 + tt % 2, :]).then_inc(s_mk["vcopied"], 1)
            split_lo_at(dve, C_OUT + 1)

            def mla_probs(u):
                n = (u % TT + 1) * P
                dve.wait_ge(s_ma["exp"], u + 1)
                chain(dve.reciprocal(stats[:, 3, u:u + 1], stats[:, 2, u:u + 1]))
                dve.tensor_scalar(scr[:, u % 2, 0:n], scr[:, u % 2, 0:n], stats[:, 3, u:u + 1], None,
                                  ALU.mult).then_inc(s_ma["probs"], 1)
                if u % (2 * TT) == 2 * TT - 1 and u >= 2 * TT:
                    mla_low(u // (2 * TT) - 1)

            def mla_low(m):
                dve.wait_ge(s_ma["hi"], m + 1)
                dve.tensor_tensor(hL[:, m, :], ps[:, 4 + m % 2, :], hH[:, m, :], ALU.subtract).then_inc(s_ma["lo"], 1)

            for u in range(MLA_H * TT):
                qt = u % TT
                n = (qt + 1) * P
                dve.wait_ge(s_ma["scores"], u + 1)
                diag = ps[:, u % 2, qt * P:(qt + 1) * P]
                chain(dve.tensor_tensor(diag, diag, tab[:, CAUSAL, :], ALU.add))
                chain(dve.reduce_max(stats[:, 0, u:u + 1], ps[:, u % 2, 0:n], AX))
                dve.tensor_scalar(stats[:, 1, u:u + 1], stats[:, 0, u:u + 1], -(MLA_QK ** -0.5), None,
                                  ALU.mult).then_inc(s_ma["negmax"], 1)
                if u >= 1:
                    mla_probs(u - 1)
            mla_probs(MLA_H * TT - 1)
            mla_low(3)
            for k in range(4):
                split_lo_at(dve, C_OUT + k + 2)
                for j in range(2):
                    t = 2 * k + j
                    dve.wait_ge(s_wo1["proj"], t + 1)
                    dve.scalar_tensor_tensor(xT[:, t, :], ps[:, t % 4, :], mod[:, 16 + t:17 + t], xT[:, t, :],
                                             ALU.mult, ALU.add).then_inc(s_wo1["added"], 1)
            dve.wait_ge(s_wo1["added"], KT)
            norm("norm2", lambda k: xT[:, k, :], KT, dstL=hL, dstH=hH)

            def top16(vals, masked, values, indices):
                chain(dve.max(values[:, 0:8], vals))
                chain(dve.max_index(indices[:, 0:8], values[:, 0:8], vals))
                chain(dve.match_replace(masked, values[:, 0:8], vals, FAR_BELOW))
                chain(dve.max(values[:, 8:16], masked))
                chain(dve.max_index(indices[:, 8:16], values[:, 8:16], masked))

            for t in range(16):
                if t % 2 == 0 and t // 2 < 7:
                    split_lo_at(dve, C_QUERY + t // 2 + 2)
                dve.wait_ge(s_q["scopied"], t + 1)
                for tt in range(TT):
                    top16(sc_k[t % 2][:, tt, :], sc_m[:, tt, :], topv[:, tt, t, :], topi[:, tt, t, :])
                dve.tensor_copy(topf[:, :, t, :], topi[:, :, t, :]).then_inc(s_q["top"], 1)
            dve.wait_ge(s_q["top"], 16)
            for tt in range(TT):
                v = topv[:, tt, :, :].rearrange("p (h two) a -> p h two a", two=2)
                f = topf[:, tt, :, :].rearrange("p (h two) a -> p h two a", two=2)
                c4 = cand[:, :, :].rearrange("p h (a b) -> p h a b", a=TOPK)
                e4 = cand2[:, :, :].rearrange("p h (k a) -> p h k a", a=TOPK)
                for h in range(PEER_H):
                    op = dve.tensor_tensor(c4[:, h], v[:, h, 0, :].unsqueeze(2).broadcast_to([P, TOPK, TOPK]),
                                           v[:, h, 1, :].unsqueeze(1).broadcast_to([P, TOPK, TOPK]), ALU.add)
                chain(op)
                for h in range(PEER_H):
                    top16(cand[:, h, :], cand2[:, h, :], best[:, h, :], pos[:, h, :])
                chain(dve.tensor_scalar(posu[:, 0], pos[:, :, :], 4, None, ALU.logical_shift_right))
                chain(dve.tensor_scalar(posu[:, 1], pos[:, :, :], TOPK - 1, None, ALU.bitwise_and))
                chain(dve.tensor_copy(posf[:, :, :, :], posu[:, :, :, :]))
                chain(dve.tensor_copy(gsum[:, 0, :], best[:, :, 0]))
                dve.tensor_tensor(best[:, :, :], best[:, :, :], gsum[:, 0, :].unsqueeze(2).broadcast_to(
                    [P, PEER_H, TOPK]), ALU.subtract).then_inc(s_q["negbest"], 1)
                iota = tab[:, IOTA, 0:TOPK]
                for half in range(2):
                    for h in range(PEER_H):
                        op = dve.tensor_tensor(e4[:, h], iota.unsqueeze(1).broadcast_to([P, TOPK, TOPK]),
                                               posf[:, half, h, :].unsqueeze(2).broadcast_to([P, TOPK, TOPK]),
                                               ALU.is_equal)
                    chain(op)
                    for h in range(PEER_H):
                        op = dve.tensor_tensor(e4[:, h], e4[:, h],
                                               f[:, h, half, :].unsqueeze(1).broadcast_to([P, TOPK, TOPK]), ALU.mult)
                    chain(op)
                    if half == 0 and tt >= 1:
                        dve.wait_ge(s_q["tcopied"], 3 * tt)
                    dve.tensor_reduce(chosen[:, half, :], cand2[:, :, :].rearrange(
                        "p h (k a) -> p (h k) a", a=TOPK), AX, ALU.add).then_inc(s_q["chosen"], 1)
                    dve.wait_ge(s_q["chosen"], 3 * tt + half + 1)
                dve.wait_ge(s_q["gexp"], tt + 1)
                chain(dve.tensor_reduce(gsum[:, 0, :], best[:, :, :], AX, ALU.add))
                chain(dve.reciprocal(gsum[:, 1, :], gsum[:, 0, :]))
                dve.tensor_tensor(chosen[:, 2, :].rearrange("p (h k) -> p h k", k=TOPK), best[:, :, :],
                                  gsum[:, 1, :].unsqueeze(2).broadcast_to([P, PEER_H, TOPK]),
                                  ALU.mult).then_inc(s_q["chosen"], 1)
                dve.wait_ge(s_q["chosen"], 3 * tt + 3)
            dve.wait_ge(s_q["tcopied"], 3 * TT)

            def gates(par, tok):
                for q in range(4):
                    dve.tensor_scalar(oneJ[par][:, q, :], tab[:, IOTA, :], fromsel[:, 1, bass.ds(tok + q, 1)], None,
                                      ALU.is_equal)
                    ins = dve.tensor_scalar(oneI[par][:, q, :], tab[:, IOTA, :], fromsel[:, 0, bass.ds(tok + q, 1)],
                                            fromsel[:, 2, bass.ds(tok + q, 1)], ALU.is_equal, ALU.mult)
                ins.then_inc(s_w["ones"], 1)

            for par in range(2):
                gates(par, 4 * par)
            with dve.Fori(1, T // 8) as i:
                for par in range(2):
                    dve.wait_ge(s_w["prod"], 2 * i + par - 1)
                    gates(par, i * 8 + 4 * par)

            def peer_dve(s0, i=0, has_a=True, splits=2, has_o=True):
                for q in range(splits):
                    split_lo(dve, C_PEER + 2 * s0 + 1 + q, CHUNK, i, 8)
                if has_a:
                    par = (s0 // 2) % 2
                    dve.wait_ge(s_e[f"ld{par}"], 16 * (s0 // 4 + 1) + 16 * i)
                    for m in range(2):
                        dve.wait_ge(s_e["gelu"], 2 * s0 + m + 1 + 8 * i)
                        if s0 >= 1:
                            dve.wait_ge(s_e["lo"], 2 * s0 + m - 1 + 8 * i)
                        dve.tensor_tensor(wa[m][:, :].rearrange("p (b t) -> p b t", b=NTB),
                                          ga[m][:, :].rearrange("p (b t) -> p b t", b=NTB),
                                          wg[par][:, :, 2 * (s0 % 2) + m, :], ALU.mult).then_inc(s_e["wa"], 1)
                    for m in range(2):
                        dve.wait_ge(s_e["hi"], 2 * s0 + m + 1 + 8 * i)
                        dve.tensor_tensor(waL[s0 % 2][m][:, :], wa[m][:, :], waH[s0 % 2][m][:, :],
                                          ALU.subtract).then_inc(s_e["lo"], 1)
                if has_o:
                    for d in range(KT):
                        dve.wait_ge(s_e["o"], KT * (s0 - 1) + d + 1 + 4 * KT * i)
                        if s0 >= 2:
                            dve.wait_ge(s_e["added"], KT * (s0 - 2) + d + 1 + 4 * KT * i)
                        dve.scalar_tensor_tensor(xT[:, d, :], ps[:, 4 + d % 4, :], mod[:, 40 + d:41 + d],
                                                 xT[:, d, :], ALU.mult, ALU.add).then_inc(s_e["added"], 1)

            peer_dve(0, has_o=False)
            peer_dve(1)
            with dve.Fori(0, PEER_STEPS // 4 - 1) as i:
                for q in range(4):
                    peer_dve(2 + q, i)
            for s in range(PEER_STEPS - 2, PEER_STEPS):
                peer_dve(s, splits=2 if s < PEER_STEPS - 1 else 1)
            peer_dve(PEER_STEPS, has_a=False, splits=0)
            norm("final1", lambda k: xT[:, k, :], KT, dst=True)
            dve.wait_ge(s_norm["t"], n_at("final1", "t") + KT)
            dve.memset(hp[:, :, :], 0.0).then_inc(s_p["filled"], 1)
            norm("mix0", lambda k: xT[:, k, :], KT, dst=True)
            split_lo_at(dve, C_POOL)
            dve.wait_ge(s_norm["t"], n_at("mix0", "t") + KT)
            dve.wait_ge(s_p["ld"], 16)
            W2 = T + 2 * PAD
            for g in range(len(WINDOWS)):
                if g >= 2:
                    dve.wait_ge(s_p["lo"], g - 1)
                h2 = hp[:, 2 * g:2 * g + 2, :]
                a = h2
                for r in range(g + 1):
                    e = 1 << r
                    l, rt = (1, 0) if r == 0 else (e // 2, e // 2)
                    chain(dve.tensor_tensor(wbuf[r % 2][:, :, e:W2 - e], a[:, :, e - l:W2 - e - l],
                                            a[:, :, e + rt:W2 - e + rt], ALU.add))
                    a = wbuf[r % 2]
                rec = recips[:, g, :].unsqueeze(1).broadcast_to([P, 2, T])
                mean = wbuf[(g + 1) % 2][:, :, 0:T]
                chain(dve.tensor_tensor(mean, a[:, :, PAD:PAD + T], rec, ALU.mult))
                dve.tensor_tensor(win[g % 2][:, :, 0:T], mean, h2[:, :, PAD:PAD + T],
                                  ALU.subtract).then_inc(s_p["pooled"], 1)
                dve.wait_ge(s_p["hi"], g + 1)
                dve.tensor_tensor(hL[:, 2 * g:2 * g + 2, :], win[g % 2][:, :, 0:T], hH[:, 2 * g:2 * g + 2, :],
                                  ALU.subtract).then_inc(s_p["lo"], 1)
            split_lo_at(dve, C_POOL + 1)
            split_lo_at(dve, C_POOL + 2)
            for t in range(KT):
                dve.wait_ge(s_p["proj"], t + 1)
                dve.scalar_tensor_tensor(xT[:, t, :], ps[:, t % 4, :], col("pool_scale", t), xT[:, t, :],
                                         ALU.mult, ALU.add).then_inc(s_p["added"], 1)
            dve.wait_ge(s_p["added"], KT)

            def ffn_dve(l, c, s0, i=0, has_a=True, splits=2, has_o=True):
                s = s_f[l]
                for q in range(splits):
                    k = c + 2 * s0 + 1 + q
                    split_lo(dve, k, CHUNK if is_up(k - c) else D, i, 4)
                if has_a:
                    b0 = VEC[f"conv{l}"][0]

                    def cv(j):
                        if isinstance(i, int):
                            return vec[:, b0 + 4 * s0 + j:b0 + 4 * s0 + j + 1]
                        return vec[:, bass.ds(b0 + 4 * s0 + j + 8 * i, 1)]

                    g, u = ps[:, 2 * (s0 % 2), :], ps[:, 2 * (s0 % 2) + 1, :]
                    y = gcv[s0 % 2]
                    dve.wait_ge(s["proj"], 2 * s0 + 2 + 4 * i)
                    chain(dve.tensor_scalar(y[:, :], g, cv(1), cv(3), ALU.mult, ALU.add))
                    chain(dve.scalar_tensor_tensor(y[:, 1:T], g[:, 0:T - 1], cv(0), y[:, 1:T], ALU.mult, ALU.add))
                    dve.scalar_tensor_tensor(y[:, 0:T - 1], g[:, 1:T], cv(2), y[:, 0:T - 1], ALU.mult,
                                             ALU.add).then_inc(s["conv"], 1)
                    dve.wait_ge(s["gelu"], s0 + 1 + 2 * i)
                    if s0 >= 2:
                        dve.wait_ge(s["lo"], s0 - 1 + 2 * i)
                    dve.tensor_tensor(fa[s0 % 2][:, :], gel[s0 % 2][:, :], u, ALU.mult).then_inc(s["act"], 1)
                    dve.wait_ge(s["hi"], s0 + 1 + 2 * i)
                    dve.tensor_tensor(faL[s0 % 2][:, :], fa[s0 % 2][:, :], faH[s0 % 2][:, :],
                                      ALU.subtract).then_inc(s["lo"], 1)
                if has_o:
                    for d in range(KT):
                        dve.wait_ge(s["o"], KT * (s0 - 1) + d + 1 + 2 * KT * i)
                        if s0 >= 2:
                            dve.wait_ge(s["added"], KT * (s0 - 2) + d + 1 + 2 * KT * i)
                        dve.tensor_tensor(xT[:, d, :], xT[:, d, :], ps[:, 4 + d % 4, :],
                                          ALU.add).then_inc(s["added"], 1)

            def ffn_vector(l, c):
                ffn_dve(l, c, 0, splits=0, has_o=False)
                split_lo(dve, c + 2, D)
                ffn_dve(l, c, 1)
                n0 = chain.n
                with dve.Fori(0, FT // 2 - 2) as i:
                    chain.n = n0 + 4 * i
                    for q in range(2):
                        ffn_dve(l, c, 2 + q, i)
                chain.n = n0 + 4 * (FT // 2 - 2)
                ffn_dve(l, c, FT - 2)
                ffn_dve(l, c, FT - 1, splits=1)
                ffn_dve(l, c, FT, has_a=False, splits=0)

            norm("ffn0", lambda k: xT[:, k, :], KT, dstL=hL, dstH=hH)
            ffn_vector(0, C_FFN1)
            split_lo_at(dve, C_QKV)
            split_lo_at(dve, C_QKV + 1)
            dve.wait_ge(s_f[0]["added"], KT * FT)
            norm("mix1", lambda k: xT[:, k, :], KT, dstL=hL, dstH=hH)
            dve.wait_ge(ld_const, 80)
            rope_tables(s_td, lambda q: rope_d[:, q, :], posi[:, :], col("inv64"), col("sign64"))
            for t in range(16):
                if t % 2 == 0:
                    split_lo_at(dve, C_QKV + t // 2 + 2)
                dve.wait_ge(s_dr["perm"], t + 1)
                rope(dqk[:, t, :], ps[:, 2 + t % 2, :], lambda q: rope_d[:, q, :], P, s_dr["roped"])
                dve.wait_ge(s_dr["roped"], t + 1)
            for j in range(16):
                c, tt = j // TT, j % TT
                if tt == 0:
                    split_lo_at(dve, C_QKV + 8 + c + 2)
                dve.wait_ge(s_dv["v"], j + 1)
                dve.tensor_copy(dv[:, tt, c * 256:(c + 1) * 256], ps[:, 4 + j % 2, 0:256]).then_inc(s_dv["copied"], 1)
            for q in range(2):
                op = dve.tensor_tensor_reduce(out=sinkv[:, 0:HD], in0=lams[:, 2 * q, :], in1=lams[:, 2 * q + 1, :],
                                              scale=1.0, scalar=0.0, op0=ALU.mult, op1=ALU.add,
                                              accum_out=small[:, q:q + 1])
                if q == 0:
                    chain(op)
                else:
                    op.then_inc(s_da["lam"], 1)
            dve.wait_ge(s_da["lam"], 2)
            chain(dve.tensor_tensor(small[:, 4:5], small[:, 3:4], small[:, 2:3], ALU.subtract))
            chain(dve.tensor_scalar(small[:, 5:6], small[:, 4:5], -LAM_INIT, None, ALU.add))

            def diff_probs(u):
                p0, p1 = scr[:, 2 * (u % 2), :], scr[:, 2 * (u % 2) + 1, :]
                dve.wait_ge(s_da["exp"], 2 * u + 2)
                for c in range(2):
                    chain(dve.reciprocal(stats[:, 4 * c + 3, u:u + 1], stats[:, 4 * c + 2, u:u + 1]))
                chain(dve.tensor_tensor(stats[:, 7, u:u + 1], stats[:, 7, u:u + 1], small[:, 5:6], ALU.mult))
                chain(dve.tensor_scalar(p1, p1, stats[:, 7, u:u + 1], None, ALU.mult))
                if u >= 1:
                    dve.wait_ge(s_da["trans"], u)
                dve.scalar_tensor_tensor(scr[:, 4, :], p0, stats[:, 3, u:u + 1], p1, ALU.mult,
                                         ALU.add).then_inc(s_da["probs"], 1)

            for u in range(DIFF_H * TT):
                for c in range(2):
                    dve.wait_ge(s_da["scores"], 2 * u + c + 1)
                    chain(dve.reduce_max(stats[:, 4 * c, u:u + 1], ps[:, 2 * (u % 2) + c, :], AX))
                    dve.tensor_scalar(stats[:, 4 * c + 1, u:u + 1], stats[:, 4 * c, u:u + 1], -(HD ** -0.5), None,
                                      ALU.mult).then_inc(s_da["negmax"], 1)
                if u >= 1:
                    diff_probs(u - 1)
            diff_probs(DIFF_H * TT - 1)
            for h in range(DIFF_H):
                dve.wait_ge(s_dn["sum"], h + 1)
                chain(dve.tensor_scalar(scr[:, 2, :], ps[:, h % 2, :], 1.0 / P, SUBLN_EPS, ALU.mult, ALU.add))
                rsqrt(scr[:, 2, :], scr[:, 1, :], s_dn["rec"], s_dn["root"], h + 1)
                chain(dve.tensor_tensor(dqk[:, h, :], dqk[:, h, :], scr[:, 1, :], ALU.mult))
                dve.tensor_scalar(dqk[:, h, :], dqk[:, h, :], col("subln"), 1.0 - LAM_INIT, ALU.mult,
                                  ALU.mult).then_inc(s_dn["yn"], 1)
                dve.wait_ge(s_dn["hi"], h + 1)
                dve.tensor_tensor(hL[:, h, :], dqk[:, h, :], hH[:, h, :], ALU.subtract).then_inc(s_dn["lo"], 1)
            for k in range(4):
                split_lo_at(dve, C_WO + k + 2)
                for j in range(2):
                    t = 2 * k + j
                    dve.wait_ge(s_wo2["proj"], t + 1)
                    dve.tensor_tensor(xT[:, t, :], xT[:, t, :], ps[:, t % 4, :], ALU.add).then_inc(s_wo2["added"], 1)
            dve.wait_ge(s_wo2["added"], KT)
            norm("ffn1", lambda k: xT[:, k, :], KT, dstL=hL, dstH=hH)
            ffn_vector(1, C_FFN2)
            dve.wait_ge(s_f[1]["added"], KT * FT)
            norm("final2", lambda k: xT[:, k, :], KT, dst=True)

        @block.tensor
        def _(pe):
            def norm(name, nkt):
                s = s_norm
                for k in range(nkt):
                    pe.wait_ge(s["sq"], n_at(name, "sq") + k + 1)
                    pe.matmul(ps[:, 7, :], tab[:, ONES, :], scr[:, k % 2, :], start=k == 0,
                              stop=k == nkt - 1).then_inc(s["sum"], 1)

            def chunk(k, i=0, per=0):
                pe.wait_ge(w_split, k + 1 + i * per)

            def tile(k, j, dst, done):
                product(pe, k, dst, slice(j * P, (j + 1) * P), KT, 256, hH, hL, done, j == 0)

            pe.wait_ge(s_ada["silu"], 1)
            with pe.Fori(0, 6) as i:
                for a in range(4):
                    pe.wait_ge(ld_ada[a], 16 * i + 16)
                    w = ada[a][:, :].rearrange("p (k n) -> p k n", k=KT)
                    for j in range(2):
                        for k in range(KT):
                            m = pe.matmul(ps[:, 0, bass.ds(i * 8 + 2 * a + j, 1)], w[:, k, j * P:(j + 1) * P],
                                          sc[:, k:k + 1], start=k == 0, stop=k == KT - 1)
                    m.then_inc(s_ada["done"], 1)
            norm("norm1", KT)
            pe.wait_ge(s_norm["lo"], n_at("norm1", "lo") + KT)
            pe.wait_ge(s_ada["mod"], 1)
            for t in range(4):
                if t % 2 == 0:
                    chunk(C_LAT + t // 2)
                if t >= 2:
                    pe.wait_ge(s_lat["copied"], t - 1)
                if t < 2:
                    tile(C_LAT, t, ps[:, t % 2, :], s_lat["proj"])
                else:
                    n = P if t == 2 else MLA_QK
                    product(pe, C_KV, ps[0:n, t % 2, :], slice((t - 2) * P, (t - 2) * P + n), KT, 224, hH, hL,
                            s_lat["proj"], t == 2)
            for t in range(9):
                if t < 8:
                    if t % 2 == 0:
                        chunk(C_RQK + t // 2)
                    if t >= 2:
                        pe.wait_ge(s_rr["copied"], t - 1)
                    else:
                        pe.wait_ge(s_lat["copied"], t + 3)
                    tile(C_RQK + t // 2, t % 2, ps[:, t % 2, :], s_rr["proj"])
                if t >= 1:
                    pe.wait_ge(s_rr["copied"], t)
                    if t >= 3:
                        pe.wait_ge(s_rr["roped"], t - 2)
                    pe.matmul(ps[:, 2 + (t - 1) % 2, :], tab[:, SWAP64, :], qk[:, t - 1, :], start=True,
                              stop=True).then_inc(s_rr["perm"], 1)
            for t in range(4):
                if t % 2 == 0:
                    chunk(C_RG + t // 2)
                if t >= 2:
                    pe.wait_ge(s_rp["gate"], t - 1)
                tile(C_RG + t // 2, t % 2, ps[:, t % 2, :], s_rp["proj"])
            for j in range(8):
                c, tt = C_RV + j // TT, j % TT
                if tt == 0:
                    chunk(c)
                if j >= 2:
                    pe.wait_ge(s_rp["value"], j - 1)
                wh = wH[c % SLOTS][:, :].rearrange("p (k n) -> p k n", k=KT)
                wl = wL[c % SLOTS][:, :].rearrange("p (k n) -> p k n", k=KT)
                rows = slice(tt * P, (tt + 1) * P)
                for k in range(KT):
                    m = three(pe, ps[:, 4 + j % 2, 0:256], hH[:, k, rows], hL[:, k, rows], wh[:, k, :], wl[:, k, :],
                              k == 0, k == KT - 1, tt == 0 and k == 0)
                m.then_inc(s_rp["proj"], 1)
            pe.wait_ge(s_rr["roped"], 8)
            pe.wait_ge(s_rp["gate"], 4)
            pe.wait_ge(s_rp["value"], 8)

            def ret_y(u):
                h, J = u // TT, u % TT
                m, half = h // 2, (h % 2) * RET_D
                pe.wait_ge(s_rt["decayed"], u + 1)
                if m >= 2 and u % (2 * TT) == 0:
                    pe.wait_ge(s_rt["ycopied"], m - 1)
                pe.matmul(ps[half:half + RET_D, 4 + m % 2, J * P:T], rv[:, J, h * RET_D:(h + 1) * RET_D],
                          scr[:, 1 + u % 2, 0:T - J * P], start=J == 0, stop=J == TT - 1).then_inc(s_rt["y"], 1)

            for u in range(RET_H * TT):
                h, J = u // TT, u % TT
                half = (h % 2) * RET_D
                if u >= 2:
                    pe.wait_ge(s_rt["decayed"], u - 1)
                pe.matmul(ps[:, u % 2, 0:T - J * P], qk[half:half + RET_D, 4 + h // 2, J * P:(J + 1) * P],
                          qk[half:half + RET_D, h // 2, J * P:T], start=True, stop=True).then_inc(s_rt["scores"], 1)
                if u >= 1:
                    ret_y(u - 1)
            ret_y(RET_H * TT - 1)
            for m in range(4):
                pe.wait_ge(s_rt["ycopied"], m + 1)
                pe.matmul(ps[:, 6, :], tab[:, BLOCKMEAN, :], qk[:, m, :], start=True,
                          stop=True).then_inc(s_rn["mean"], 1)
                pe.wait_ge(s_rn["sq"], m + 1)
                pe.matmul(ps[:, 7, :], tab[:, BLOCKMEAN, :], scr[:, 1, :], start=True,
                          stop=True).then_inc(s_rn["var"], 1)
            norm("normq", 2)
            norm("normkv", 1)
            pe.wait_ge(s_lat["copied"], 4)
            pe.matmul(ps[0:MLA_QK, 2, :], tab[0:MLA_QK, SWAP96, 0:MLA_QK], lat[0:MLA_QK, 3, :], start=True,
                      stop=True).then_inc(s_mr["perm"], 1)
            pe.wait_ge(s_norm["lo"], n_at("normkv", "lo") + 1)
            chunk(C_UQ)
            for h in range(MLA_H + 1):
                if h < MLA_H:
                    if h >= 2:
                        pe.wait_ge(s_mr["copied"], h - 1)
                    product(pe, C_UQ, ps[0:MLA_QK, h % 2, :], slice(h * MLA_QK, (h + 1) * MLA_QK), 2,
                            MLA_H * MLA_QK, qnH, qnL, s_mr["proj"], h == 0)
                if h >= 1:
                    pe.wait_ge(s_mr["copied"], h)
                    if h == 2:
                        pe.wait_ge(s_mr["kr"], 1)
                    if h >= 3:
                        pe.wait_ge(s_mr["roped"], h - 2)
                    pe.matmul(ps[0:MLA_QK, 2 + h % 2, :], tab[0:MLA_QK, SWAP96, 0:MLA_QK], qh[0:MLA_QK, h - 1, :],
                              start=True, stop=True).then_inc(s_mr["perm"], 1)
            chunk(C_UKV)
            for h in range(MLA_H):
                if h >= 2:
                    pe.wait_ge(s_mk["kcopied"], h - 1)
                product(pe, C_UKV, ps[:, h % 2, :], slice(h * P, (h + 1) * P), 1, MLA_H * P, kvH, kvL, s_mk["k"],
                        h == 0)
            vh = wH[C_UKV % SLOTS][:, 0:MLA_H * P].rearrange("p (h n) -> p h n", n=P)[:, :, NOPE:P]
            vl = wL[C_UKV % SLOTS][:, 0:MLA_H * P].rearrange("p (h n) -> p h n", n=P)[:, :, NOPE:P]
            for tt in range(TT):
                if tt >= 2:
                    pe.wait_ge(s_mk["vcopied"], tt - 1)
                rows = slice(tt * P, (tt + 1) * P)
                dst = ps[:, 4 + tt % 2, :].rearrange("p (h n) -> p h n", n=MLA_V)
                three(pe, dst, kvH[:, 0, rows], kvL[:, 0, rows], vh, vl, True, True).then_inc(s_mk["v"], 1)
            pe.wait_ge(s_mr["roped"], MLA_H)
            pe.wait_ge(s_mr["kr"], MLA_H + 1)
            pe.wait_ge(s_mk["kcopied"], MLA_H)
            pe.wait_ge(s_mk["vcopied"], TT)

            def mla_rest(u):
                h, qt = u // TT, u % TT
                pe.wait_ge(s_ma["probs"], u + 1)
                if u >= 2:
                    pe.wait_ge(s_ma["pt"], u - 1)
                for k in range(qt + 1):
                    m = pe.transpose(ps[:, 2 + u % 2, k * P:(k + 1) * P], scr[:, u % 2, k * P:(k + 1) * P],
                                     tab[:, IDENT, :])
                m.then_inc(s_ma["trans"], 1)
                if qt == TT - 1:
                    pe.wait_ge(s_ma["pt"], u + 1)
                    mm, half = h // 2, (h % 2) * MLA_V
                    if mm >= 2 and h % 2 == 0:
                        pe.wait_ge(s_ma["lo"], mm - 1)
                    for k in range(TT):
                        m = pe.matmul(ps[half:half + MLA_V, 4 + mm % 2, k * P:T], lat[:, k, h * MLA_V:(h + 1) * MLA_V],
                                      scr[:, 2 + k, k * P:T], start=k == 0, stop=k == TT - 1)
                    m.then_inc(s_ma["o"], 1)

            for u in range(MLA_H * TT):
                h, qt = u // TT, u % TT
                n = (qt + 1) * P
                if u >= 2:
                    pe.wait_ge(s_ma["exp"], u - 1)
                pe.matmul(ps[:, u % 2, 0:n], qh[0:MLA_QK, h, qt * P:n], kh[0:MLA_QK, h, 0:n], start=True,
                          stop=True).then_inc(s_ma["scores"], 1)
                if u >= 1:
                    mla_rest(u - 1)
            mla_rest(MLA_H * TT - 1)
            pe.wait_ge(s_ma["lo"], 4)
            pe.wait_ge(s_rn["lo"], 4)
            for t in range(KT):
                if t % 2 == 0:
                    chunk(C_OUT + t // 2)
                if t >= 4:
                    pe.wait_ge(s_wo1["added"], t - 3)
                tile(C_OUT + t // 2, t % 2, ps[:, t % 4, :], s_wo1["proj"])
            norm("norm2", KT)
            pe.wait_ge(s_norm["lo"], n_at("norm2", "lo") + KT)
            pe.wait_ge(s_q["keys"], 16)

            def key_scores(t):
                pe.wait_ge(s_q["copied"], t + 1)
                if t >= 2:
                    pe.wait_ge(s_q["scopied"], t - 1)
                for tt in range(TT):
                    m = pe.matmul(ps[:, 2 + t % 2, tt * P:(tt + 1) * P], qp[t % 2][:, tt * P:(tt + 1) * P],
                                  keysT[:, t % 2, :], start=True, stop=True)
                m.then_inc(s_q["scores"], 1)

            for t in range(16):
                if t % 2 == 0:
                    chunk(C_QUERY + t // 2)
                if t >= 2:
                    pe.wait_ge(s_q["copied"], t - 1)
                tile(C_QUERY + t // 2, t % 2, ps[:, t % 2, :], s_q["proj"])
                if t >= 1:
                    key_scores(t - 1)
            key_scores(15)
            for tt in range(TT):
                for r in range(3):
                    pe.wait_ge(s_q["chosen"], 3 * tt + r + 1)
                    if tt >= 1:
                        pe.wait_ge(s_q["tcopied"], 3 * tt - 2 + r)
                    pe.transpose(ps[:, 4 + r, 0:P], chosen[:, r, :], tab[:, IDENT, :]).then_inc(s_q["trans"], 1)

            def spread_four(par):
                for q in range(4):
                    m = pe.matmul(ps[:, par, q * P:(q + 1) * P], oneJ[par][:, q, :], oneI[par][:, q, :], start=True,
                                  stop=True)
                m.then_inc(s_w["prod"], 1)

            for par in range(2):
                pe.wait_ge(s_w["ones"], par + 1)
                spread_four(par)
            with pe.Fori(1, T // 8) as i:
                for par in range(2):
                    pe.wait_ge(s_w["ones"], 2 * i + par + 1)
                    pe.wait_ge(s_w["copied"], 2 * i + par - 1)
                    spread_four(par)
            pe.wait_ge(s_w["copied"], T // 4)

            def peer_pe(s0, i=0, has_a=True, has_o=True):
                if has_a:
                    k = C_PEER + max(0, 2 * s0 - 1)
                    chunk(k, i, 8)
                    for m in range(2):
                        if s0 >= 2:
                            pe.wait_ge(s_e["gelu"], 2 * (s0 - 2) + m + 1 + 8 * i)
                        tile(k, m, ps[:, 2 * (s0 % 2) + m, :], s_e["a"])
                if has_o:
                    k = C_PEER + (2 * s0 if has_a else 2 * s0 - 1)
                    chunk(k, i, 8)
                    pe.wait_ge(s_e["lo"], 2 * s0 + 8 * i)
                    wh = wH[k % SLOTS][:, :].rearrange("p (m d) -> p m d", m=2)
                    wl = wL[k % SLOTS][:, :].rearrange("p (m d) -> p m d", m=2)
                    par = (s0 - 1) % 2
                    for d in range(KT):
                        if s0 > 1 or d >= 4:
                            pe.wait_ge(s_e["added"], KT * (s0 - 1) + d - 3 + 4 * KT * i)
                        for m in range(2):
                            ins = three(pe, ps[:, 4 + d % 4, :], wh[:, m, d * P:(d + 1) * P],
                                        wl[:, m, d * P:(d + 1) * P], waH[par][m][:, :], waL[par][m][:, :],
                                        m == 0, m == 1, d == 0 and m == 0)
                        ins.then_inc(s_e["o"], 1)

            peer_pe(0, has_o=False)
            peer_pe(1)
            with pe.Fori(0, PEER_STEPS // 4 - 1) as i:
                for q in range(4):
                    peer_pe(2 + q, i)
            for s in range(PEER_STEPS - 2, PEER_STEPS):
                peer_pe(s)
            peer_pe(PEER_STEPS, has_a=False)
            norm("final1", KT)
            norm("mix0", KT)
            pe.wait_ge(s_p["lo"], len(WINDOWS))
            chunk(C_POOL)
            wph = wH[C_POOL % SLOTS][:, :].rearrange("p (g k n) -> p g k n", g=4, k=2)
            wpl = wL[C_POOL % SLOTS][:, :].rearrange("p (g k n) -> p g k n", g=4, k=2)
            for t in range(KT):
                g, e = t // 2, slice((t % 2) * P, (t % 2 + 1) * P)
                if t >= 4:
                    pe.wait_ge(s_p["added"], t - 3)
                for k in range(2):
                    m = three(pe, ps[:, t % 4, :], wph[:, g, k, e], wpl[:, g, k, e], hH[:, 2 * g + k, :],
                              hL[:, 2 * g + k, :], k == 0, k == 1, t == 0 and k == 0)
                m.then_inc(s_p["proj"], 1)

            def ffn_pe(l, c, s0, i=0, has_a=True, has_o=True):
                s = s_f[l]
                if has_a:
                    k = c + max(0, 2 * s0 - 1)
                    chunk(k, i, 4)
                    if s0 >= 2:
                        pe.wait_ge(s["act"], s0 - 1 + 2 * i)
                    for m in range(2):
                        tile(k, m, ps[:, 2 * (s0 % 2) + m, :], s["proj"])
                if has_o:
                    k = c + (2 * s0 if has_a else 2 * s0 - 1)
                    chunk(k, i, 4)
                    pe.wait_ge(s["lo"], s0 + 2 * i)
                    par = (s0 - 1) % 2
                    for d in range(KT):
                        if s0 > 1 or d >= 4:
                            pe.wait_ge(s["added"], KT * (s0 - 1) + d - 3 + 2 * KT * i)
                        cols = slice(d * P, (d + 1) * P)
                        three(pe, ps[:, 4 + d % 4, :], wH[k % SLOTS][:, cols], wL[k % SLOTS][:, cols], faH[par][:, :],
                              faL[par][:, :], True, True, d == 0).then_inc(s["o"], 1)

            def ffn_tensor(l, c):
                ffn_pe(l, c, 0, has_o=False)
                ffn_pe(l, c, 1)
                with pe.Fori(0, FT // 2 - 2) as i:
                    for q in range(2):
                        ffn_pe(l, c, 2 + q, i)
                ffn_pe(l, c, FT - 2)
                ffn_pe(l, c, FT - 1)
                ffn_pe(l, c, FT, has_a=False)

            norm("ffn0", KT)
            pe.wait_ge(s_norm["lo"], n_at("ffn0", "lo") + KT)
            ffn_tensor(0, C_FFN1)
            norm("mix1", KT)
            pe.wait_ge(s_norm["lo"], n_at("mix1", "lo") + KT)
            for t in range(17):
                if t < 16:
                    if t % 2 == 0:
                        chunk(C_QKV + t // 2)
                    if t >= 2:
                        pe.wait_ge(s_dr["copied"], t - 1)
                    tile(C_QKV + t // 2, t % 2, ps[:, t % 2, :], s_dr["proj"])
                if t >= 1:
                    pe.wait_ge(s_dr["copied"], t)
                    if t >= 3:
                        pe.wait_ge(s_dr["roped"], t - 2)
                    pe.matmul(ps[:, 2 + (t - 1) % 2, :], tab[:, SWAP64, :], dqk[:, t - 1, :], start=True,
                              stop=True).then_inc(s_dr["perm"], 1)
            for j in range(16):
                c, tt = C_QKV + 8 + j // TT, j % TT
                if tt == 0:
                    chunk(c)
                if j >= 2:
                    pe.wait_ge(s_dv["copied"], j - 1)
                wh = wH[c % SLOTS][:, :].rearrange("p (k n) -> p k n", k=KT)
                wl = wL[c % SLOTS][:, :].rearrange("p (k n) -> p k n", k=KT)
                rows = slice(tt * P, (tt + 1) * P)
                for k in range(KT):
                    m = three(pe, ps[:, 4 + j % 2, 0:256], hH[:, k, rows], hL[:, k, rows], wh[:, k, :], wl[:, k, :],
                              k == 0, k == KT - 1, tt == 0 and k == 0)
                m.then_inc(s_dv["v"], 1)
            pe.wait_ge(s_dr["roped"], 16)
            pe.wait_ge(s_dv["copied"], 16)

            def diff_rest(u):
                h, qt = u // TT, u % TT
                pe.wait_ge(s_da["probs"], u + 1)
                if u >= 2:
                    pe.wait_ge(s_da["at"], u - 1)
                for k in range(TT):
                    m = pe.transpose(ps[:, 4 + u % 2, k * P:(k + 1) * P], scr[:, 4, k * P:(k + 1) * P],
                                     tab[:, IDENT, :])
                m.then_inc(s_da["trans"], 1)
                if qt == TT - 1:
                    pe.wait_ge(s_da["at"], u + 1)
                    if h >= 2:
                        pe.wait_ge(s_da["ycopied"], h - 1)
                    for k in range(TT):
                        m = pe.matmul(ps[:, 6 + h % 2, :], dv[:, k, h * P:(h + 1) * P], scr[:, 5 + k, :],
                                      start=k == 0, stop=k == TT - 1)
                    m.then_inc(s_da["o"], 1)

            for u in range(DIFF_H * TT):
                h, qt = u // TT, u % TT
                for c in range(2):
                    if u >= 2:
                        pe.wait_ge(s_da["exp"], 2 * (u - 2) + c + 1)
                    half = slice(c * HD, (c + 1) * HD)
                    pe.matmul(ps[:, 2 * (u % 2) + c, :], dqk[half, h, qt * P:(qt + 1) * P], dqk[half, 8 + h, :],
                              start=True, stop=True).then_inc(s_da["scores"], 1)
                if u >= 1:
                    diff_rest(u - 1)
            diff_rest(DIFF_H * TT - 1)
            for h in range(DIFF_H):
                pe.wait_ge(s_dn["sq"], h + 1)
                pe.matmul(ps[:, h % 2, :], tab[:, ONES, :], scr[:, 0, :], start=True,
                          stop=True).then_inc(s_dn["sum"], 1)
            pe.wait_ge(s_dn["lo"], DIFF_H)
            for t in range(KT):
                if t % 2 == 0:
                    chunk(C_WO + t // 2)
                if t >= 4:
                    pe.wait_ge(s_wo2["added"], t - 3)
                tile(C_WO + t // 2, t % 2, ps[:, t % 4, :], s_wo2["proj"])
            norm("ffn1", KT)
            pe.wait_ge(s_norm["lo"], n_at("ffn1", "lo") + KT)
            ffn_tensor(1, C_FFN2)
            norm("final2", KT)


def constants():
    inv64 = np.float32(ROPE_THETA) ** (-np.arange(0, 64, 2, dtype=np.float32) / np.float32(64))
    inv32 = np.float32(ROPE_THETA) ** (-np.arange(0, 32, 2, dtype=np.float32) / np.float32(32))
    p = np.arange(P)
    f64 = inv64[p % 32].astype(np.float32)
    f96 = np.where((p >= NOPE) & (p < MLA_QK), inv32[(p - NOPE) % 16], 0).astype(np.float32)
    sign64 = np.where(p % 64 < 32, -1, 1).astype(np.float32)
    sign96 = np.where((p - NOPE) % 32 < 16, -1, 1).astype(np.float32)
    tables = np.zeros((P, NTAB, P), np.float32)
    tables[:, ONES] = 1
    tables[:, IDENT] = np.eye(P)
    for a in p:
        tables[a, SWAP64, a ^ 32] = 1
        if NOPE <= a < MLA_QK:
            tables[a, SWAP96, NOPE + ((a - NOPE) ^ 16)] = 1
    tables[:, BLOCKMEAN] = (p[:, None] // RET_D == p[None, :] // RET_D) / RET_D
    tables[:, CAUSAL] = np.where(p[None, :] <= p[:, None], 0, NEG)
    tables[:, IOTA] = p[None, :]
    gamma = 1.0 - 2.0 ** (-5.0 - np.arange(RET_H, dtype=np.float64))
    diff = np.arange(T)[None, :] - p[:, None]
    decays = np.where(diff >= 0, gamma[:, None, None] ** np.maximum(diff, 0), 0) * RET_D ** -0.5
    t = np.arange(T)
    recips = np.stack([1.0 / (np.clip(t + w - w // 2, 0, T) - np.clip(t - w // 2, 0, T)) for w in WINDOWS])
    return {
        "freq": [("inv64", f64), ("inv96", f96), ("sign64", sign64), ("sign96", sign96)],
        "tables": tables,
        "decays": decays.astype(np.float32),
        "recips": np.broadcast_to(recips[None].astype(np.float32), (P, len(WINDOWS), T)),
    }


def layout(inputs):
    g = {k: np.asarray(v) for k, v in inputs.items()}

    def cols(v):
        return v.reshape(-1, P).T

    def chunks(w, n=256):
        k, m = w.shape
        return w.reshape(k // P, P, m // n, n).transpose(2, 1, 0, 3).reshape(m // n, P, (k // P) * n)

    con = constants()
    vec = np.zeros((P, NVEC), np.float32)

    def put(name, v):
        o, n = VEC[name]
        vec[:, o:o + n] = v.reshape(P, n)

    for name, v in (("c", g["c"][0]), ("b_ada", g["b_ada"][0]), ("g_norm1", g["g_norm1"][0]), ("g_q", g["g_q_norm"][0]),
                    ("g_kv", g["g_kv_norm"][0]), ("g_ret", g["g_ret_norm"][0]), ("g_norm2", g["g_norm2"][0]),
                    ("g_final", g["g_final"]), ("mix0", g["mix_norm_2"][0]), ("mix1", g["mix_norm_2"][1]),
                    ("pool_scale", g["pool_scale_2"][0]), ("subln", g["diff_subln_2"][0]),
                    ("ffn0", g["ffn_norm_2"][0]), ("ffn1", g["ffn_norm_2"][1]), ("final", g["final_norm_2"])):
        put(name, cols(v))
    for l in range(2):
        cv = np.concatenate([g["ffn_conv_w_2"][l], g["ffn_conv_b_2"][l][None]])
        put(f"conv{l}", cv.reshape(4, FT, P).transpose(2, 1, 0))
    for name, v in con["freq"]:
        put(name, v)
    w_in = g["w_in"][0]
    o = Q_RANK + P + ROPE
    w_kv = np.concatenate([w_in[:, Q_RANK:Q_RANK + P], w_in[:, Q_RANK:Q_RANK + NOPE], w_in[:, Q_RANK + P:o]], 1)
    rw = RET_H * RET_D
    ret = np.concatenate([w_in[:, o:o + 2 * rw], w_in[:, o + 3 * rw:], w_in[:, o + 2 * rw:o + 3 * rw]], 1)
    up = g["ffn_w_up_2"].reshape(2, KT, P, 2, FT, P).transpose(0, 4, 2, 1, 3, 5).reshape(2, FT, P, CHUNK)
    a = {
        "vectors": vec,
        "tables": con["tables"],
        "decays": con["decays"],
        "recips": con["recips"],
        "positions_l": np.concatenate([g["positions"].reshape(1, T), g["positions_2"].reshape(1, T)], 1),
        "lams": np.concatenate([g[f"diff_lam_{n}_2"].reshape(1, HD) for n in ("q1", "k1", "q2", "k2")], 1),
        "x_l": g["x"][0].T.reshape(KT, P, T).transpose(1, 0, 2),
        "w_ada_l": chunks(g["w_ada"][0]),
        "w_lat0": chunks(w_in[:, 0:Q_RANK])[0],
        "w_lat1": chunks(w_kv, 224)[0],
        "w_ret_l": chunks(ret),
        "w_uq_l": chunks(g["w_uq"][0], MLA_H * MLA_QK)[0],
        "w_ukv_l": g["w_ukv"][0],
        "w_out_l": chunks(g["w_out"][0]),
        "w_query_l": chunks(g["w_query"][0]),
        "keys_l": g["sub_keys"][0].transpose(2, 0, 1),
        "u_l": chunks(g["expert_u"][0].T),
        "v_l": g["expert_v"][0].reshape(PEER_STEPS, 2, P, D).transpose(0, 2, 1, 3).reshape(PEER_STEPS, P, CHUNK),
        "pool_l": g["pool_w_2"][0].reshape(4, 2, P, 256).transpose(2, 0, 1, 3).reshape(P, CHUNK),
        "up_l": up,
        "down_l": g["ffn_w_down_2"].reshape(2, FT, P, D),
        "w_qkv_l": chunks(g["diff_w_qkv_2"][0]),
        "w_o_l": chunks(g["diff_w_o_2"][0]),
    }
    return {k: np.ascontiguousarray(v) for k, v in a.items()}


def kernel(**inputs):
    import concourse.bacc as bacc
    from concourse.bass_utils import run_bass_kernel_spmd

    arrays = layout(inputs)
    nc = bacc.Bacc("TRN2", target_bir_lowering=False, num_devices=1)
    args = {n: nc.dram_tensor(n, a.shape, mybir.dt.from_np(a.dtype), kind="ExternalInput").ap()
            for n, a in arrays.items()}
    args["w_scratch"] = nc.dram_tensor("w_scratch", (NTB, P, P, TB), F32).ap()
    outs = {"out": nc.dram_tensor("out", (P, KT, T), F32, kind="ExternalOutput").ap()}
    build(nc, args, outs)
    r = run_bass_kernel_spmd(nc, [arrays], core_ids=[0])
    y = r.results[0]["out"]
    return np.ascontiguousarray(y.transpose(2, 1, 0).reshape(1, T, D))
```

```python
from contextlib import ExitStack

import numpy as np

import concourse.bass as bass
from concourse import mybir

F32 = mybir.dt.float32
F32R = mybir.dt.float32r
I32 = mybir.dt.int32
U32 = mybir.dt.uint32
ACT = mybir.ActivationFunctionType
ALU = mybir.AluOpType
AX = mybir.AxisListType.X

P = 128
D, T = 1024, 512
KT, TT = D // P, T // P
EPS = 1e-6
ROPE_THETA = 10000.0
MLA_H, NOPE, ROPE, MLA_V, Q_RANK = 8, 64, 32, 64, 256
MLA_QK = NOPE + ROPE
RET_H, RET_D = 8, 64
PEER_H, PEER_KEYS, TOPK = 8, 128, 16
N_EXP = PEER_KEYS * PEER_KEYS
DIFF_H, HD = 8, 64
SUBLN_EPS = 1e-5
LAM_INIT = float(0.8 - 0.6 * np.exp(-0.3))
D_FF = 2816
FT = D_FF // P
WINDOWS = (2, 4, 8, 16)
NEG = -1e30
FAR_BELOW = -3.0e38

CHUNK, STAGES, SLOTS = 2048, 2, 4

C_LAT, C_KV, C_RQK, C_RG, C_RV = 0, 1, 2, 6, 8
C_UQ, C_UKV, C_OUT, C_QUERY, C_PEER = 10, 11, 12, 16, 24
PEER_STEPS = N_EXP // 256
C_POOL = C_PEER + 2 * PEER_STEPS
C_FFN1 = C_POOL + 1
C_QKV = C_FFN1 + 2 * FT
C_WO = C_QKV + 12
C_FFN2 = C_WO + 4
C_END = C_FFN2 + 2 * FT

VEC = {}
for _name, _n in (("c", 8), ("b_ada", 48), ("g_norm1", 8), ("g_q", 2), ("g_kv", 1), ("g_ret", 4), ("g_norm2", 8),
                  ("g_final", 8), ("mix0", 8), ("mix1", 8), ("pool_scale", 8), ("subln", 1), ("ffn0", 8),
                  ("ffn1", 8), ("final", 8), ("conv0", 4 * FT), ("conv1", 4 * FT),
                  ("inv64", 1), ("inv96", 1), ("sign64", 1), ("sign96", 1)):
    VEC[_name] = (sum(n for _, n in VEC.values()), _n)
NVEC = sum(n for _, n in VEC.values())
ONES, IDENT, SWAP64, SWAP96, BLOCKMEAN, CAUSAL, IOTA = range(7)
NTAB = 7

TB = 32
NTB = T // TB


class Chain:

    def __init__(self, eng, sem):
        self.eng, self.sem, self.n = eng, sem, 0

    def __call__(self, ins):
        ins.then_inc(self.sem, 1)
        self.n = self.n + 1
        self.eng.wait_ge(self.sem, self.n)


def build(nc, A, O):
    out = O.get("out")
    with ExitStack() as ctx:
        def sb(name, shape, dt=F32, scope=ctx):
            return scope.enter_context(nc.sbuf_tensor("sb_" + name, shape, dt))

        def sem(name):
            return ctx.enter_context(nc.semaphore(name))

        def sems(stage, *names):
            return {n: sem(stage + "_" + n) for n in names}

        xT = sb("xT", [P, KT, T])
        hH = sb("hH", [P, KT, T], F32R)
        hL = sb("hL", [P, KT, T], F32R)
        stage = [sb(f"stage{i}", [P, CHUNK]) for i in range(STAGES)]
        wH = [sb(f"wH{i}", [P, CHUNK], F32R) for i in range(SLOTS)]
        wL = [sb(f"wL{i}", [P, CHUNK], F32R) for i in range(SLOTS)]
        vec = sb("vec", [P, NVEC])
        tab = sb("tab", [P, NTAB, P])
        mod = sb("mod", [P, 48])
        gain1 = sb("gain1", [P, KT])
        gain2 = sb("gain2", [P, KT])
        small = sb("small", [P, 16])
        scr = sb("scr", [P, 9, T])
        posi = sb("posi", [P, T], I32)
        lams = sb("lams", [P, 4, HD])
        sinkv = sb("sinkv", [P, HD])
        stats = sb("stats", [P, 8, 32])
        sc = small[:, 8:8 + KT]
        ps = ctx.enter_context(nc.psum_tensor("ps", [P, 8, T], F32))

        def col(name, i=0, n=1):
            o, m = VEC[name]
            assert i + n <= m
            return vec[:, o + i:o + i + n]

        with ExitStack() as s1:
            ada = [sb(f"ada{i}", [P, CHUNK], scope=s1) for i in range(4)]
            ada_sum1 = sb("ada_sum1", [P, CHUNK], scope=s1)
            sc1 = sb("sc1", [P, KT], scope=s1)
        lat_scope = ExitStack()
        lat = sb("lat", [P, 4, T], scope=lat_scope)
        with ExitStack() as s2:
            qk = sb("qk", [P, 8, T], scope=s2)
            rv = sb("rv", [P, TT, RET_H * RET_D], scope=s2)
            rg = sb("rg", [P, 4, T], scope=s2)
            rope_r = sb("rope_r", [P, 2, T], scope=s2)
            decay = [sb(f"decay{i}", [P, T], scope=s2) for i in range(2)]
            ada_sum = sb("ada_sum", [P, D], scope=s2)
        with ExitStack() as s3:
            qnH = sb("qnH", [P, 2, T], F32R, scope=s3)
            qnL = sb("qnL", [P, 2, T], F32R, scope=s3)
            kvH = sb("kvH", [P, 1, T], F32R, scope=s3)
            kvL = sb("kvL", [P, 1, T], F32R, scope=s3)
            qh = sb("qh", [P, MLA_H, T], scope=s3)
            kh = sb("kh", [P, MLA_H, T], scope=s3)
        lat_scope.close()
        with ExitStack() as s4:
            fromsel = sb("fromsel", [P, 3, T], scope=s4)
            with ExitStack() as s5:
                keysT = sb("keysT", [P, 2, P], scope=s5)
                qp = [sb(f"qp{i}", [P, T], scope=s5) for i in range(2)]
                sc_k = [sb(f"sc_k{i}", [P, TT, P], scope=s5) for i in range(2)]
                sc_m = sb("sc_m", [P, TT, P], scope=s5)
                topv = sb("topv", [P, TT, 16, TOPK], scope=s5)
                topi = sb("topi", [P, TT, 16, TOPK], U32, scope=s5)
                topf = sb("topf", [P, TT, 16, TOPK], scope=s5)
                cand = sb("cand", [P, PEER_H, TOPK * TOPK], scope=s5)
                cand2 = sb("cand2", [P, PEER_H, TOPK * TOPK], scope=s5)
                best = sb("best", [P, PEER_H, TOPK], scope=s5)
                pos = sb("pos", [P, PEER_H, TOPK], U32, scope=s5)
                posu = sb("posu", [P, 2, PEER_H, TOPK], U32, scope=s5)
                posf = sb("posf", [P, 2, PEER_H, TOPK], scope=s5)
                chosen = sb("chosen", [P, 3, PEER_H * TOPK], scope=s5)
                gsum = sb("gsum", [P, 2, PEER_H], scope=s5)
            with ExitStack() as s6:
                wst = [sb(f"wst{i}", [P, P, TB], scope=s6) for i in range(2)]
        oneJ, oneI = [[scr[:, 4 * q + i, :].rearrange("p (t n) -> p t n", t=4) for i in range(4)] for q in range(2)]
        with ExitStack() as s7:
            wg = [sb(f"wg{i}", [P, NTB, 4, TB], scope=s7) for i in range(2)]
            ga = [sb(f"ga{i}", [P, T], scope=s7) for i in range(2)]
            wa = [sb(f"wa{i}", [P, T], scope=s7) for i in range(2)]
            waH = [[sb(f"waH{i}{m}", [P, T], F32R, scope=s7) for m in range(2)] for i in range(2)]
            waL = [[sb(f"waL{i}{m}", [P, T], F32R, scope=s7) for m in range(2)] for i in range(2)]
        PAD = 8
        with ExitStack() as s8:
            hp = sb("hp", [P, KT, T + 2 * PAD], scope=s8)
            wbuf = [sb(f"wbuf{i}", [P, 2, T + 2 * PAD], scope=s8) for i in range(2)]
            win = [sb(f"win{i}", [P, 2, T], scope=s8) for i in range(2)]
            recips = sb("recips", [P, len(WINDOWS), T], scope=s8)
        with ExitStack() as s9:
            dqk = sb("dqk", [P, 16, T], scope=s9)
            dv = sb("dv", [P, TT, D], scope=s9)
            rope_d = sb("rope_d", [P, 2, T], scope=s9)
        with ExitStack() as s10:
            gcv = [sb(f"gcv{i}", [P, T], scope=s10) for i in range(2)]
            gel = [sb(f"gel{i}", [P, T], scope=s10) for i in range(2)]
            fa = [sb(f"fa{i}", [P, T], scope=s10) for i in range(2)]
            faH = [sb(f"faH{i}", [P, T], F32R, scope=s10) for i in range(2)]
            faL = [sb(f"faL{i}", [P, T], F32R, scope=s10) for i in range(2)]

        wd = A["w_scratch"]

        ld_const = sem("ld_const")
        ld_x = sem("ld_x")
        ld_ada = [sem(f"ld_ada{i}") for i in range(4)]
        ld_stage = [sem(f"ld_stage{i}") for i in range(STAGES)]
        w_hi = sem("w_hi")
        w_split = sem("w_split")
        w_begun = sem("w_begun")
        s_ada = sems("ada", "silu", "exp", "summed", "cols", "mod", "ld0", "ld1")
        s_norm = sems("norm", "sq", "sum", "rec", "root", "xr", "t", "hi", "lo")
        NORMS = (("norm1", KT, 1), ("normq", 2, 1), ("normkv", 1, 1), ("norm2", KT, 1), ("final1", KT, 0),
                 ("mix0", KT, 0), ("ffn0", KT, 1), ("mix1", KT, 1), ("ffn1", KT, 1), ("final2", KT, 0))

        def norm_bank(name):
            return 0 if name in ("final1", "mix1", "final2") else 7

        def n_at(name, what):
            at = 0
            for n, tiles, split in NORMS:
                if n == name:
                    return at
                at += 1 if what in ("rec", "root") else tiles * split if what in ("hi", "lo") else tiles

        s_lat = sems("lat", "proj", "copied")
        s_tr = sems("tabr", "arg", "sin")
        s_tm = sems("tabm", "arg", "sin")
        s_td = sems("tabd", "arg", "sin")
        s_rr = sems("rrope", "proj", "copied", "perm", "roped")
        s_rp = sems("rproj", "proj", "gate", "value")
        s_rt = sems("ret", "scores", "decayed", "y", "ycopied", "ld0", "ld1")
        s_rn = sems("retn", "mean", "cent", "sq", "var", "rec", "root", "gexp", "yn", "hi", "lo")
        s_mr = sems("mrope", "proj", "copied", "perm", "roped", "kr")
        s_mk = sems("mkv", "k", "kcopied", "v", "vcopied")
        s_ma = sems("mla", "scores", "negmax", "exp", "probs", "trans", "pt", "o", "hi", "lo")
        s_wo1 = sems("wout", "proj", "added")
        s_q = sems("query", "keys", "proj", "copied", "scores", "scopied", "top", "sel", "negbest", "gexp", "chosen",
                   "trans", "tcopied", "hits", "spread")
        s_w = sems("wbuild", "hits", "ones", "prod", "copied", "st0", "st1")
        s_e = sems("peer", "ld0", "ld1", "a", "gelu", "wa", "hi", "lo", "o", "added")
        s_p = sems("pool", "ld", "filled", "pooled", "hi", "lo", "proj", "added")
        s_f = [sems(f"ffn{i}_l", "proj", "conv", "gelu", "act", "hi", "lo", "o", "added") for i in range(2)]
        s_dr = sems("drope", "proj", "copied", "perm", "roped")
        s_dv = sems("dvals", "v", "copied")
        s_da = sems("diff", "lam", "scores", "negmax", "exp", "probs", "trans", "at", "o", "ycopied")
        s_dn = sems("subln", "sq", "sum", "rec", "root", "yn", "hi", "lo")
        s_wo2 = sems("wo", "proj", "added")
        v_chain = sem("v_chain")
        a_chain = sem("a_chain")
        stored = sem("stored")

        def load(sp, c, src, c0=None):
            k = c if c0 is None else c0
            n = src.shape[-1]
            if k >= STAGES:
                sp.wait_ge(w_split, c - (STAGES - 1))
            sp.dma_start(stage[k % STAGES][:, 0:n], src).then_inc(ld_stage[k % STAGES], 16)

        def landed(k, i=0, per=0):
            return 16 * (k // STAGES + 1) + i * (16 * per // STAGES)

        def split_hi(act, k, n=CHUNK, i=0, per=0):
            act.wait_ge(ld_stage[k % STAGES], landed(k, i, per))
            if k >= SLOTS:
                act.wait_ge(w_begun, k - SLOTS + 2 + i * per)
            act.activation(wH[k % SLOTS][:, 0:n], stage[k % STAGES][:, 0:n], ACT.Copy).then_inc(w_hi, 1)

        def split_lo(dve, k, n=CHUNK, i=0, per=0):
            dve.wait_ge(w_hi, k + 1 + i * per)
            dve.tensor_tensor(wL[k % SLOTS][:, 0:n], stage[k % STAGES][:, 0:n], wH[k % SLOTS][:, 0:n],
                              ALU.subtract).then_inc(w_split, 1)

        def chunk_len(k):
            if k == C_KV:
                return KT * 224
            if k == C_UQ:
                return 2 * MLA_H * MLA_QK
            if k == C_UKV:
                return MLA_H * (NOPE + MLA_V)
            if k > C_FFN1 and k < C_QKV:
                return CHUNK if is_up(k - C_FFN1) else D
            if k > C_FFN2 and k < C_END:
                return CHUNK if is_up(k - C_FFN2) else D
            return CHUNK

        def is_up(r):
            return r == 0 or (r % 2 == 1 and r != 2 * FT - 1)

        def split_hi_at(act, k):
            if k < C_END:
                split_hi(act, k, chunk_len(k))

        def split_lo_at(dve, k):
            if k < C_END:
                split_lo(dve, k, chunk_len(k))

        def three(pe, dst, lh, ll, rh, rl, first, last, begins=False):
            m = pe.matmul(dst, lh, rl, start=first, stop=False)
            if begins:
                m.then_inc(w_begun, 1)
            pe.matmul(dst, ll, rh, start=False, stop=False)
            return pe.matmul(dst, lh, rh, start=False, stop=last)

        def product(pe, k, dst, cols, nkt, width, rH, rL, done, begins):
            wh = wH[k % SLOTS][:, 0:nkt * width].rearrange("p (k n) -> p k n", k=nkt)
            wl = wL[k % SLOTS][:, 0:nkt * width].rearrange("p (k n) -> p k n", k=nkt)
            for q in range(nkt):
                m = three(pe, dst, wh[:, q, cols], wl[:, q, cols], rH[:, q, :], rL[:, q, :], q == 0, q == nkt - 1,
                          begins and q == 0)
            m.then_inc(done, 1)

        def pick_buffers():
            return [scr[:, 4 * q:4 * q + 4, :].rearrange("p b (k a) -> p (b k) a", a=TOPK) for q in range(2)]

        block = ctx.enter_context(nc.Block())

        @block.sync
        def _(sp):
            sp.dma_start(vec[:, :], A["vectors"]).then_inc(ld_const, 16)
            sp.dma_start(posi[:, :], A["positions_l"][:, 0:T].broadcast_to([P, T])).then_inc(ld_const, 16)
            sp.dma_start(lams[:, :, :].rearrange("p a b -> p (a b)"),
                         A["lams"].broadcast_to([P, 4 * HD])).then_inc(ld_const, 16)
            sp.dma_start(tab[:, :, :], A["tables"]).then_inc(ld_const, 16)
            for k in range(KT):
                if k == 4:
                    sp.dma_start(xT[:, :, :], A["x_l"]).then_inc(ld_x, 16)
                if k >= 4:
                    sp.wait_ge(s_ada["summed"], k - 3)
                sp.dma_start(ada[k % 4][:, :], A["w_ada_l"][k]).then_inc(ld_ada[k % 4], 16)
            for k in range(2):
                load(sp, k, [A["w_lat0"], A["w_lat1"]][k])
            for k in range(8):
                load(sp, 2 + k, A["w_ret_l"][k])
            load(sp, C_UQ, A["w_uq_l"])
            load(sp, C_UKV, A["w_ukv_l"])
            for r in range(16):
                if r < 2:
                    sp.wait_ge(w_split, C_UQ + r + 1)
                else:
                    sp.wait_ge(s_ada["summed"], KT + 2 * (r - 1))
                sp.dma_start(stage[r % 2][:, :], A["w_ada_l"][KT + r]).then_inc(s_ada[f"ld{r % 2}"], 16)
            sp.wait_ge(s_ada["summed"], KT + 32)
            for k in range(4):
                load(sp, C_OUT + k, A["w_out_l"][k])
            sp.wait_ge(s_tm["arg"], 1)
            sp.dma_start(posi[:, :], A["positions_l"][:, T:2 * T].broadcast_to([P, T])).then_inc(ld_const, 16)
            load(sp, C_QUERY, A["w_query_l"][0])
            load(sp, C_QUERY + 1, A["w_query_l"][1])
            sp.wait_ge(s_wo1["added"], KT)
            sp.dma_start(keysT[:, :, :], A["keys_l"]).then_inc(s_q["keys"], 16)
            for k in range(2, 8):
                load(sp, C_QUERY + k, A["w_query_l"][k])
            load(sp, C_PEER, A["u_l"][0])
            with sp.Fori(0, NTB // 2) as b:
                for par in range(2):
                    sp.wait_ge(s_w["copied"], (TB // 4) * (2 * b + par + 1))
                    sp.dma_start(wd[2 * b + par], wst[par][:, :, :]).then_inc(s_w[f"st{par}"], 16)
            load(sp, C_PEER + 1, A["u_l"][1])
            for par in range(2):
                sp.wait_ge(s_w[f"st{par}"], 16 * (NTB // 2))
            wd_i = wd.rearrange("b j i t -> j b i t")
            for par in range(2):
                sp.dma_start(wg[par][:, :, :, :], wd_i[:, :, 4 * par:4 * par + 4, :]).then_inc(s_e[f"ld{par}"], 16)
            load(sp, C_PEER + 2, A["v_l"][0])
            with sp.Fori(0, PEER_STEPS // 4 - 1) as i:
                for q in range(4):
                    load(sp, C_PEER + 3 + 2 * q + 8 * i, A["u_l"][4 * i + q + 2], C_PEER + 3 + 2 * q)
                    load(sp, C_PEER + 4 + 2 * q + 8 * i, A["v_l"][4 * i + q + 1], C_PEER + 4 + 2 * q)
                    if q % 2 == 1:
                        par = q // 2
                        sp.wait_ge(s_e["wa"], 4 * (2 * i + par) + 4)
                        sp.dma_start(wg[par][:, :, :, :], wd_i[:, :, bass.ds((2 * i + par + 2) * 4, 4), :]
                                     ).then_inc(s_e[f"ld{par}"], 16)
            for s in range(PEER_STEPS - 4, PEER_STEPS + 1):
                c = C_PEER + 2 * s + 3
                if s + 2 < PEER_STEPS:
                    load(sp, c, A["u_l"][s + 2])
                    load(sp, c + 1, A["v_l"][s + 1])
                elif s + 1 < PEER_STEPS:
                    load(sp, c, A["v_l"][s + 1])
            sp.wait_ge(s_norm["t"], n_at("final1", "t") + KT)
            sp.dma_start(recips[:, :, :], A["recips"]).then_inc(s_p["ld"], 16)
            load(sp, C_POOL, A["pool_l"])

            def ffn_loads(l, c):
                load(sp, c, A["up_l"][l, 0])
                load(sp, c + 1, A["up_l"][l, 1])
                load(sp, c + 2, A["down_l"][l, 0])
                with sp.Fori(0, FT // 2 - 1) as i:
                    for q in range(2):
                        load(sp, c + 3 + 2 * q + 4 * i, A["up_l"][l, 2 * i + q + 2], c + 3 + 2 * q)
                        load(sp, c + 4 + 2 * q + 4 * i, A["down_l"][l, 2 * i + q + 1], c + 4 + 2 * q)
                load(sp, c + 2 * FT - 1, A["down_l"][l, FT - 1])

            ffn_loads(0, C_FFN1)
            for k in range(12):
                load(sp, C_QKV + k, A["w_qkv_l"][k])
            for k in range(4):
                load(sp, C_WO + k, A["w_o_l"][k])
            ffn_loads(1, C_FFN2)
            for k in range(KT):
                sp.wait_ge(s_norm["t"], n_at("final2", "t") + k + 1)
                sp.dma_start(out[:, k, :], xT[:, k, :]).then_inc(stored, 16)
            sp.wait_ge(stored, 16 * KT)

        @block.scalar
        def _(act):
            chain = Chain(act, a_chain)

            def norm(name, src, nkt, gains, shifts, dst=None, dstH=None, dstL=None, ready=None,
                     mod_at=None):
                s = s_norm
                for k in range(nkt):
                    if ready:
                        act.wait_ge(ready[0], ready[1] + k + 1)
                    if k >= 2:
                        act.wait_ge(s["sum"], n_at(name, "sum") + k - 1)
                    act.activation(scr[:, k % 2, :], src(k), ACT.Square).then_inc(s["sq"], 1)
                if mod_at:
                    act.wait_ge(s_ada["mod"], mod_at)
                act.wait_ge(s["rec"], n_at(name, "rec") + 1)
                act.activation(scr[:, 3, :], scr[:, 4, :], ACT.Sqrt).then_inc(s["root"], 1)
                for k in range(nkt):
                    act.wait_ge(s["xr"], n_at(name, "xr") + k + 1)
                    if dst is None and k >= 2:
                        act.wait_ge(s["lo"], n_at(name, "lo") + k - 1)
                    d = scr[:, 7 + k % 2, :] if dst is None else dst(k)
                    act.activation(d, scr[:, k % 2, :], ACT.Identity, scale=gains(k),
                                   bias=shifts(k) if shifts else 0.0).then_inc(s["t"], 1)
                    if dst is None:
                        act.wait_ge(s["t"], n_at(name, "t") + k + 1)
                        act.activation(dstH[:, k, :], d, ACT.Copy).then_inc(s["hi"], 1)

            def rope_tables(s, tabs):
                for q in range(2):
                    act.wait_ge(s["arg"], q + 1)
                    act.activation(tabs(q), tabs(q), ACT.Sin).then_inc(s["sin"], 1)

            act.wait_ge(ld_const, 64)
            act.activation(sc1[:, :], col("c", 0, 8), ACT.Exp, scale=-1.0).then_inc(s_ada["exp"], 1)
            act.wait_ge(ld_x, 16)
            norm("norm1", lambda k: xT[:, k, :], KT, lambda k: gain1[:, k:k + 1], lambda k: mod[:, k:k + 1],
                 dstH=hH, dstL=hL, mod_at=2)
            split_hi_at(act, 0)
            split_hi_at(act, 1)

            def load_decay(h):
                if h >= 2:
                    act.wait_ge(s_rt["decayed"], TT * (h - 1))
                act.dma_start(decay[h % 2][:, :], A["decays"][h]).then_inc(s_rt[f"ld{h % 2}"], 16)

            act.wait_ge(s_norm["lo"], n_at("norm1", "lo") + KT)
            load_decay(0)
            load_decay(1)
            rope_tables(s_tr, lambda q: rope_r[:, q, :])
            for t in range(4):
                if t % 2 == 0:
                    split_hi_at(act, C_LAT + t // 2 + 2)
                n = P if t < 3 else MLA_QK
                act.wait_ge(s_lat["proj"], t + 1)
                act.activation(lat[0:n, t, :], ps[0:n, t % 2, :], ACT.Copy).then_inc(s_lat["copied"], 1)
            for t in range(8):
                if t % 2 == 0:
                    split_hi_at(act, C_RQK + t // 2 + 2)
                act.wait_ge(s_rr["proj"], t + 1)
                act.activation(qk[:, t, :], ps[:, t % 2, :], ACT.Copy).then_inc(s_rr["copied"], 1)
            for t in range(4):
                if t % 2 == 0:
                    split_hi_at(act, C_RG + t // 2 + 2)
                act.wait_ge(s_rp["proj"], t + 1)
                act.activation(rg[:, t, :], ps[:, t % 2, :], ACT.Copy).then_inc(s_rp["gate"], 1)
            split_hi_at(act, C_RV + 2)
            split_hi_at(act, C_RV + 3)
            for m in range(4):
                if m < 3:
                    load_decay(2 * m + 2)
                    load_decay(2 * m + 3)
                act.wait_ge(s_rt["y"], 2 * TT * (m + 1))
                act.activation(qk[:, m, :], ps[:, 4 + m % 2, :], ACT.Copy).then_inc(s_rt["ycopied"], 1)
            for m in range(4):
                act.wait_ge(s_rn["cent"], m + 1)
                act.activation(scr[:, 1, :], qk[:, m, :], ACT.Square).then_inc(s_rn["sq"], 1)
                act.wait_ge(s_rn["rec"], m + 1)
                act.activation(scr[:, 3, :], scr[:, 4, :], ACT.Sqrt).then_inc(s_rn["root"], 1)
                act.activation(scr[:, 5, :], rg[:, m, :], ACT.Exp, scale=-1.0).then_inc(s_rn["gexp"], 1)
                act.wait_ge(s_rn["yn"], m + 1)
                act.activation(hH[:, 4 + m, :], qk[:, m, :], ACT.Copy).then_inc(s_rn["hi"], 1)
            act.wait_ge(s_rn["lo"], 4)
            norm("normq", lambda k: lat[:, k, :], 2, lambda k: col("g_q", k), None, dstH=qnH, dstL=qnL)
            act.wait_ge(s_norm["lo"], n_at("normq", "lo") + 2)
            norm("normkv", lambda k: lat[:, 2, :], 1, lambda k: col("g_kv"), None, dstH=kvH, dstL=kvL)
            rope_tables(s_tm, lambda q: scr[:, 7 + q, :])
            for h in range(MLA_H):
                act.wait_ge(s_mr["proj"], h + 1)
                act.activation(qh[0:MLA_QK, h, :], ps[0:MLA_QK, h % 2, :], ACT.Copy).then_inc(s_mr["copied"], 1)
            split_hi_at(act, C_OUT)
            for h in range(MLA_H):
                act.wait_ge(s_mk["k"], h + 1)
                act.activation(kh[0:NOPE, h, :], ps[0:NOPE, h % 2, :], ACT.Copy).then_inc(s_mk["kcopied"], 1)
            split_hi_at(act, C_OUT + 1)

            def mla_pt(u):
                h, qt = u // TT, u % TT
                act.wait_ge(s_ma["trans"], u + 1)
                if qt == 0 and h >= 1:
                    act.wait_ge(s_ma["o"], h)
                act.activation(scr[:, 2:2 + qt + 1, qt * P:(qt + 1) * P],
                               ps[:, 2 + u % 2, 0:(qt + 1) * P].rearrange("p (k n) -> p k n", n=P),
                               ACT.Copy).then_inc(s_ma["pt"], 1)
                if qt == TT - 1 and h % 2 == 1:
                    m = h // 2
                    act.wait_ge(s_ma["o"], h + 1)
                    act.activation(hH[:, m, :], ps[:, 4 + m % 2, :], ACT.Copy).then_inc(s_ma["hi"], 1)

            for u in range(MLA_H * TT):
                n = (u % TT + 1) * P
                act.wait_ge(s_ma["negmax"], u + 1)
                if u >= 2:
                    act.wait_ge(s_ma["trans"], u - 1)
                act.activation(scr[:, u % 2, 0:n], ps[:, u % 2, 0:n], ACT.Exp, bias=stats[:, 1, u:u + 1],
                               scale=MLA_QK ** -0.5, accum_out=stats[:, 2, u:u + 1]).then_inc(s_ma["exp"], 1)
                if u >= 2:
                    mla_pt(u - 2)
            mla_pt(MLA_H * TT - 2)
            mla_pt(MLA_H * TT - 1)
            for k in range(4):
                split_hi_at(act, C_OUT + k + 2)
            norm("norm2", lambda k: xT[:, k, :], KT, lambda k: gain2[:, k:k + 1], lambda k: mod[:, 24 + k:25 + k],
                 dstH=hH, dstL=hL,
                 ready=(s_wo1["added"], 0), mod_at=4)

            def keys_copy(t):
                act.wait_ge(s_q["scores"], t + 1)
                if t >= 2:
                    act.wait_ge(s_q["top"], t - 1)
                act.activation(sc_k[t % 2][:, :, :], ps[:, 2 + t % 2, :].rearrange("p (a n) -> p a n", n=P),
                               ACT.Copy).then_inc(s_q["scopied"], 1)

            for t in range(16):
                if t % 2 == 0 and t // 2 < 7:
                    split_hi_at(act, C_QUERY + t // 2 + 2)
                act.wait_ge(s_q["proj"], t + 1)
                if t >= 2:
                    act.wait_ge(s_q["scores"], t - 1)
                act.activation(qp[t % 2][:, :], ps[:, t % 2, :], ACT.Copy).then_inc(s_q["copied"], 1)
                if t >= 1:
                    keys_copy(t - 1)
            keys_copy(15)
            for tt in range(TT):
                act.wait_ge(s_q["negbest"], tt + 1)
                act.activation(best[:, :, :], best[:, :, :], ACT.Exp).then_inc(s_q["gexp"], 1)
                for n, r in enumerate((2, 0, 1)):
                    act.wait_ge(s_q["trans"], 3 * tt + n + 1)
                    act.activation(fromsel[:, r, tt * P:(tt + 1) * P], ps[:, 4 + r, 0:P],
                                   ACT.Copy).then_inc(s_q["tcopied"], 1)
            with act.Fori(0, NTB // 2) as b:
                for par in range(2):
                    for g in range(TB // 4):
                        if g == 0:
                            act.wait_ge(s_w[f"st{par}"], b * 16)
                        act.wait_ge(s_w["prod"], (2 * b + par) * (TB // 4) + g + 1)
                        act.activation(wst[par][:, :, 4 * g:4 * g + 4],
                                       ps[:, g % 4, :].rearrange("p (t i) -> p i t", t=4),
                                       ACT.Copy).then_inc(s_w["copied"], 1)
            def peer_act(s0, i=0, has_a=True, splits=2):
                for q in range(splits):
                    split_hi(act, C_PEER + 2 * s0 + 1 + q, CHUNK, i, 8)
                if not has_a:
                    return
                for m in range(2):
                    act.wait_ge(s_e["a"], 2 * s0 + m + 1 + 8 * i)
                    if s0 > 0:
                        act.wait_ge(s_e["wa"], 2 * s0 - 2 + m + 1 + 8 * i)
                    act.activation(ga[m][:, :], ps[:, 2 * (s0 % 2) + m, :], ACT.Gelu).then_inc(s_e["gelu"], 1)
                for m in range(2):
                    act.wait_ge(s_e["wa"], 2 * s0 + m + 1 + 8 * i)
                    if s0 >= 2:
                        act.wait_ge(s_e["o"], KT * (s0 - 1) + 8 * KT // 2 * i)
                    act.activation(waH[s0 % 2][m][:, :], wa[m][:, :], ACT.Copy).then_inc(s_e["hi"], 1)

            peer_act(0)
            peer_act(1)
            with act.Fori(0, PEER_STEPS // 4 - 1) as i:
                for q in range(4):
                    peer_act(2 + q, i)
            for s in range(PEER_STEPS - 2, PEER_STEPS):
                peer_act(s, splits=2 if s < PEER_STEPS - 1 else 1)
            norm("final1", lambda k: xT[:, k, :], KT, lambda k: col("g_final", k), None, dst=lambda k: xT[:, k, :],
                 ready=(s_e["added"], KT * (PEER_STEPS - 1)))
            act.wait_ge(s_norm["t"], n_at("final1", "t") + KT)
            act.wait_ge(s_p["filled"], 1)
            norm("mix0", lambda k: xT[:, k, :], KT, lambda k: col("mix0", k), None,
                 dst=lambda k: hp[:, k, PAD:PAD + T])
            split_hi_at(act, C_POOL)
            for g in range(len(WINDOWS)):
                act.wait_ge(s_p["pooled"], g + 1)
                act.activation(hH[:, 2 * g:2 * g + 2, :], win[g % 2][:, :, 0:T], ACT.Copy).then_inc(s_p["hi"], 1)
            split_hi_at(act, C_POOL + 1)
            split_hi_at(act, C_POOL + 2)

            def ffn_act(l, c, s0, i=0, has_a=True, splits=2):
                s = s_f[l]
                for q in range(splits):
                    k = c + 2 * s0 + 1 + q
                    split_hi(act, k, CHUNK if is_up(k - c) else D, i, 4)
                if not has_a:
                    return
                act.wait_ge(s["conv"], s0 + 1 + 2 * i)
                if s0 >= 1:
                    act.wait_ge(s["act"], s0 + 2 * i)
                act.activation(gel[s0 % 2][:, :], gcv[s0 % 2][:, :], ACT.Gelu).then_inc(s["gelu"], 1)
                act.wait_ge(s["act"], s0 + 1 + 2 * i)
                if s0 >= 2:
                    act.wait_ge(s["o"], KT * (s0 - 1) + 2 * KT * i)
                act.activation(faH[s0 % 2][:, :], fa[s0 % 2][:, :], ACT.Copy).then_inc(s["hi"], 1)

            def ffn_scalar(l, c):
                ffn_act(l, c, 0, splits=0)
                split_hi(act, c + 2, D)
                ffn_act(l, c, 1)
                with act.Fori(0, FT // 2 - 2) as i:
                    for q in range(2):
                        ffn_act(l, c, 2 + q, i)
                ffn_act(l, c, FT - 2)
                ffn_act(l, c, FT - 1, splits=1)

            norm("ffn0", lambda k: xT[:, k, :], KT, lambda k: col("ffn0", k), None, dstH=hH, dstL=hL,
                 ready=(s_p["added"], 0))
            ffn_scalar(0, C_FFN1)
            split_hi_at(act, C_QKV)
            split_hi_at(act, C_QKV + 1)
            norm("mix1", lambda k: xT[:, k, :], KT, lambda k: col("mix1", k), None, dstH=hH, dstL=hL,
                 ready=(s_f[0]["added"], KT * (FT - 1)))
            rope_tables(s_td, lambda q: rope_d[:, q, :])
            for t in range(16):
                if t % 2 == 0:
                    split_hi_at(act, C_QKV + t // 2 + 2)
                act.wait_ge(s_dr["proj"], t + 1)
                act.activation(dqk[:, t, :], ps[:, t % 2, :], ACT.Copy).then_inc(s_dr["copied"], 1)
            for k in range(4):
                split_hi_at(act, C_QKV + 8 + k + 2)
            act.wait_ge(s_da["lam"], 1)
            act.activation(small[:, 2:4], small[:, 0:2], ACT.Exp).then_inc(s_da["lam"], 1)

            def diff_at(u):
                h, qt = u // TT, u % TT
                act.wait_ge(s_da["trans"], u + 1)
                if qt == 0 and h >= 1:
                    act.wait_ge(s_da["o"], h)
                act.activation(scr[:, 5:9, qt * P:(qt + 1) * P],
                               ps[:, 4 + u % 2, :].rearrange("p (k n) -> p k n", n=P),
                               ACT.Copy).then_inc(s_da["at"], 1)
                if qt == TT - 1:
                    act.wait_ge(s_da["o"], h + 1)
                    act.activation(dqk[:, h, :], ps[:, 6 + h % 2, :], ACT.Copy).then_inc(s_da["ycopied"], 1)

            for u in range(DIFF_H * TT):
                for c in range(2):
                    act.wait_ge(s_da["negmax"], 2 * u + c + 1)
                    if u >= 2:
                        act.wait_ge(s_da["trans"], u - 1)
                    act.activation(scr[:, 2 * (u % 2) + c, :], ps[:, 2 * (u % 2) + c, :], ACT.Exp,
                                   bias=stats[:, 4 * c + 1, u:u + 1], scale=HD ** -0.5,
                                   accum_out=stats[:, 4 * c + 2, u:u + 1]).then_inc(s_da["exp"], 1)
                if u >= 2:
                    diff_at(u - 2)
            diff_at(DIFF_H * TT - 2)
            diff_at(DIFF_H * TT - 1)
            for h in range(DIFF_H):
                if h >= 1:
                    act.wait_ge(s_dn["sum"], h)
                act.activation(scr[:, 0, :], dqk[:, h, :], ACT.Square).then_inc(s_dn["sq"], 1)
                act.wait_ge(s_dn["rec"], h + 1)
                act.activation(scr[:, 3, :], scr[:, 4, :], ACT.Sqrt).then_inc(s_dn["root"], 1)
                act.wait_ge(s_dn["yn"], h + 1)
                act.activation(hH[:, h, :], dqk[:, h, :], ACT.Copy).then_inc(s_dn["hi"], 1)
            for k in range(4):
                split_hi_at(act, C_WO + k + 2)
            norm("ffn1", lambda k: xT[:, k, :], KT, lambda k: col("ffn1", k), None, dstH=hH, dstL=hL,
                 ready=(s_wo2["added"], 0))
            ffn_scalar(1, C_FFN2)
            norm("final2", lambda k: xT[:, k, :], KT, lambda k: col("final", k), None, dst=lambda k: xT[:, k, :],
                 ready=(s_f[1]["added"], KT * (FT - 1)))

        @block.vector
        def _(dve):
            chain = Chain(dve, v_chain)

            def rsqrt(var, root, rec_done, root_done, n):
                dve.reciprocal(scr[:, 4, :], var).then_inc(rec_done, 1)
                dve.wait_ge(root_done, n)
                chain(dve.tensor_tensor(scr[:, 5, :], var, scr[:, 3, :], ALU.mult))
                chain(dve.tensor_tensor(scr[:, 5, :], scr[:, 5, :], scr[:, 3, :], ALU.mult))
                chain(dve.tensor_scalar(scr[:, 5, :], scr[:, 5, :], -0.5, 1.5, ALU.mult, ALU.add))
                chain(dve.tensor_tensor(root, scr[:, 5, :], scr[:, 3, :], ALU.mult))

            def norm(name, src, nkt, dst=None, dstL=None, dstH=None):
                s = s_norm
                dve.wait_ge(s["sum"], n_at(name, "sum") + nkt)
                chain(dve.tensor_scalar(scr[:, 2, :], ps[:, norm_bank(name), :], 1.0 / (nkt * P), EPS, ALU.mult, ALU.add))
                rsqrt(scr[:, 2, :], scr[:, 6, :], s["rec"], s["root"], n_at(name, "root") + 1)

                def low(k):
                    dve.wait_ge(s["hi"], n_at(name, "hi") + k + 1)
                    dve.tensor_tensor(dstL[:, k, :], scr[:, 7 + k % 2, :], dstH[:, k, :],
                                      ALU.subtract).then_inc(s["lo"], 1)

                for k in range(nkt):
                    if k >= 2:
                        dve.wait_ge(s["t"], n_at(name, "t") + k - 1)
                    dve.tensor_tensor(scr[:, k % 2, :], src(k), scr[:, 6, :], ALU.mult).then_inc(s["xr"], 1)
                    if dst is None and k >= 1:
                        low(k - 1)
                if dst is None:
                    low(nkt - 1)

            def rope_tables(s, tabs, positions, inv, sign):
                two_pi = 2.0 * np.pi
                hi = float(np.float32(6.28125))
                mid = float(np.float32(two_pi - hi))
                mid = float((np.float32(mid).view(np.uint32) & np.uint32(0xFFFFF000)).view(np.float32))
                lo = float(np.float32(two_pi - hi - mid))
                ang, turn = scr[:, 5, :], scr[:, 6, :]
                chain(dve.tensor_copy(ang, positions))
                chain(dve.tensor_scalar(ang, ang, inv, None, ALU.mult))
                for q in range(2):
                    chain(dve.tensor_scalar(turn, ang, 1.0 / two_pi, 0.25 if q == 0 else 0.0, ALU.mult, ALU.add))
                    chain(dve.tensor_scalar(turn, turn, 12582912.0, None, ALU.add))
                    chain(dve.tensor_scalar(turn, turn, -12582912.0, None, ALU.add))
                    chain(dve.scalar_tensor_tensor(tabs(q), turn, -hi, ang, ALU.mult, ALU.add))
                    chain(dve.scalar_tensor_tensor(tabs(q), turn, -mid, tabs(q), ALU.mult, ALU.add))
                    chain(dve.scalar_tensor_tensor(tabs(q), turn, -lo, tabs(q), ALU.mult, ALU.add))
                    if q == 0:
                        chain(dve.tensor_scalar(tabs(q), tabs(q), float(np.pi / 2), None, ALU.add))
                    dve.tensor_scalar(tabs(q), tabs(q), 3.1415925, -3.1415925, ALU.min, ALU.max).then_inc(s["arg"], 1)
                dve.wait_ge(s["sin"], 2)
                chain(dve.tensor_scalar(tabs(1), tabs(1), sign, None, ALU.mult))

            def rope(x, swapped, tabs, n, done):
                tmp = scr[0:n, 0, :]
                chain(dve.tensor_tensor(tmp, swapped, tabs(1)[0:n], ALU.mult))
                chain(dve.tensor_tensor(x, x, tabs(0)[0:n], ALU.mult))
                dve.tensor_tensor(x, x, tmp, ALU.add).then_inc(done, 1)

            dve.wait_ge(ld_const, 64)
            dve.wait_ge(s_ada["exp"], 1)
            chain(dve.tensor_scalar(sc1[:, :], sc1[:, :], 1.0, None, ALU.add))
            chain(dve.reciprocal(sc1[:, :], sc1[:, :]))
            dve.tensor_tensor(sc[:, :], sc1[:, :], col("c", 0, 8), ALU.mult).then_inc(s_ada["silu"], 1)
            dve.wait_ge(s_ada["silu"], 1)
            for k in range(KT):
                dve.wait_ge(ld_ada[k % 4], 16 * (k // 4 + 1))
                if k == 0:
                    op = dve.tensor_scalar(ada_sum1[:, :], ada[0][:, :], sc[:, 0:1], None, ALU.mult)
                else:
                    op = dve.scalar_tensor_tensor(ada_sum1[:, :], ada[k % 4][:, :], sc[:, k:k + 1], ada_sum1[:, :],
                                                  ALU.mult, ALU.add)
                op.then_inc(s_ada["summed"], 1)
                dve.wait_ge(s_ada["summed"], k + 1)
            dve.wait_ge(s_ada["cols"], 1)
            dve.tensor_tensor(mod[:, 0:16], ps[:, 0, 0:16], col("b_ada", 0, 16), ALU.add).then_inc(s_ada["mod"], 1)
            dve.wait_ge(s_ada["mod"], 1)

            def gain(g, scale, name):
                chain(dve.tensor_scalar(g[:, :], scale, 1.0, None, ALU.add))
                dve.tensor_tensor(g[:, :], g[:, :], col(name, 0, 8), ALU.mult).then_inc(s_ada["mod"], 1)

            gain(gain1, mod[:, 8:16], "g_norm1")
            norm("norm1", lambda k: xT[:, k, :], KT, dstL=hL, dstH=hH)
            split_lo_at(dve, 0)
            split_lo_at(dve, 1)
            dve.wait_ge(s_norm["lo"], n_at("norm1", "lo") + KT)
            rope_tables(s_tr, lambda q: rope_r[:, q, :], posi[:, :], col("inv64"), col("sign64"))
            split_lo_at(dve, 2)
            split_lo_at(dve, 3)
            for t in range(8):
                if t % 2 == 0:
                    split_lo_at(dve, C_RQK + t // 2 + 2)
                dve.wait_ge(s_rr["perm"], t + 1)
                rope(qk[:, t, :], ps[:, 2 + t % 2, :], lambda q: rope_r[:, q, :], P, s_rr["roped"])
                dve.wait_ge(s_rr["roped"], t + 1)
            split_lo_at(dve, C_RG + 2)
            split_lo_at(dve, C_RG + 3)
            for j in range(8):
                c, tt = j // TT, j % TT
                dve.wait_ge(s_rp["proj"], 4 + j + 1)
                dve.tensor_copy(rv[:, tt, c * 256:(c + 1) * 256], ps[:, 4 + j % 2, 0:256]).then_inc(s_rp["value"], 1)
            split_lo_at(dve, C_RV + 2)
            split_lo_at(dve, C_RV + 3)
            def ada_chunk(r):
                dve.wait_ge(s_ada[f"ld{r % 2}"], 16 * (r // 2 + 1))
                if r % 4 == 0 and r:
                    dve.wait_ge(s_ada["cols"], 1 + r // 4)
                for j in range(2):
                    k = 2 * (r % 4) + j
                    w = stage[r % 2][:, j * D:(j + 1) * D]
                    if k == 0:
                        op = dve.tensor_scalar(ada_sum[:, :], w, sc[:, 0:1], None, ALU.mult)
                    else:
                        op = dve.scalar_tensor_tensor(ada_sum[:, :], w, sc[:, k:k + 1], ada_sum[:, :], ALU.mult,
                                                      ALU.add)
                    op.then_inc(s_ada["summed"], 1)
                    dve.wait_ge(s_ada["summed"], KT + 2 * r + j + 1)

            for u in range(RET_H * TT):
                h, J = u // TT, u % TT
                n = T - P * J
                dve.wait_ge(s_rt["scores"], u + 1)
                dve.wait_ge(s_rt[f"ld{h % 2}"], 16 * (h // 2 + 1))
                if u >= 2:
                    dve.wait_ge(s_rt["y"], u - 1)
                dve.tensor_tensor(scr[:, 1 + u % 2, 0:n], ps[:, u % 2, 0:n], decay[h % 2][:, 0:n],
                                  ALU.mult).then_inc(s_rt["decayed"], 1)
                if u % 2 == 1:
                    ada_chunk(u // 2)
            dve.wait_ge(s_ada["cols"], 5)
            dve.tensor_tensor(mod[:, 16:48], ps[:, 3, 16:48], col("b_ada", 16, 32), ALU.add).then_inc(s_ada["mod"], 1)
            dve.wait_ge(s_ada["mod"], 3)
            gain(gain2, mod[:, 32:40], "g_norm2")
            for m in range(4):
                y = qk[:, m, :]
                dve.wait_ge(s_rn["mean"], m + 1)
                dve.tensor_tensor(y, y, ps[:, 6, :], ALU.subtract).then_inc(s_rn["cent"], 1)
                dve.wait_ge(s_rn["var"], m + 1)
                chain(dve.tensor_scalar(scr[:, 2, :], ps[:, 7, :], EPS, None, ALU.add))
                dve.reciprocal(scr[:, 4, :], scr[:, 2, :]).then_inc(s_rn["rec"], 1)
                dve.wait_ge(s_rn["gexp"], m + 1)
                chain(dve.tensor_scalar(scr[:, 7, :], scr[:, 5, :], 1.0, None, ALU.add))
                chain(dve.reciprocal(scr[:, 8, :], scr[:, 7, :]))
                chain(dve.tensor_tensor(scr[:, 8, :], scr[:, 8, :], rg[:, m, :], ALU.mult))
                chain(dve.tensor_tensor(scr[:, 5, :], scr[:, 2, :], scr[:, 3, :], ALU.mult))
                chain(dve.tensor_tensor(scr[:, 5, :], scr[:, 5, :], scr[:, 3, :], ALU.mult))
                chain(dve.tensor_scalar(scr[:, 5, :], scr[:, 5, :], -0.5, 1.5, ALU.mult, ALU.add))
                chain(dve.tensor_tensor(scr[:, 6, :], scr[:, 5, :], scr[:, 3, :], ALU.mult))
                chain(dve.tensor_tensor(y, y, scr[:, 6, :], ALU.mult))
                dve.scalar_tensor_tensor(y, y, col("g_ret", m), scr[:, 8, :], ALU.mult,
                                         ALU.mult).then_inc(s_rn["yn"], 1)
                dve.wait_ge(s_rn["hi"], m + 1)
                dve.tensor_tensor(hL[:, 4 + m, :], y, hH[:, 4 + m, :], ALU.subtract).then_inc(s_rn["lo"], 1)
            norm("normq", lambda k: lat[:, k, :], 2, dstL=qnL, dstH=qnH)
            norm("normkv", lambda k: lat[:, 2, :], 1, dstL=kvL, dstH=kvH)
            dve.wait_ge(s_norm["lo"], n_at("normkv", "lo") + 1)
            rope_tables(s_tm, lambda q: scr[:, 7 + q, :], posi[:, :], col("inv96"), col("sign96"))
            mla_tabs = lambda q: scr[:, 7 + q, :]
            dve.wait_ge(s_mr["perm"], 1)
            rope(lat[0:MLA_QK, 3, :], ps[0:MLA_QK, 2, :], mla_tabs, MLA_QK, s_mr["kr"])
            dve.wait_ge(s_mr["kr"], 1)
            for h in range(MLA_H):
                dve.tensor_copy(kh[NOPE:MLA_QK, h, :], lat[NOPE:MLA_QK, 3, :]).then_inc(s_mr["kr"], 1)
            for h in range(MLA_H):
                dve.wait_ge(s_mr["perm"], h + 2)
                rope(qh[0:MLA_QK, h, :], ps[0:MLA_QK, 2 + (h + 1) % 2, :], mla_tabs, MLA_QK, s_mr["roped"])
                dve.wait_ge(s_mr["roped"], h + 1)
            split_lo_at(dve, C_OUT)
            for tt in range(TT):
                dve.wait_ge(s_mk["v"], tt + 1)
                dve.wait_ge(s_mr["kr"], MLA_H + 1)
                dve.tensor_copy(lat[:, tt, :], ps[:, 4 + tt % 2, :]).then_inc(s_mk["vcopied"], 1)
            split_lo_at(dve, C_OUT + 1)

            def mla_probs(u):
                n = (u % TT + 1) * P
                dve.wait_ge(s_ma["exp"], u + 1)
                chain(dve.reciprocal(stats[:, 3, u:u + 1], stats[:, 2, u:u + 1]))
                dve.tensor_scalar(scr[:, u % 2, 0:n], scr[:, u % 2, 0:n], stats[:, 3, u:u + 1], None,
                                  ALU.mult).then_inc(s_ma["probs"], 1)
                if u % (2 * TT) == 2 * TT - 1 and u >= 2 * TT:
                    mla_low(u // (2 * TT) - 1)

            def mla_low(m):
                dve.wait_ge(s_ma["hi"], m + 1)
                dve.tensor_tensor(hL[:, m, :], ps[:, 4 + m % 2, :], hH[:, m, :], ALU.subtract).then_inc(s_ma["lo"], 1)

            for u in range(MLA_H * TT):
                qt = u % TT
                n = (qt + 1) * P
                dve.wait_ge(s_ma["scores"], u + 1)
                diag = ps[:, u % 2, qt * P:(qt + 1) * P]
                chain(dve.tensor_tensor(diag, diag, tab[:, CAUSAL, :], ALU.add))
                chain(dve.reduce_max(stats[:, 0, u:u + 1], ps[:, u % 2, 0:n], AX))
                dve.tensor_scalar(stats[:, 1, u:u + 1], stats[:, 0, u:u + 1], -(MLA_QK ** -0.5), None,
                                  ALU.mult).then_inc(s_ma["negmax"], 1)
                if u >= 1:
                    mla_probs(u - 1)
            mla_probs(MLA_H * TT - 1)
            mla_low(3)
            for k in range(4):
                split_lo_at(dve, C_OUT + k + 2)
                for j in range(2):
                    t = 2 * k + j
                    dve.wait_ge(s_wo1["proj"], t + 1)
                    dve.scalar_tensor_tensor(xT[:, t, :], ps[:, t % 4, :], mod[:, 16 + t:17 + t], xT[:, t, :],
                                             ALU.mult, ALU.add).then_inc(s_wo1["added"], 1)
            dve.wait_ge(s_wo1["added"], KT)
            norm("norm2", lambda k: xT[:, k, :], KT, dstL=hL, dstH=hH)

            def top16(rows):
                for q, step in enumerate((
                        lambda vals, masked, v, i: dve.max(v[:, 0:8], vals),
                        lambda vals, masked, v, i: dve.max_index(i[:, 0:8], v[:, 0:8], vals),
                        lambda vals, masked, v, i: dve.match_replace(masked, v[:, 0:8], vals, FAR_BELOW),
                        lambda vals, masked, v, i: dve.max(v[:, 8:16], masked),
                        lambda vals, masked, v, i: dve.max_index(i[:, 8:16], v[:, 8:16], masked))):
                    for row in rows:
                        op = step(*row)
                    if q != 1:
                        chain(op)

            for t in range(16):
                if t % 2 == 0 and t // 2 < 7:
                    split_lo_at(dve, C_QUERY + t // 2 + 2)
                dve.wait_ge(s_q["scopied"], t + 1)
                top16([(sc_k[t % 2][:, tt, :], sc_m[:, tt, :], topv[:, tt, t, :], topi[:, tt, t, :])
                       for tt in range(TT)])
                dve.tensor_copy(topf[:, :, t, :], topi[:, :, t, :]).then_inc(s_q["top"], 1)
            dve.wait_ge(s_q["top"], 16)
            picks = pick_buffers()

            def key_indices(tt):
                for half in range(2):
                    dve.wait_ge(s_q["spread"], 2 * tt + half + 1)
                    if half == 0 and tt >= 1:
                        dve.wait_ge(s_q["trans"], 3 * tt)
                    dve.tensor_reduce(chosen[:, half, :], picks[half], AX, ALU.add).then_inc(s_q["chosen"], 1)

            for tt in range(TT):
                v = topv[:, tt, :, :].rearrange("p (h two) a -> p h two a", two=2)
                c4 = cand[:, :, :].rearrange("p h (a b) -> p h a b", a=TOPK)
                chain(dve.tensor_tensor(c4, v[:, :, 0, :].unsqueeze(3).broadcast_to([P, PEER_H, TOPK, TOPK]),
                                        v[:, :, 1, :].unsqueeze(2).broadcast_to([P, PEER_H, TOPK, TOPK]), ALU.add))
                top16([(cand[:, h, :], cand2[:, h, :], best[:, h, :], pos[:, h, :]) for h in range(PEER_H)])
                chain(dve.tensor_copy(gsum[:, 0, :], best[:, :, 0]))
                dve.tensor_tensor(best[:, :, :], best[:, :, :], gsum[:, 0, :].unsqueeze(2).broadcast_to(
                    [P, PEER_H, TOPK]), ALU.subtract).then_inc(s_q["negbest"], 1)
                dve.tensor_scalar(posu[:, 0], pos[:, :, :], 4, None, ALU.logical_shift_right)
                chain(dve.tensor_scalar(posu[:, 1], pos[:, :, :], TOPK - 1, None, ALU.bitwise_and))
                chain(dve.tensor_copy(posf[:, :, :, :], posu[:, :, :, :]))
                if tt >= 1:
                    key_indices(tt - 1)
                    dve.wait_ge(s_q["chosen"], 3 * tt)
                iota = tab[:, IOTA, 0:TOPK].unsqueeze(1).broadcast_to([P, PEER_H * TOPK, TOPK])
                for half in range(2):
                    dve.tensor_tensor(picks[half], iota, posf[:, half].rearrange("p h k -> p (h k)").unsqueeze(2)
                                      .broadcast_to([P, PEER_H * TOPK, TOPK]), ALU.is_equal).then_inc(s_q["hits"], 1)
                dve.wait_ge(s_q["gexp"], tt + 1)
                chain(dve.tensor_reduce(gsum[:, 0, :], best[:, :, :], AX, ALU.add))
                chain(dve.reciprocal(gsum[:, 1, :], gsum[:, 0, :]))
                if tt >= 1:
                    dve.wait_ge(s_q["trans"], 3 * tt - 2)
                dve.tensor_tensor(chosen[:, 2, :].rearrange("p (h k) -> p h k", k=TOPK), best[:, :, :],
                                  gsum[:, 1, :].unsqueeze(2).broadcast_to([P, PEER_H, TOPK]),
                                  ALU.mult).then_inc(s_q["chosen"], 1)
                dve.wait_ge(s_q["chosen"], 3 * tt + 1)
            key_indices(TT - 1)
            dve.wait_ge(s_q["tcopied"], 3 * TT)

            iota4 = tab[:, IOTA, :].unsqueeze(1).broadcast_to([P, 4, P])

            def hits(par, tok):
                for half, ones in ((1, oneJ[par]), (0, oneI[par])):
                    ins = dve.tensor_tensor(ones[:, :, :], iota4, fromsel[:, half, bass.ds(tok, 4)].unsqueeze(2)
                                            .broadcast_to([P, 4, P]), ALU.is_equal)
                ins.then_inc(s_w["hits"], 1)

            for par in range(4):
                hits(par, 4 * par)
            with dve.Fori(1, T // 16) as i:
                for par in range(4):
                    dve.wait_ge(s_w["prod"], 4 * i + par - 3)
                    hits(par, i * 16 + 4 * par)

            def peer_dve(s0, i=0, has_a=True, splits=2, has_o=True):
                for q in range(splits):
                    split_lo(dve, C_PEER + 2 * s0 + 1 + q, CHUNK, i, 8)
                if has_a:
                    par = (s0 // 2) % 2
                    dve.wait_ge(s_e[f"ld{par}"], 16 * (s0 // 4 + 1) + 16 * i)
                    for m in range(2):
                        dve.wait_ge(s_e["gelu"], 2 * s0 + m + 1 + 8 * i)
                        if s0 >= 1:
                            dve.wait_ge(s_e["lo"], 2 * s0 + m - 1 + 8 * i)
                        dve.tensor_tensor(wa[m][:, :].rearrange("p (b t) -> p b t", b=NTB),
                                          ga[m][:, :].rearrange("p (b t) -> p b t", b=NTB),
                                          wg[par][:, :, 2 * (s0 % 2) + m, :], ALU.mult).then_inc(s_e["wa"], 1)
                    for m in range(2):
                        dve.wait_ge(s_e["hi"], 2 * s0 + m + 1 + 8 * i)
                        dve.tensor_tensor(waL[s0 % 2][m][:, :], wa[m][:, :], waH[s0 % 2][m][:, :],
                                          ALU.subtract).then_inc(s_e["lo"], 1)
                if has_o:
                    for d in range(KT):
                        dve.wait_ge(s_e["o"], KT * (s0 - 1) + d + 1 + 4 * KT * i)
                        if s0 >= 2:
                            dve.wait_ge(s_e["added"], KT * (s0 - 2) + d + 1 + 4 * KT * i)
                        dve.scalar_tensor_tensor(xT[:, d, :], ps[:, 4 + d % 4, :], mod[:, 40 + d:41 + d],
                                                 xT[:, d, :], ALU.mult, ALU.add).then_inc(s_e["added"], 1)

            peer_dve(0, has_o=False)
            peer_dve(1)
            with dve.Fori(0, PEER_STEPS // 4 - 1) as i:
                for q in range(4):
                    peer_dve(2 + q, i)
            for s in range(PEER_STEPS - 2, PEER_STEPS):
                peer_dve(s, splits=2 if s < PEER_STEPS - 1 else 1)
            peer_dve(PEER_STEPS, has_a=False, splits=0)
            norm("final1", lambda k: xT[:, k, :], KT, dst=True)
            dve.wait_ge(s_norm["t"], n_at("final1", "t") + KT)
            dve.memset(hp[:, :, :], 0.0).then_inc(s_p["filled"], 1)
            norm("mix0", lambda k: xT[:, k, :], KT, dst=True)
            split_lo_at(dve, C_POOL)
            dve.wait_ge(s_norm["t"], n_at("mix0", "t") + KT)
            dve.wait_ge(s_p["ld"], 16)
            W2 = T + 2 * PAD
            for g in range(len(WINDOWS)):
                if g >= 2:
                    dve.wait_ge(s_p["lo"], g - 1)
                h2 = hp[:, 2 * g:2 * g + 2, :]
                a = h2
                for r in range(g + 1):
                    e = 1 << r
                    l, rt = (1, 0) if r == 0 else (e // 2, e // 2)
                    chain(dve.tensor_tensor(wbuf[r % 2][:, :, e:W2 - e], a[:, :, e - l:W2 - e - l],
                                            a[:, :, e + rt:W2 - e + rt], ALU.add))
                    a = wbuf[r % 2]
                rec = recips[:, g, :].unsqueeze(1).broadcast_to([P, 2, T])
                mean = wbuf[(g + 1) % 2][:, :, 0:T]
                chain(dve.tensor_tensor(mean, a[:, :, PAD:PAD + T], rec, ALU.mult))
                dve.tensor_tensor(win[g % 2][:, :, 0:T], mean, h2[:, :, PAD:PAD + T],
                                  ALU.subtract).then_inc(s_p["pooled"], 1)
                dve.wait_ge(s_p["hi"], g + 1)
                dve.tensor_tensor(hL[:, 2 * g:2 * g + 2, :], win[g % 2][:, :, 0:T], hH[:, 2 * g:2 * g + 2, :],
                                  ALU.subtract).then_inc(s_p["lo"], 1)
            split_lo_at(dve, C_POOL + 1)
            split_lo_at(dve, C_POOL + 2)
            for t in range(KT):
                dve.wait_ge(s_p["proj"], t + 1)
                dve.scalar_tensor_tensor(xT[:, t, :], ps[:, t % 4, :], col("pool_scale", t), xT[:, t, :],
                                         ALU.mult, ALU.add).then_inc(s_p["added"], 1)
            dve.wait_ge(s_p["added"], KT)

            def ffn_dve(l, c, s0, i=0, has_a=True, splits=2, has_o=True):
                s = s_f[l]

                def add(d):
                    dve.wait_ge(s["o"], KT * (s0 - 1) + d + 1 + 2 * KT * i)
                    if s0 >= 2:
                        dve.wait_ge(s["added"], KT * (s0 - 2) + d + 1 + 2 * KT * i)
                    dve.tensor_tensor(xT[:, d, :], xT[:, d, :], ps[:, 4 + d % 4, :], ALU.add).then_inc(s["added"], 1)

                for q in range(2):
                    k = c + 2 * s0 + 1 + q
                    if q < splits:
                        split_lo(dve, k, CHUNK if is_up(k - c) else D, i, 4)
                    if has_o:
                        for d in range(4 * q, 4 * q + 4):
                            add(d)
                if has_a:
                    b0 = VEC[f"conv{l}"][0]

                    def cv(j):
                        if isinstance(i, int):
                            return vec[:, b0 + 4 * s0 + j:b0 + 4 * s0 + j + 1]
                        return vec[:, bass.ds(b0 + 4 * s0 + j + 8 * i, 1)]

                    g, u = ps[:, 2 * (s0 % 2), :], ps[:, 2 * (s0 % 2) + 1, :]
                    y = gcv[s0 % 2]
                    dve.wait_ge(s["proj"], 2 * s0 + 2 + 4 * i)
                    chain(dve.tensor_scalar(y[:, :], g, cv(1), cv(3), ALU.mult, ALU.add))
                    chain(dve.scalar_tensor_tensor(y[:, 1:T], g[:, 0:T - 1], cv(0), y[:, 1:T], ALU.mult, ALU.add))
                    dve.scalar_tensor_tensor(y[:, 0:T - 1], g[:, 1:T], cv(2), y[:, 0:T - 1], ALU.mult,
                                             ALU.add).then_inc(s["conv"], 1)
                    dve.wait_ge(s["gelu"], s0 + 1 + 2 * i)
                    if s0 >= 2:
                        dve.wait_ge(s["lo"], s0 - 1 + 2 * i)
                    dve.tensor_tensor(fa[s0 % 2][:, :], gel[s0 % 2][:, :], u, ALU.mult).then_inc(s["act"], 1)
                    dve.wait_ge(s["hi"], s0 + 1 + 2 * i)
                    dve.tensor_tensor(faL[s0 % 2][:, :], fa[s0 % 2][:, :], faH[s0 % 2][:, :],
                                      ALU.subtract).then_inc(s["lo"], 1)

            def ffn_vector(l, c):
                ffn_dve(l, c, 0, splits=0, has_o=False)
                split_lo(dve, c + 2, D)
                ffn_dve(l, c, 1)
                n0 = chain.n
                with dve.Fori(0, FT // 2 - 2) as i:
                    chain.n = n0 + 4 * i
                    for q in range(2):
                        ffn_dve(l, c, 2 + q, i)
                chain.n = n0 + 4 * (FT // 2 - 2)
                ffn_dve(l, c, FT - 2)
                ffn_dve(l, c, FT - 1, splits=1)
                ffn_dve(l, c, FT, has_a=False, splits=0)

            norm("ffn0", lambda k: xT[:, k, :], KT, dstL=hL, dstH=hH)
            ffn_vector(0, C_FFN1)
            split_lo_at(dve, C_QKV)
            split_lo_at(dve, C_QKV + 1)
            dve.wait_ge(s_f[0]["added"], KT * FT)
            norm("mix1", lambda k: xT[:, k, :], KT, dstL=hL, dstH=hH)
            dve.wait_ge(ld_const, 80)
            rope_tables(s_td, lambda q: rope_d[:, q, :], posi[:, :], col("inv64"), col("sign64"))
            for t in range(16):
                if t % 2 == 0:
                    split_lo_at(dve, C_QKV + t // 2 + 2)
                dve.wait_ge(s_dr["perm"], t + 1)
                rope(dqk[:, t, :], ps[:, 2 + t % 2, :], lambda q: rope_d[:, q, :], P, s_dr["roped"])
                dve.wait_ge(s_dr["roped"], t + 1)
            for j in range(16):
                c, tt = j // TT, j % TT
                if tt == 0:
                    split_lo_at(dve, C_QKV + 8 + c + 2)
                dve.wait_ge(s_dv["v"], j + 1)
                dve.tensor_copy(dv[:, tt, c * 256:(c + 1) * 256], ps[:, 4 + j % 2, 0:256]).then_inc(s_dv["copied"], 1)
            for q in range(2):
                op = dve.tensor_tensor_reduce(out=sinkv[:, 0:HD], in0=lams[:, 2 * q, :], in1=lams[:, 2 * q + 1, :],
                                              scale=1.0, scalar=0.0, op0=ALU.mult, op1=ALU.add,
                                              accum_out=small[:, q:q + 1])
                if q == 0:
                    chain(op)
                else:
                    op.then_inc(s_da["lam"], 1)
            dve.wait_ge(s_da["lam"], 2)
            chain(dve.tensor_tensor(small[:, 4:5], small[:, 3:4], small[:, 2:3], ALU.subtract))
            chain(dve.tensor_scalar(small[:, 5:6], small[:, 4:5], -LAM_INIT, None, ALU.add))

            def diff_probs(u):
                p0, p1 = scr[:, 2 * (u % 2), :], scr[:, 2 * (u % 2) + 1, :]
                dve.wait_ge(s_da["exp"], 2 * u + 2)
                for c in range(2):
                    chain(dve.reciprocal(stats[:, 4 * c + 3, u:u + 1], stats[:, 4 * c + 2, u:u + 1]))
                chain(dve.tensor_tensor(stats[:, 7, u:u + 1], stats[:, 7, u:u + 1], small[:, 5:6], ALU.mult))
                chain(dve.tensor_scalar(p1, p1, stats[:, 7, u:u + 1], None, ALU.mult))
                dve.scalar_tensor_tensor(p0, p0, stats[:, 3, u:u + 1], p1, ALU.mult,
                                         ALU.add).then_inc(s_da["probs"], 1)

            for u in range(DIFF_H * TT):
                for c in range(2):
                    dve.wait_ge(s_da["scores"], 2 * u + c + 1)
                    chain(dve.reduce_max(stats[:, 4 * c, u:u + 1], ps[:, 2 * (u % 2) + c, :], AX))
                    dve.tensor_scalar(stats[:, 4 * c + 1, u:u + 1], stats[:, 4 * c, u:u + 1], -(HD ** -0.5), None,
                                      ALU.mult).then_inc(s_da["negmax"], 1)
                if u >= 1:
                    diff_probs(u - 1)
            diff_probs(DIFF_H * TT - 1)
            for h in range(DIFF_H):
                dve.wait_ge(s_dn["sum"], h + 1)
                chain(dve.tensor_scalar(scr[:, 2, :], ps[:, h % 2, :], 1.0 / P, SUBLN_EPS, ALU.mult, ALU.add))
                rsqrt(scr[:, 2, :], scr[:, 1, :], s_dn["rec"], s_dn["root"], h + 1)
                chain(dve.tensor_tensor(dqk[:, h, :], dqk[:, h, :], scr[:, 1, :], ALU.mult))
                dve.tensor_scalar(dqk[:, h, :], dqk[:, h, :], col("subln"), 1.0 - LAM_INIT, ALU.mult,
                                  ALU.mult).then_inc(s_dn["yn"], 1)
                dve.wait_ge(s_dn["hi"], h + 1)
                dve.tensor_tensor(hL[:, h, :], dqk[:, h, :], hH[:, h, :], ALU.subtract).then_inc(s_dn["lo"], 1)
            for k in range(4):
                split_lo_at(dve, C_WO + k + 2)
                for j in range(2):
                    t = 2 * k + j
                    dve.wait_ge(s_wo2["proj"], t + 1)
                    dve.tensor_tensor(xT[:, t, :], xT[:, t, :], ps[:, t % 4, :], ALU.add).then_inc(s_wo2["added"], 1)
            dve.wait_ge(s_wo2["added"], KT)
            norm("ffn1", lambda k: xT[:, k, :], KT, dstL=hL, dstH=hH)
            ffn_vector(1, C_FFN2)
            dve.wait_ge(s_f[1]["added"], KT * FT)
            norm("final2", lambda k: xT[:, k, :], KT, dst=True)

        @block.gpsimd
        def _(pool):
            picks = pick_buffers()
            for tt in range(TT):
                f = topf[:, tt, :, :].rearrange("p (h two) a -> p h two a", two=2)
                for half in range(2):
                    pool.wait_ge(s_q["hits"], 2 * tt + half + 1)
                    e4 = picks[half].rearrange("p (h k) a -> p h k a", h=PEER_H)
                    pool.tensor_tensor(e4, e4, f[:, :, half, :].unsqueeze(2).broadcast_to([P, PEER_H, TOPK, TOPK]),
                                       ALU.mult).then_inc(s_q["spread"], 1)
            pool.wait_ge(s_q["tcopied"], 3 * TT)
            with pool.Fori(0, T // 16) as i:
                for par in range(4):
                    pool.wait_ge(s_w["hits"], 4 * i + par + 1)
                    pool.tensor_tensor(oneI[par][:, :, :], oneI[par][:, :, :],
                                       fromsel[:, 2, bass.ds(i * 16 + 4 * par, 4)].unsqueeze(2)
                                       .broadcast_to([P, 4, P]), ALU.mult).then_inc(s_w["ones"], 1)

        @block.tensor
        def _(pe):
            def norm(name, nkt):
                s = s_norm
                for k in range(nkt):
                    pe.wait_ge(s["sq"], n_at(name, "sq") + k + 1)
                    pe.matmul(ps[:, norm_bank(name), :], tab[:, ONES, :], scr[:, k % 2, :], start=k == 0,
                              stop=k == nkt - 1).then_inc(s["sum"], 1)

            def chunk(k, i=0, per=0):
                pe.wait_ge(w_split, k + 1 + i * per)

            def tile(k, j, dst, done):
                product(pe, k, dst, slice(j * P, (j + 1) * P), KT, 256, hH, hL, done, j == 0)

            def mod_cols(bank, first, weights, n):
                for f in range(n):
                    m = pe.matmul(ps[:, bank, first + f:first + f + 1], weights[:, f * P:(f + 1) * P],
                                  tab[:, ONES, 0:1], start=True, stop=True)
                m.then_inc(s_ada["cols"], 1)

            pe.wait_ge(ld_const, 64)
            norm("norm1", KT)
            pe.wait_ge(s_ada["summed"], KT)
            mod_cols(0, 0, ada_sum1, 16)
            pe.wait_ge(s_norm["lo"], n_at("norm1", "lo") + KT)
            pe.wait_ge(s_ada["mod"], 1)
            for t in range(4):
                if t % 2 == 0:
                    chunk(C_LAT + t // 2)
                if t >= 2:
                    pe.wait_ge(s_lat["copied"], t - 1)
                if t < 2:
                    tile(C_LAT, t, ps[:, t % 2, :], s_lat["proj"])
                else:
                    n = P if t == 2 else MLA_QK
                    product(pe, C_KV, ps[0:n, t % 2, :], slice((t - 2) * P, (t - 2) * P + n), KT, 224, hH, hL,
                            s_lat["proj"], t == 2)
            for t in range(9):
                if t < 8:
                    if t % 2 == 0:
                        chunk(C_RQK + t // 2)
                    if t >= 2:
                        pe.wait_ge(s_rr["copied"], t - 1)
                    else:
                        pe.wait_ge(s_lat["copied"], t + 3)
                    tile(C_RQK + t // 2, t % 2, ps[:, t % 2, :], s_rr["proj"])
                if t >= 1:
                    pe.wait_ge(s_rr["copied"], t)
                    if t >= 3:
                        pe.wait_ge(s_rr["roped"], t - 2)
                    pe.matmul(ps[:, 2 + (t - 1) % 2, :], tab[:, SWAP64, :], qk[:, t - 1, :], start=True,
                              stop=True).then_inc(s_rr["perm"], 1)
            for t in range(4):
                if t % 2 == 0:
                    chunk(C_RG + t // 2)
                if t >= 2:
                    pe.wait_ge(s_rp["gate"], t - 1)
                tile(C_RG + t // 2, t % 2, ps[:, t % 2, :], s_rp["proj"])
            for j in range(8):
                c, tt = C_RV + j // TT, j % TT
                if tt == 0:
                    chunk(c)
                if j >= 2:
                    pe.wait_ge(s_rp["value"], j - 1)
                wh = wH[c % SLOTS][:, :].rearrange("p (k n) -> p k n", k=KT)
                wl = wL[c % SLOTS][:, :].rearrange("p (k n) -> p k n", k=KT)
                rows = slice(tt * P, (tt + 1) * P)
                for k in range(KT):
                    m = three(pe, ps[:, 4 + j % 2, 0:256], hH[:, k, rows], hL[:, k, rows], wh[:, k, :], wl[:, k, :],
                              k == 0, k == KT - 1, tt == 0 and k == 0)
                m.then_inc(s_rp["proj"], 1)
            pe.wait_ge(s_rr["roped"], 8)
            pe.wait_ge(s_rp["gate"], 4)
            pe.wait_ge(s_rp["value"], 8)

            def ret_y(u):
                h, J = u // TT, u % TT
                m, half = h // 2, (h % 2) * RET_D
                pe.wait_ge(s_rt["decayed"], u + 1)
                if m >= 2 and u % (2 * TT) == 0:
                    pe.wait_ge(s_rt["ycopied"], m - 1)
                pe.matmul(ps[half:half + RET_D, 4 + m % 2, J * P:T], rv[:, J, h * RET_D:(h + 1) * RET_D],
                          scr[:, 1 + u % 2, 0:T - J * P], start=J == 0, stop=J == TT - 1).then_inc(s_rt["y"], 1)

            def late_mod(g):
                pe.wait_ge(s_ada["summed"], KT + 8 * (g + 1))
                mod_cols(3, 16 + 8 * g, ada_sum, 8)

            for u in range(RET_H * TT):
                h, J = u // TT, u % TT
                half = (h % 2) * RET_D
                if u > 8 and u % 8 == 1:
                    late_mod(u // 8 - 1)
                if u >= 2:
                    pe.wait_ge(s_rt["decayed"], u - 1)
                pe.matmul(ps[:, u % 2, 0:T - J * P], qk[half:half + RET_D, 4 + h // 2, J * P:(J + 1) * P],
                          qk[half:half + RET_D, h // 2, J * P:T], start=True, stop=True).then_inc(s_rt["scores"], 1)
                if u >= 1:
                    ret_y(u - 1)
            ret_y(RET_H * TT - 1)
            late_mod(3)
            for m in range(4):
                pe.wait_ge(s_rt["ycopied"], m + 1)
                pe.matmul(ps[:, 6, :], tab[:, BLOCKMEAN, :], qk[:, m, :], start=True,
                          stop=True).then_inc(s_rn["mean"], 1)
                pe.wait_ge(s_rn["sq"], m + 1)
                pe.matmul(ps[:, 7, :], tab[:, BLOCKMEAN, :], scr[:, 1, :], start=True,
                          stop=True).then_inc(s_rn["var"], 1)
            norm("normq", 2)
            norm("normkv", 1)
            pe.wait_ge(s_lat["copied"], 4)
            pe.matmul(ps[0:MLA_QK, 2, :], tab[0:MLA_QK, SWAP96, 0:MLA_QK], lat[0:MLA_QK, 3, :], start=True,
                      stop=True).then_inc(s_mr["perm"], 1)
            pe.wait_ge(s_norm["lo"], n_at("normkv", "lo") + 1)
            chunk(C_UQ)
            for h in range(MLA_H + 1):
                if h < MLA_H:
                    if h >= 2:
                        pe.wait_ge(s_mr["copied"], h - 1)
                    product(pe, C_UQ, ps[0:MLA_QK, h % 2, :], slice(h * MLA_QK, (h + 1) * MLA_QK), 2,
                            MLA_H * MLA_QK, qnH, qnL, s_mr["proj"], h == 0)
                if h >= 1:
                    pe.wait_ge(s_mr["copied"], h)
                    if h == 2:
                        pe.wait_ge(s_mr["kr"], 1)
                    if h >= 3:
                        pe.wait_ge(s_mr["roped"], h - 2)
                    pe.matmul(ps[0:MLA_QK, 2 + h % 2, :], tab[0:MLA_QK, SWAP96, 0:MLA_QK], qh[0:MLA_QK, h - 1, :],
                              start=True, stop=True).then_inc(s_mr["perm"], 1)
            chunk(C_UKV)
            for h in range(MLA_H):
                if h >= 2:
                    pe.wait_ge(s_mk["kcopied"], h - 1)
                product(pe, C_UKV, ps[:, h % 2, :], slice(h * P, (h + 1) * P), 1, MLA_H * P, kvH, kvL, s_mk["k"],
                        h == 0)
            vh = wH[C_UKV % SLOTS][:, 0:MLA_H * P].rearrange("p (h n) -> p h n", n=P)[:, :, NOPE:P]
            vl = wL[C_UKV % SLOTS][:, 0:MLA_H * P].rearrange("p (h n) -> p h n", n=P)[:, :, NOPE:P]
            for tt in range(TT):
                if tt >= 2:
                    pe.wait_ge(s_mk["vcopied"], tt - 1)
                rows = slice(tt * P, (tt + 1) * P)
                dst = ps[:, 4 + tt % 2, :].rearrange("p (h n) -> p h n", n=MLA_V)
                three(pe, dst, kvH[:, 0, rows], kvL[:, 0, rows], vh, vl, True, True).then_inc(s_mk["v"], 1)
            pe.wait_ge(s_mr["roped"], MLA_H)
            pe.wait_ge(s_mr["kr"], MLA_H + 1)
            pe.wait_ge(s_mk["kcopied"], MLA_H)
            pe.wait_ge(s_mk["vcopied"], TT)

            def mla_rest(u):
                h, qt = u // TT, u % TT
                pe.wait_ge(s_ma["probs"], u + 1)
                if u >= 2:
                    pe.wait_ge(s_ma["pt"], u - 1)
                for k in range(qt + 1):
                    m = pe.transpose(ps[:, 2 + u % 2, k * P:(k + 1) * P], scr[:, u % 2, k * P:(k + 1) * P],
                                     tab[:, IDENT, :])
                m.then_inc(s_ma["trans"], 1)
                if qt == TT - 1:
                    pe.wait_ge(s_ma["pt"], u + 1)
                    mm, half = h // 2, (h % 2) * MLA_V
                    if mm >= 2 and h % 2 == 0:
                        pe.wait_ge(s_ma["lo"], mm - 1)
                    for k in range(TT):
                        m = pe.matmul(ps[half:half + MLA_V, 4 + mm % 2, k * P:T], lat[:, k, h * MLA_V:(h + 1) * MLA_V],
                                      scr[:, 2 + k, k * P:T], start=k == 0, stop=k == TT - 1)
                    m.then_inc(s_ma["o"], 1)

            for u in range(MLA_H * TT):
                h, qt = u // TT, u % TT
                n = (qt + 1) * P
                if u >= 2:
                    pe.wait_ge(s_ma["exp"], u - 1)
                pe.matmul(ps[:, u % 2, 0:n], qh[0:MLA_QK, h, qt * P:n], kh[0:MLA_QK, h, 0:n], start=True,
                          stop=True).then_inc(s_ma["scores"], 1)
                if u >= 2:
                    mla_rest(u - 2)
            mla_rest(MLA_H * TT - 2)
            mla_rest(MLA_H * TT - 1)
            pe.wait_ge(s_ma["lo"], 4)
            pe.wait_ge(s_rn["lo"], 4)
            for t in range(KT):
                if t % 2 == 0:
                    chunk(C_OUT + t // 2)
                if t >= 4:
                    pe.wait_ge(s_wo1["added"], t - 3)
                tile(C_OUT + t // 2, t % 2, ps[:, t % 4, :], s_wo1["proj"])
            norm("norm2", KT)
            pe.wait_ge(s_norm["lo"], n_at("norm2", "lo") + KT)
            pe.wait_ge(s_q["keys"], 16)

            def key_scores(t):
                pe.wait_ge(s_q["copied"], t + 1)
                if t >= 2:
                    pe.wait_ge(s_q["scopied"], t - 1)
                for tt in range(TT):
                    m = pe.matmul(ps[:, 2 + t % 2, tt * P:(tt + 1) * P], qp[t % 2][:, tt * P:(tt + 1) * P],
                                  keysT[:, t % 2, :], start=True, stop=True)
                m.then_inc(s_q["scores"], 1)

            for t in range(16):
                if t % 2 == 0:
                    chunk(C_QUERY + t // 2)
                if t >= 2:
                    pe.wait_ge(s_q["copied"], t - 1)
                tile(C_QUERY + t // 2, t % 2, ps[:, t % 2, :], s_q["proj"])
                if t >= 1:
                    key_scores(t - 1)
            key_scores(15)
            for tt in range(TT):
                for n, r in enumerate((2, 0, 1)):
                    pe.wait_ge(s_q["chosen"], 3 * tt + n + 1)
                    if tt >= 1:
                        pe.wait_ge(s_q["tcopied"], 3 * tt - 2 + n)
                    pe.transpose(ps[:, 4 + r, 0:P], chosen[:, r, :], tab[:, IDENT, :]).then_inc(s_q["trans"], 1)

            def spread_four(par):
                for q in range(4):
                    m = pe.matmul(ps[:, par, q * P:(q + 1) * P], oneJ[par][:, q, :], oneI[par][:, q, :], start=True,
                                  stop=True)
                m.then_inc(s_w["prod"], 1)

            for par in range(4):
                pe.wait_ge(s_w["ones"], par + 1)
                spread_four(par)
            with pe.Fori(1, T // 16) as i:
                for par in range(4):
                    pe.wait_ge(s_w["ones"], 4 * i + par + 1)
                    pe.wait_ge(s_w["copied"], 4 * i + par - 3)
                    spread_four(par)
            pe.wait_ge(s_w["copied"], T // 4)

            def peer_pe(s0, i=0, has_a=True, has_o=True):
                if has_a:
                    k = C_PEER + max(0, 2 * s0 - 1)
                    chunk(k, i, 8)
                    for m in range(2):
                        if s0 >= 2:
                            pe.wait_ge(s_e["gelu"], 2 * (s0 - 2) + m + 1 + 8 * i)
                        tile(k, m, ps[:, 2 * (s0 % 2) + m, :], s_e["a"])
                if has_o:
                    k = C_PEER + (2 * s0 if has_a else 2 * s0 - 1)
                    chunk(k, i, 8)
                    pe.wait_ge(s_e["lo"], 2 * s0 + 8 * i)
                    wh = wH[k % SLOTS][:, :].rearrange("p (m d) -> p m d", m=2)
                    wl = wL[k % SLOTS][:, :].rearrange("p (m d) -> p m d", m=2)
                    par = (s0 - 1) % 2
                    for d in range(KT):
                        if s0 > 1 or d >= 4:
                            pe.wait_ge(s_e["added"], KT * (s0 - 1) + d - 3 + 4 * KT * i)
                        for m in range(2):
                            ins = three(pe, ps[:, 4 + d % 4, :], wh[:, m, d * P:(d + 1) * P],
                                        wl[:, m, d * P:(d + 1) * P], waH[par][m][:, :], waL[par][m][:, :],
                                        m == 0, m == 1, d == 0 and m == 0)
                        ins.then_inc(s_e["o"], 1)

            peer_pe(0, has_o=False)
            peer_pe(1)
            with pe.Fori(0, PEER_STEPS // 4 - 1) as i:
                for q in range(4):
                    peer_pe(2 + q, i)
            for s in range(PEER_STEPS - 2, PEER_STEPS):
                peer_pe(s)
            peer_pe(PEER_STEPS, has_a=False)
            norm("final1", KT)
            norm("mix0", KT)
            pe.wait_ge(s_p["lo"], len(WINDOWS))
            chunk(C_POOL)
            wph = wH[C_POOL % SLOTS][:, :].rearrange("p (g k n) -> p g k n", g=4, k=2)
            wpl = wL[C_POOL % SLOTS][:, :].rearrange("p (g k n) -> p g k n", g=4, k=2)
            for t in range(KT):
                g, e = t // 2, slice((t % 2) * P, (t % 2 + 1) * P)
                if t >= 4:
                    pe.wait_ge(s_p["added"], t - 3)
                for k in range(2):
                    m = three(pe, ps[:, t % 4, :], wph[:, g, k, e], wpl[:, g, k, e], hH[:, 2 * g + k, :],
                              hL[:, 2 * g + k, :], k == 0, k == 1, t == 0 and k == 0)
                m.then_inc(s_p["proj"], 1)

            def ffn_pe(l, c, s0, i=0, has_a=True, has_o=True):
                s = s_f[l]
                if has_a:
                    k = c + max(0, 2 * s0 - 1)
                    chunk(k, i, 4)
                    if s0 >= 2:
                        pe.wait_ge(s["act"], s0 - 1 + 2 * i)
                    for m in range(2):
                        tile(k, m, ps[:, 2 * (s0 % 2) + m, :], s["proj"])
                if has_o:
                    k = c + (2 * s0 if has_a else 2 * s0 - 1)
                    chunk(k, i, 4)
                    pe.wait_ge(s["lo"], s0 + 2 * i)
                    par = (s0 - 1) % 2
                    for d in range(KT):
                        if s0 > 1 or d >= 4:
                            pe.wait_ge(s["added"], KT * (s0 - 1) + d - 3 + 2 * KT * i)
                        cols = slice(d * P, (d + 1) * P)
                        three(pe, ps[:, 4 + d % 4, :], wH[k % SLOTS][:, cols], wL[k % SLOTS][:, cols], faH[par][:, :],
                              faL[par][:, :], True, True, d == 0).then_inc(s["o"], 1)

            def ffn_tensor(l, c):
                ffn_pe(l, c, 0, has_o=False)
                ffn_pe(l, c, 1)
                with pe.Fori(0, FT // 2 - 2) as i:
                    for q in range(2):
                        ffn_pe(l, c, 2 + q, i)
                ffn_pe(l, c, FT - 2)
                ffn_pe(l, c, FT - 1)
                ffn_pe(l, c, FT, has_a=False)

            norm("ffn0", KT)
            pe.wait_ge(s_norm["lo"], n_at("ffn0", "lo") + KT)
            ffn_tensor(0, C_FFN1)
            norm("mix1", KT)
            pe.wait_ge(s_norm["lo"], n_at("mix1", "lo") + KT)
            for t in range(17):
                if t < 16:
                    if t % 2 == 0:
                        chunk(C_QKV + t // 2)
                    if t >= 2:
                        pe.wait_ge(s_dr["copied"], t - 1)
                    tile(C_QKV + t // 2, t % 2, ps[:, t % 2, :], s_dr["proj"])
                if t >= 1:
                    pe.wait_ge(s_dr["copied"], t)
                    if t >= 3:
                        pe.wait_ge(s_dr["roped"], t - 2)
                    pe.matmul(ps[:, 2 + (t - 1) % 2, :], tab[:, SWAP64, :], dqk[:, t - 1, :], start=True,
                              stop=True).then_inc(s_dr["perm"], 1)
            for j in range(16):
                c, tt = C_QKV + 8 + j // TT, j % TT
                if tt == 0:
                    chunk(c)
                if j >= 2:
                    pe.wait_ge(s_dv["copied"], j - 1)
                wh = wH[c % SLOTS][:, :].rearrange("p (k n) -> p k n", k=KT)
                wl = wL[c % SLOTS][:, :].rearrange("p (k n) -> p k n", k=KT)
                rows = slice(tt * P, (tt + 1) * P)
                for k in range(KT):
                    m = three(pe, ps[:, 4 + j % 2, 0:256], hH[:, k, rows], hL[:, k, rows], wh[:, k, :], wl[:, k, :],
                              k == 0, k == KT - 1, tt == 0 and k == 0)
                m.then_inc(s_dv["v"], 1)
            pe.wait_ge(s_dr["roped"], 16)
            pe.wait_ge(s_dv["copied"], 16)

            def diff_rest(u):
                h, qt = u // TT, u % TT
                pe.wait_ge(s_da["probs"], u + 1)
                if u >= 2:
                    pe.wait_ge(s_da["at"], u - 1)
                for k in range(TT):
                    m = pe.transpose(ps[:, 4 + u % 2, k * P:(k + 1) * P], scr[:, 2 * (u % 2), k * P:(k + 1) * P],
                                     tab[:, IDENT, :])
                m.then_inc(s_da["trans"], 1)
                if qt == TT - 1:
                    pe.wait_ge(s_da["at"], u + 1)
                    if h >= 2:
                        pe.wait_ge(s_da["ycopied"], h - 1)
                    for k in range(TT):
                        m = pe.matmul(ps[:, 6 + h % 2, :], dv[:, k, h * P:(h + 1) * P], scr[:, 5 + k, :],
                                      start=k == 0, stop=k == TT - 1)
                    m.then_inc(s_da["o"], 1)

            for u in range(DIFF_H * TT):
                h, qt = u // TT, u % TT
                for c in range(2):
                    if u >= 2:
                        pe.wait_ge(s_da["exp"], 2 * (u - 2) + c + 1)
                    half = slice(c * HD, (c + 1) * HD)
                    pe.matmul(ps[:, 2 * (u % 2) + c, :], dqk[half, h, qt * P:(qt + 1) * P], dqk[half, 8 + h, :],
                              start=True, stop=True).then_inc(s_da["scores"], 1)
                if u >= 2:
                    diff_rest(u - 2)
            diff_rest(DIFF_H * TT - 2)
            diff_rest(DIFF_H * TT - 1)
            for h in range(DIFF_H):
                pe.wait_ge(s_dn["sq"], h + 1)
                pe.matmul(ps[:, h % 2, :], tab[:, ONES, :], scr[:, 0, :], start=True,
                          stop=True).then_inc(s_dn["sum"], 1)
            pe.wait_ge(s_dn["lo"], DIFF_H)
            for t in range(KT):
                if t % 2 == 0:
                    chunk(C_WO + t // 2)
                if t >= 4:
                    pe.wait_ge(s_wo2["added"], t - 3)
                tile(C_WO + t // 2, t % 2, ps[:, t % 4, :], s_wo2["proj"])
            norm("ffn1", KT)
            pe.wait_ge(s_norm["lo"], n_at("ffn1", "lo") + KT)
            ffn_tensor(1, C_FFN2)
            norm("final2", KT)


def ada_chunks(w):
    a = w[:, 0:2 * D].reshape(KT, P, 2 * D)
    b = w[:, 2 * D:].reshape(KT // 2, 2, P, 4, D).transpose(3, 0, 2, 1, 4).reshape(2 * KT, P, 2 * D)
    return np.concatenate([a, b], axis=0)


def constants():
    inv64 = np.float32(ROPE_THETA) ** (-np.arange(0, 64, 2, dtype=np.float32) / np.float32(64))
    inv32 = np.float32(ROPE_THETA) ** (-np.arange(0, 32, 2, dtype=np.float32) / np.float32(32))
    p = np.arange(P)
    f64 = inv64[p % 32].astype(np.float32)
    f96 = np.where((p >= NOPE) & (p < MLA_QK), inv32[(p - NOPE) % 16], 0).astype(np.float32)
    sign64 = np.where(p % 64 < 32, -1, 1).astype(np.float32)
    sign96 = np.where((p - NOPE) % 32 < 16, -1, 1).astype(np.float32)
    tables = np.zeros((P, NTAB, P), np.float32)
    tables[:, ONES] = 1
    tables[:, IDENT] = np.eye(P)
    for a in p:
        tables[a, SWAP64, a ^ 32] = 1
        if NOPE <= a < MLA_QK:
            tables[a, SWAP96, NOPE + ((a - NOPE) ^ 16)] = 1
    tables[:, BLOCKMEAN] = (p[:, None] // RET_D == p[None, :] // RET_D) / RET_D
    tables[:, CAUSAL] = np.where(p[None, :] <= p[:, None], 0, NEG)
    tables[:, IOTA] = p[None, :]
    gamma = 1.0 - 2.0 ** (-5.0 - np.arange(RET_H, dtype=np.float64))
    diff = np.arange(T)[None, :] - p[:, None]
    decays = np.where(diff >= 0, gamma[:, None, None] ** np.maximum(diff, 0), 0) * RET_D ** -0.5
    t = np.arange(T)
    recips = np.stack([1.0 / (np.clip(t + w - w // 2, 0, T) - np.clip(t - w // 2, 0, T)) for w in WINDOWS])
    return {
        "freq": [("inv64", f64), ("inv96", f96), ("sign64", sign64), ("sign96", sign96)],
        "tables": tables,
        "decays": decays.astype(np.float32),
        "recips": np.broadcast_to(recips[None].astype(np.float32), (P, len(WINDOWS), T)),
    }


def layout(inputs):
    g = {k: np.asarray(v) for k, v in inputs.items()}

    def cols(v):
        return v.reshape(-1, P).T

    def chunks(w, n=256):
        k, m = w.shape
        return w.reshape(k // P, P, m // n, n).transpose(2, 1, 0, 3).reshape(m // n, P, (k // P) * n)

    con = constants()
    vec = np.zeros((P, NVEC), np.float32)

    def put(name, v):
        o, n = VEC[name]
        vec[:, o:o + n] = v.reshape(P, n)

    for name, v in (("c", g["c"][0]), ("b_ada", g["b_ada"][0]), ("g_norm1", g["g_norm1"][0]), ("g_q", g["g_q_norm"][0]),
                    ("g_kv", g["g_kv_norm"][0]), ("g_ret", g["g_ret_norm"][0]), ("g_norm2", g["g_norm2"][0]),
                    ("g_final", g["g_final"]), ("mix0", g["mix_norm_2"][0]), ("mix1", g["mix_norm_2"][1]),
                    ("pool_scale", g["pool_scale_2"][0]), ("subln", g["diff_subln_2"][0]),
                    ("ffn0", g["ffn_norm_2"][0]), ("ffn1", g["ffn_norm_2"][1]), ("final", g["final_norm_2"])):
        put(name, cols(v))
    for l in range(2):
        cv = np.concatenate([g["ffn_conv_w_2"][l], g["ffn_conv_b_2"][l][None]])
        put(f"conv{l}", cv.reshape(4, FT, P).transpose(2, 1, 0))
    for name, v in con["freq"]:
        put(name, v)
    w_in = g["w_in"][0]
    o = Q_RANK + P + ROPE
    w_kv = np.concatenate([w_in[:, Q_RANK:Q_RANK + P], w_in[:, Q_RANK:Q_RANK + NOPE], w_in[:, Q_RANK + P:o]], 1)
    rw = RET_H * RET_D
    ret = np.concatenate([w_in[:, o:o + 2 * rw], w_in[:, o + 3 * rw:], w_in[:, o + 2 * rw:o + 3 * rw]], 1)
    up = g["ffn_w_up_2"].reshape(2, KT, P, 2, FT, P).transpose(0, 4, 2, 1, 3, 5).reshape(2, FT, P, CHUNK)
    a = {
        "vectors": vec,
        "tables": con["tables"],
        "decays": con["decays"],
        "recips": con["recips"],
        "positions_l": np.concatenate([g["positions"].reshape(1, T), g["positions_2"].reshape(1, T)], 1),
        "lams": np.concatenate([g[f"diff_lam_{n}_2"].reshape(1, HD) for n in ("q1", "k1", "q2", "k2")], 1),
        "x_l": g["x"][0].T.reshape(KT, P, T).transpose(1, 0, 2),
        "w_ada_l": ada_chunks(g["w_ada"][0]),
        "w_lat0": chunks(w_in[:, 0:Q_RANK])[0],
        "w_lat1": chunks(w_kv, 224)[0],
        "w_ret_l": chunks(ret),
        "w_uq_l": chunks(g["w_uq"][0], MLA_H * MLA_QK)[0],
        "w_ukv_l": g["w_ukv"][0],
        "w_out_l": chunks(g["w_out"][0]),
        "w_query_l": chunks(g["w_query"][0]),
        "keys_l": g["sub_keys"][0].transpose(2, 0, 1),
        "u_l": chunks(g["expert_u"][0].T),
        "v_l": g["expert_v"][0].reshape(PEER_STEPS, 2, P, D).transpose(0, 2, 1, 3).reshape(PEER_STEPS, P, CHUNK),
        "pool_l": g["pool_w_2"][0].reshape(4, 2, P, 256).transpose(2, 0, 1, 3).reshape(P, CHUNK),
        "up_l": up,
        "down_l": g["ffn_w_down_2"].reshape(2, FT, P, D),
        "w_qkv_l": chunks(g["diff_w_qkv_2"][0]),
        "w_o_l": chunks(g["diff_w_o_2"][0]),
    }
    return {k: np.ascontiguousarray(v) for k, v in a.items()}


def kernel(**inputs):
    import concourse.bacc as bacc
    from concourse.bass_utils import run_bass_kernel_spmd

    arrays = layout(inputs)
    nc = bacc.Bacc("TRN2", target_bir_lowering=False, num_devices=1)
    args = {n: nc.dram_tensor(n, a.shape, mybir.dt.from_np(a.dtype), kind="ExternalInput").ap()
            for n, a in arrays.items()}
    args["w_scratch"] = nc.dram_tensor("w_scratch", (NTB, P, P, TB), F32).ap()
    outs = {"out": nc.dram_tensor("out", (P, KT, T), F32, kind="ExternalOutput").ap()}
    build(nc, args, outs)
    r = run_bass_kernel_spmd(nc, [arrays], core_ids=[0])
    y = r.results[0]["out"]
    return np.ascontiguousarray(y.transpose(2, 1, 0).reshape(1, T, D))
```

```python
from contextlib import ExitStack

import numpy as np

import concourse.bass as bass
from concourse import mybir

F32 = mybir.dt.float32
F32R = mybir.dt.float32r
I32 = mybir.dt.int32
U32 = mybir.dt.uint32
ACT = mybir.ActivationFunctionType
ALU = mybir.AluOpType
AX = mybir.AxisListType.X

P = 128
D, T = 1024, 512
KT, TT = D // P, T // P
EPS = 1e-6
ROPE_THETA = 10000.0
MLA_H, NOPE, ROPE, MLA_V, Q_RANK = 8, 64, 32, 64, 256
MLA_QK = NOPE + ROPE
RET_H, RET_D = 8, 64
PEER_H, PEER_KEYS, TOPK = 8, 128, 16
N_EXP = PEER_KEYS * PEER_KEYS
DIFF_H, HD = 8, 64
SUBLN_EPS = 1e-5
LAM_INIT = float(0.8 - 0.6 * np.exp(-0.3))
D_FF = 2816
FT = D_FF // P
WINDOWS = (2, 4, 8, 16)
NEG = -1e30
FAR_BELOW = -3.0e38
PAIRS = 16 + 7 * 8 + 8

CHUNK, STAGES, SLOTS = 2048, 2, 4

C_LAT, C_KV, C_RQK, C_RG, C_RV = 0, 1, 2, 6, 8
C_UQ, C_UKV, C_OUT, C_QUERY, C_PEER = 10, 11, 12, 16, 24
PEER_STEPS = N_EXP // 256
C_POOL = C_PEER + 2 * PEER_STEPS
C_FFN1 = C_POOL + 1
C_QKV = C_FFN1 + 2 * FT
C_WO = C_QKV + 12
C_FFN2 = C_WO + 4
C_END = C_FFN2 + 2 * FT

VEC = {}
for _name, _n in (("c", 8), ("b_ada", 48), ("g_norm1", 8), ("g_q", 2), ("g_kv", 1), ("g_ret", 4), ("g_norm2", 8),
                  ("g_final", 8), ("mix0", 8), ("mix1", 8), ("pool_scale", 8), ("subln", 1), ("ffn0", 8),
                  ("ffn1", 8), ("final", 8), ("conv0", 4 * FT), ("conv1", 4 * FT),
                  ("inv64", 1), ("inv96", 1), ("sign64", 1), ("sign96", 1)):
    VEC[_name] = (sum(n for _, n in VEC.values()), _n)
NVEC = sum(n for _, n in VEC.values())
ONES, IDENT, SWAP64, SWAP96, BLOCKMEAN, CAUSAL, IOTA = range(7)
NTAB = 7

TB = 32
NTB = T // TB


class Chain:

    def __init__(self, eng, sem):
        self.eng, self.sem, self.n = eng, sem, 0

    def __call__(self, ins):
        ins.then_inc(self.sem, 1)
        self.n = self.n + 1
        self.eng.wait_ge(self.sem, self.n)


def build(nc, A, O):
    out = O.get("out")
    with ExitStack() as ctx:
        def sb(name, shape, dt=F32, scope=ctx):
            return scope.enter_context(nc.sbuf_tensor("sb_" + name, shape, dt))

        def sem(name):
            return ctx.enter_context(nc.semaphore(name))

        def sems(stage, *names):
            return {n: sem(stage + "_" + n) for n in names}

        xT = sb("xT", [P, KT, T])
        hH = sb("hH", [P, KT, T], F32R)
        hL = sb("hL", [P, KT, T], F32R)
        stage = [sb(f"stage{i}", [P, CHUNK]) for i in range(STAGES)]
        wH = [sb(f"wH{i}", [P, CHUNK], F32R) for i in range(SLOTS)]
        wL = [sb(f"wL{i}", [P, CHUNK], F32R) for i in range(SLOTS)]
        vec = sb("vec", [P, NVEC])
        tab = sb("tab", [P, NTAB, P])
        mod = sb("mod", [P, 48])
        gain1 = sb("gain1", [P, KT])
        gain2 = sb("gain2", [P, KT])
        small = sb("small", [P, 16])
        scr = sb("scr", [P, 9, T])
        posi = sb("posi", [P, T], I32)
        lams = sb("lams", [P, 4, HD])
        sinkv = sb("sinkv", [P, HD])
        stats = sb("stats", [P, 8, 32])
        sc = small[:, 8:8 + KT]
        ps = ctx.enter_context(nc.psum_tensor("ps", [P, 8, T], F32))

        def col(name, i=0, n=1):
            o, m = VEC[name]
            assert i + n <= m
            return vec[:, o + i:o + i + n]

        with ExitStack() as s1:
            ada = [sb(f"ada{i}", [P, CHUNK], scope=s1) for i in range(4)]
            ada_sum1 = sb("ada_sum1", [P, CHUNK], scope=s1)
            sc1 = sb("sc1", [P, KT], scope=s1)
        lat_scope = ExitStack()
        lat = sb("lat", [P, 4, T], scope=lat_scope)
        with ExitStack() as s2:
            qk = sb("qk", [P, 8, T], scope=s2)
            rv = sb("rv", [P, TT, RET_H * RET_D], scope=s2)
            rg = sb("rg", [P, 4, T], scope=s2)
            rope_r = sb("rope_r", [P, 2, T], scope=s2)
            decay = [sb(f"decay{i}", [P, T], scope=s2) for i in range(2)]
            ada_sum = sb("ada_sum", [P, D], scope=s2)
        with ExitStack() as s3:
            qnH = sb("qnH", [P, 2, T], F32R, scope=s3)
            qnL = sb("qnL", [P, 2, T], F32R, scope=s3)
            kvH = sb("kvH", [P, 1, T], F32R, scope=s3)
            kvL = sb("kvL", [P, 1, T], F32R, scope=s3)
            qh = sb("qh", [P, MLA_H, T], scope=s3)
            kh = sb("kh", [P, MLA_H, T], scope=s3)
        lat_scope.close()
        with ExitStack() as s4:
            fromsel = sb("fromsel", [P, 3, T], scope=s4)
            with ExitStack() as s5:
                keysT = sb("keysT", [P, 2, P], scope=s5)
                qp = [sb(f"qp{i}", [P, T], scope=s5) for i in range(2)]
                sc_k = [sb(f"sc_k{i}", [P, TT, P], scope=s5) for i in range(2)]
                sc_m = sb("sc_m", [P, TT, P], scope=s5)
                topv = sb("topv", [P, TT, 16, TOPK], scope=s5)
                topi = sb("topi", [P, TT, 16, TOPK], U32, scope=s5)
                topf = sb("topf", [P, TT, 16, TOPK], scope=s5)
                cand = sb("cand", [P, PEER_H, PAIRS], scope=s5)
                cand2 = sb("cand2", [P, PEER_H, PAIRS], scope=s5)
                best = sb("best", [P, PEER_H, TOPK], scope=s5)
                pos = sb("pos", [P, PEER_H, TOPK], U32, scope=s5)
                posu = sb("posu", [P, 2, PEER_H, TOPK], U32, scope=s5)
                posf = sb("posf", [P, 2, PEER_H, TOPK], scope=s5)
                last = sb("last", [P, PEER_H, TOPK], scope=s5)
                second = sb("second", [P, PEER_H, TOPK], scope=s5)
                chosen = sb("chosen", [P, 3, PEER_H * TOPK], scope=s5)
                gsum = sb("gsum", [P, 2, PEER_H], scope=s5)
            with ExitStack() as s6:
                wst = [sb(f"wst{i}", [P, P, TB], scope=s6) for i in range(2)]
        oneJ, oneI = [[scr[:, 4 * q + i, :].rearrange("p (t n) -> p t n", t=4) for i in range(4)] for q in range(2)]
        with ExitStack() as s7:
            wg = [sb(f"wg{i}", [P, NTB, 4, TB], scope=s7) for i in range(2)]
            ga = [sb(f"ga{i}", [P, T], scope=s7) for i in range(2)]
            wa = [sb(f"wa{i}", [P, T], scope=s7) for i in range(2)]
            waH = [[sb(f"waH{i}{m}", [P, T], F32R, scope=s7) for m in range(2)] for i in range(2)]
            waL = [[sb(f"waL{i}{m}", [P, T], F32R, scope=s7) for m in range(2)] for i in range(2)]
        PAD = 8
        with ExitStack() as s8:
            hp = sb("hp", [P, KT, T + 2 * PAD], scope=s8)
            wbuf = [sb(f"wbuf{i}", [P, 2, T + 2 * PAD], scope=s8) for i in range(2)]
            wbuf2 = [sb(f"wbuf2{i}", [P, 2, T + 2 * PAD], scope=s8) for i in range(2)]
            recips = sb("recips", [P, len(WINDOWS), T], scope=s8)
        with ExitStack() as s9:
            dqk = sb("dqk", [P, 16, T], scope=s9)
            dv = sb("dv", [P, TT, D], scope=s9)
            rope_d = sb("rope_d", [P, 2, T], scope=s9)
        with ExitStack() as s10:
            gcv = [sb(f"gcv{i}", [P, T], scope=s10) for i in range(2)]
            gel = [sb(f"gel{i}", [P, T], scope=s10) for i in range(2)]
            fa = [sb(f"fa{i}", [P, T], scope=s10) for i in range(2)]
            faH = [sb(f"faH{i}", [P, T], F32R, scope=s10) for i in range(2)]
            faL = [sb(f"faL{i}", [P, T], F32R, scope=s10) for i in range(2)]

        wd = A["w_scratch"]

        ld_const = sem("ld_const")
        ld_x = sem("ld_x")
        ld_ada = [sem(f"ld_ada{i}") for i in range(4)]
        ld_stage = [sem(f"ld_stage{i}") for i in range(STAGES)]
        w_hi = sem("w_hi")
        w_split = sem("w_split")
        w_begun = sem("w_begun")
        s_ada = sems("ada", "silu", "exp", "summed", "cols", "mod", "ld0", "ld1")
        s_norm = sems("norm", "sq", "sum", "rec", "root", "xr", "t", "hi", "lo")
        NORMS = (("norm1", KT, 1), ("normq", 2, 1), ("normkv", 1, 1), ("norm2", KT, 1), ("final1", KT, 0),
                 ("mix0", KT, 0), ("ffn0", KT, 1), ("mix1", KT, 1), ("ffn1", KT, 1), ("final2", KT, 0))

        NORM_GAIN = {"normq": "g_q", "normkv": "g_kv", "final1": "g_final", "mix0": "mix0", "ffn0": "ffn0",
                     "mix1": "mix1", "ffn1": "ffn1", "final2": "final"}

        def norm_out(k):
            return scr[:, (7, 8, 0, 1)[k % 4], :]

        def norm_bank(name):
            return 0 if name in ("final1", "mix1", "ffn1", "final2") else 7

        def n_at(name, what):
            at = 0
            for n, tiles, split in NORMS:
                if n == name:
                    return at
                if what in ("rec", "root"):
                    at += 1
                elif what == "xr":
                    at += 0 if n in NORM_GAIN else tiles
                else:
                    at += tiles * split if what in ("hi", "lo") else tiles

        s_lat = sems("lat", "proj", "copied")
        s_tr = sems("tabr", "arg", "sin")
        s_tm = sems("tabm", "arg", "sin")
        s_td = sems("tabd", "arg", "sin")
        s_rr = sems("rrope", "proj", "copied", "perm", "roped")
        s_rp = sems("rproj", "proj", "gate", "value")
        s_rt = sems("ret", "scores", "decayed", "y", "ycopied", "ld0", "ld1")
        s_rn = sems("retn", "mean", "cent", "sq", "var", "rec", "root", "gexp", "yn", "hi", "lo")
        s_mr = sems("mrope", "proj", "copied", "perm", "roped", "kr")
        s_mk = sems("mkv", "k", "kcopied", "v", "vcopied")
        s_ma = sems("mla", "scores", "negmax", "exp", "probs", "trans", "pt", "o", "hi", "lo")
        s_wo1 = sems("wout", "proj", "added")
        s_q = sems("query", "keys", "proj", "copied", "scores", "scopied", "top", "negbest", "gexp", "chosen",
                   "trans", "tcopied", "hits", "spread")
        s_w = sems("wbuild", "hits", "ones", "prod", "copied", "st0", "st1")
        s_e = sems("peer", "ld0", "ld1", "a", "gelu", "wa", "hi", "lo", "o", "added")
        s_p = sems("pool", "ld", "filled", "win_dve", "win_pool", "hi_dve", "hi_pool", "lo_dve", "lo_pool",
                   "proj", "added")
        s_f = [sems(f"ffn{i}_l", "proj", "conv", "gelu", "act", "hi", "lo", "o", "added") for i in range(2)]
        s_dr = sems("drope", "proj", "copied", "perm", "roped")
        s_dv = sems("dvals", "v", "copied")
        s_da = sems("diff", "lam", "scores", "negmax", "exp", "probs", "trans", "at", "o")
        s_dn = sems("subln", "sq", "sum", "rec", "root", "yn", "hi", "lo")
        s_wo2 = sems("wo", "proj", "added")
        v_chain = sem("v_chain")
        g_chain = sem("g_chain")
        stored = sem("stored")

        def load(sp, c, src, c0=None):
            k = c if c0 is None else c0
            n = src.shape[-1]
            if k >= STAGES:
                sp.wait_ge(w_split, c - (STAGES - 1))
            sp.dma_start(stage[k % STAGES][:, 0:n], src).then_inc(ld_stage[k % STAGES], 16)

        def landed(k, i=0, per=0):
            return 16 * (k // STAGES + 1) + i * (16 * per // STAGES)

        def split_hi(act, k, n=CHUNK, i=0, per=0):
            act.wait_ge(ld_stage[k % STAGES], landed(k, i, per))
            if k >= SLOTS:
                act.wait_ge(w_begun, k - SLOTS + 2 + i * per)
            act.activation(wH[k % SLOTS][:, 0:n], stage[k % STAGES][:, 0:n], ACT.Copy).then_inc(w_hi, 1)

        def split_lo(dve, k, n=CHUNK, i=0, per=0):
            dve.wait_ge(w_hi, k + 1 + i * per)
            dve.tensor_tensor(wL[k % SLOTS][:, 0:n], stage[k % STAGES][:, 0:n], wH[k % SLOTS][:, 0:n],
                              ALU.subtract).then_inc(w_split, 1)

        def chunk_len(k):
            if k == C_KV:
                return KT * 224
            if k == C_UQ:
                return 2 * MLA_H * MLA_QK
            if k == C_UKV:
                return MLA_H * (NOPE + MLA_V)
            if k > C_FFN1 and k < C_QKV:
                return CHUNK if is_up(k - C_FFN1) else D
            if k > C_FFN2 and k < C_END:
                return CHUNK if is_up(k - C_FFN2) else D
            return CHUNK

        def is_up(r):
            return r == 0 or (r % 2 == 1 and r != 2 * FT - 1)

        def split_hi_at(act, k):
            if k < C_END:
                split_hi(act, k, chunk_len(k))

        def split_lo_at(dve, k):
            if k < C_END:
                split_lo(dve, k, chunk_len(k))

        def three(pe, dst, lh, ll, rh, rl, first, last, begins=False):
            m = pe.matmul(dst, lh, rl, start=first, stop=False)
            if begins:
                m.then_inc(w_begun, 1)
            pe.matmul(dst, ll, rh, start=False, stop=False)
            return pe.matmul(dst, lh, rh, start=False, stop=last)

        def product(pe, k, dst, cols, nkt, width, rH, rL, done, begins, arriving=None):
            wh = wH[k % SLOTS][:, 0:nkt * width].rearrange("p (k n) -> p k n", k=nkt)
            wl = wL[k % SLOTS][:, 0:nkt * width].rearrange("p (k n) -> p k n", k=nkt)
            for q in range(nkt):
                if arriving:
                    pe.wait_ge(*arriving(q))
                m = three(pe, dst, wh[:, q, cols], wl[:, q, cols], rH[:, q, :], rL[:, q, :], q == 0, q == nkt - 1,
                          begins and q == 0)
            m.then_inc(done, 1)

        def window(g):
            return scr[:, 2 * g:2 * g + 2, :]

        def pool_windows(eng, groups, chained, buf, who):
            eng.wait_ge(s_norm["t"], n_at("mix0", "t") + KT)
            eng.wait_ge(s_p["ld"], 16)
            width = T + 2 * PAD
            for g in groups:
                h2 = hp[:, 2 * g:2 * g + 2, :]
                a = h2
                for r in range(g + 1):
                    e = 1 << r
                    l, rt = (1, 0) if r == 0 else (e // 2, e // 2)
                    chained(eng.tensor_tensor(buf[r % 2][:, :, e:width - e], a[:, :, e - l:width - e - l],
                                              a[:, :, e + rt:width - e + rt], ALU.add))
                    a = buf[r % 2]
                rec = recips[:, g, :].unsqueeze(1).broadcast_to([P, 2, T])
                mean = buf[(g + 1) % 2][:, :, 0:T]
                chained(eng.tensor_tensor(mean, a[:, :, PAD:PAD + T], rec, ALU.mult))
                eng.tensor_tensor(window(g), mean, h2[:, :, PAD:PAD + T], ALU.subtract).then_inc(s_p["win_" + who], 1)
                eng.wait_ge(s_p["hi_" + who], g % 2 + 1)
                eng.tensor_tensor(hL[:, 2 * g:2 * g + 2, :], window(g), hH[:, 2 * g:2 * g + 2, :],
                                  ALU.subtract).then_inc(s_p["lo_" + who], 1)

        def sub_root(b):
            return dv[:, b, :].rearrange("p (h t) -> p h t", h=2)

        def pick_buffers():
            return [scr[:, 4 * q:4 * q + 4, :].rearrange("p b (k a) -> p (b k) a", a=TOPK) for q in range(2)]

        block = ctx.enter_context(nc.Block())

        @block.sync
        def _(sp):
            sp.dma_start(vec[:, :], A["vectors"]).then_inc(ld_const, 16)
            sp.dma_start(posi[:, :], A["positions_l"][:, 0:T].broadcast_to([P, T])).then_inc(ld_const, 16)
            sp.dma_start(lams[:, :, :].rearrange("p a b -> p (a b)"),
                         A["lams"].broadcast_to([P, 4 * HD])).then_inc(ld_const, 16)
            sp.dma_start(tab[:, :, :], A["tables"]).then_inc(ld_const, 16)
            for k in range(KT):
                if k == 4:
                    sp.dma_start(xT[:, :, :], A["x_l"]).then_inc(ld_x, 16)
                if k >= 4:
                    sp.wait_ge(s_ada["summed"], k - 3)
                sp.dma_start(ada[k % 4][:, :], A["w_ada_l"][k]).then_inc(ld_ada[k % 4], 16)
            for k in range(2):
                load(sp, k, [A["w_lat0"], A["w_lat1"]][k])
            for k in range(8):
                load(sp, 2 + k, A["w_ret_l"][k])
            load(sp, C_UQ, A["w_uq_l"])
            load(sp, C_UKV, A["w_ukv_l"])
            for r in range(16):
                if r < 2:
                    sp.wait_ge(w_split, C_UQ + r + 1)
                else:
                    sp.wait_ge(s_ada["summed"], KT + 2 * (r - 1))
                sp.dma_start(stage[r % 2][:, :], A["w_ada_l"][KT + r]).then_inc(s_ada[f"ld{r % 2}"], 16)
            sp.wait_ge(s_ada["summed"], KT + 32)
            for k in range(4):
                load(sp, C_OUT + k, A["w_out_l"][k])
            sp.wait_ge(s_tm["arg"], 1)
            sp.dma_start(posi[:, :], A["positions_l"][:, T:2 * T].broadcast_to([P, T])).then_inc(ld_const, 16)
            load(sp, C_QUERY, A["w_query_l"][0])
            load(sp, C_QUERY + 1, A["w_query_l"][1])
            sp.wait_ge(s_wo1["added"], KT)
            sp.dma_start(keysT[:, :, :], A["keys_l"]).then_inc(s_q["keys"], 16)
            for k in range(2, 8):
                load(sp, C_QUERY + k, A["w_query_l"][k])
            load(sp, C_PEER, A["u_l"][0])
            load(sp, C_PEER + 1, A["u_l"][1])
            load(sp, C_PEER + 2, A["v_l"][0])
            with sp.Fori(0, NTB // 2) as b:
                for par in range(2):
                    sp.wait_ge(s_w["copied"], (TB // 4) * (2 * b + par + 1))
                    sp.dma_start(wd[2 * b + par], wst[par][:, :, :]).then_inc(s_w[f"st{par}"], 16)
            for par in range(2):
                sp.wait_ge(s_w[f"st{par}"], 16 * (NTB // 2))
            wd_i = wd.rearrange("b j i t -> j b i t")
            for par in range(2):
                sp.dma_start(wg[par][:, :, :, :], wd_i[:, :, 4 * par:4 * par + 4, :]).then_inc(s_e[f"ld{par}"], 16)
            with sp.Fori(0, PEER_STEPS // 4 - 1) as i:
                for q in range(4):
                    load(sp, C_PEER + 3 + 2 * q + 8 * i, A["u_l"][4 * i + q + 2], C_PEER + 3 + 2 * q)
                    load(sp, C_PEER + 4 + 2 * q + 8 * i, A["v_l"][4 * i + q + 1], C_PEER + 4 + 2 * q)
                    if q % 2 == 1:
                        par = q // 2
                        sp.wait_ge(s_e["wa"], 4 * (2 * i + par) + 4)
                        sp.dma_start(wg[par][:, :, :, :], wd_i[:, :, bass.ds((2 * i + par + 2) * 4, 4), :]
                                     ).then_inc(s_e[f"ld{par}"], 16)
            for s in range(PEER_STEPS - 4, PEER_STEPS + 1):
                c = C_PEER + 2 * s + 3
                if s + 2 < PEER_STEPS:
                    load(sp, c, A["u_l"][s + 2])
                    load(sp, c + 1, A["v_l"][s + 1])
                elif s + 1 < PEER_STEPS:
                    load(sp, c, A["v_l"][s + 1])
            load(sp, C_POOL, A["pool_l"])
            sp.wait_ge(s_norm["t"], n_at("final1", "t") + KT)
            sp.dma_start(recips[:, :, :], A["recips"]).then_inc(s_p["ld"], 16)

            def ffn_loads(l, c):
                load(sp, c, A["up_l"][l, 0])
                load(sp, c + 1, A["up_l"][l, 1])
                load(sp, c + 2, A["down_l"][l, 0])
                with sp.Fori(0, FT // 2 - 1) as i:
                    for q in range(2):
                        load(sp, c + 3 + 2 * q + 4 * i, A["up_l"][l, 2 * i + q + 2], c + 3 + 2 * q)
                        load(sp, c + 4 + 2 * q + 4 * i, A["down_l"][l, 2 * i + q + 1], c + 4 + 2 * q)
                load(sp, c + 2 * FT - 1, A["down_l"][l, FT - 1])

            ffn_loads(0, C_FFN1)
            for k in range(12):
                load(sp, C_QKV + k, A["w_qkv_l"][k])
            for k in range(4):
                load(sp, C_WO + k, A["w_o_l"][k])
            ffn_loads(1, C_FFN2)
            for k in range(KT):
                sp.wait_ge(s_norm["t"], n_at("final2", "t") + k + 1)
                sp.dma_start(out[:, k, :], xT[:, k, :]).then_inc(stored, 16)
            sp.wait_ge(stored, 16 * KT)

        @block.scalar
        def _(act):
            def norm(name, src, nkt, gains=None, shifts=None, dstH=None, dstL=None, ready=None, mod_at=None):
                s = s_norm
                for k in range(nkt):
                    if ready:
                        act.wait_ge(ready[0], ready[1] + k + 1)
                    if k >= 2:
                        act.wait_ge(s["sum"], n_at(name, "sum") + k - 1)
                    act.activation(scr[:, k % 2, :], src(k), ACT.Square).then_inc(s["sq"], 1)
                act.wait_ge(s["rec"], n_at(name, "rec") + 1)
                act.activation(scr[:, 3, :], scr[:, 4, :], ACT.Sqrt).then_inc(s["root"], 1)
                if mod_at:
                    act.wait_ge(s_ada["mod"], mod_at)
                if name in NORM_GAIN:
                    for k in range(nkt if dstH is not None else 0):
                        act.wait_ge(s["t"], n_at(name, "t") + k + 1)
                        act.activation(dstH[:, k, :], norm_out(k), ACT.Copy).then_inc(s["hi"], 1)
                    return
                for k in range(nkt):
                    act.wait_ge(s["xr"], n_at(name, "xr") + k + 1)
                    if k >= 2:
                        act.wait_ge(s["lo"], n_at(name, "lo") + k - 1)
                    d = scr[:, 7 + k % 2, :]
                    act.activation(d, scr[:, k % 2, :], ACT.Identity, scale=gains(k),
                                   bias=shifts(k)).then_inc(s["t"], 1)
                    act.wait_ge(s["t"], n_at(name, "t") + k + 1)
                    act.activation(dstH[:, k, :], d, ACT.Copy).then_inc(s["hi"], 1)

            def rope_tables(s, tabs):
                for q in range(2):
                    act.wait_ge(s["arg"], q + 1)
                    act.activation(tabs(q), tabs(q), ACT.Sin).then_inc(s["sin"], 1)

            act.wait_ge(ld_const, 64)
            act.activation(sc1[:, :], col("c", 0, 8), ACT.Exp, scale=-1.0).then_inc(s_ada["exp"], 1)
            act.wait_ge(ld_x, 16)
            norm("norm1", lambda k: xT[:, k, :], KT, lambda k: gain1[:, k:k + 1], lambda k: mod[:, k:k + 1],
                 dstH=hH, dstL=hL, mod_at=2)
            split_hi_at(act, 0)
            split_hi_at(act, 1)

            def load_decay(h):
                if h >= 2:
                    act.wait_ge(s_rt["decayed"], TT * (h - 1))
                act.dma_start(decay[h % 2][:, :], A["decays"][h]).then_inc(s_rt[f"ld{h % 2}"], 16)

            act.wait_ge(s_norm["lo"], n_at("norm1", "lo") + KT)
            load_decay(0)
            load_decay(1)
            rope_tables(s_tr, lambda q: rope_r[:, q, :])
            for t in range(4):
                if t % 2 == 0:
                    split_hi_at(act, C_LAT + t // 2 + 2)
                n = P if t < 3 else MLA_QK
                act.wait_ge(s_lat["proj"], t + 1)
                act.activation(lat[0:n, t, :], ps[0:n, t % 2, :], ACT.Copy).then_inc(s_lat["copied"], 1)
            for t in range(8):
                if t % 2 == 0:
                    split_hi_at(act, C_RQK + t // 2 + 2)
                act.wait_ge(s_rr["proj"], t + 1)
                act.activation(qk[:, t, :], ps[:, t % 2, :], ACT.Copy).then_inc(s_rr["copied"], 1)
            act.wait_ge(s_rr["roped"], 8)
            act.wait_ge(s_lat["copied"], 4)
            norm("normq", lambda k: lat[:, k, :], 2)
            for t in range(4):
                if t % 2 == 0:
                    split_hi_at(act, C_RG + t // 2 + 2)
                act.wait_ge(s_rp["proj"], t + 1)
                act.activation(rg[:, t, :], ps[:, t % 2, :], ACT.Copy).then_inc(s_rp["gate"], 1)
            norm("normkv", lambda k: lat[:, 2, :], 1)
            split_hi_at(act, C_RV + 2)
            split_hi_at(act, C_RV + 3)
            act.wait_ge(s_rp["gate"], 4)
            act.wait_ge(s_norm["t"], n_at("normkv", "t") + 1)
            act.activation(scr[:, 5:9, :], rg[:, :, :], ACT.Exp, scale=-1.0).then_inc(s_rn["gexp"], 1)
            for m in range(4):
                if m < 3:
                    load_decay(2 * m + 2)
                    load_decay(2 * m + 3)
                act.wait_ge(s_rt["y"], 2 * TT * (m + 1))
                act.activation(qk[:, m, :], ps[:, 4 + m % 2, :], ACT.Copy).then_inc(s_rt["ycopied"], 1)
            for b in range(2):
                act.wait_ge(s_rn["cent"], b + 1)
                act.activation(qk[:, 4 + 2 * b:6 + 2 * b, :], qk[:, 2 * b:2 * b + 2, :], ACT.Square
                               ).then_inc(s_rn["sq"], 1)
            for b in range(2):
                act.wait_ge(s_rn["rec"], b + 1)
                act.activation(qk[:, 4 + 2 * b:6 + 2 * b, :], qk[:, 4 + 2 * b:6 + 2 * b, :], ACT.Sqrt
                               ).then_inc(s_rn["root"], 1)
            for b in range(2):
                act.wait_ge(s_rn["yn"], b + 1)
                act.activation(hH[:, 4 + 2 * b:6 + 2 * b, :], qk[:, 2 * b:2 * b + 2, :], ACT.Copy
                               ).then_inc(s_rn["hi"], 1)
            act.wait_ge(s_rn["lo"], 2)
            for k in range(2):
                act.activation(qnH[:, k, :], lat[:, k, :], ACT.Copy).then_inc(s_norm["hi"], 1)
            act.activation(kvH[:, 0, :], lat[:, 2, :], ACT.Copy).then_inc(s_norm["hi"], 1)
            rope_tables(s_tm, lambda q: scr[:, 7 + q, :])
            for h in range(MLA_H):
                act.wait_ge(s_mr["proj"], h + 1)
                act.activation(qh[0:MLA_QK, h, :], ps[0:MLA_QK, h % 2, :], ACT.Copy).then_inc(s_mr["copied"], 1)
            split_hi_at(act, C_OUT)
            for h in range(MLA_H):
                act.wait_ge(s_mk["k"], h + 1)
                act.activation(kh[0:NOPE, h, :], ps[0:NOPE, h % 2, :], ACT.Copy).then_inc(s_mk["kcopied"], 1)
            split_hi_at(act, C_OUT + 1)

            def mla_pt(u):
                h, qt = u // TT, u % TT
                act.wait_ge(s_ma["trans"], u + 1)
                if qt == 0 and h >= 1:
                    act.wait_ge(s_ma["o"], h)
                act.activation(scr[:, 2:2 + qt + 1, qt * P:(qt + 1) * P],
                               ps[:, 2 + u % 2, 0:(qt + 1) * P].rearrange("p (k n) -> p k n", n=P),
                               ACT.Copy).then_inc(s_ma["pt"], 1)
                if qt == 0 and h >= 1 and h % 2 == 0:
                    mla_hi(h // 2 - 1)

            def mla_hi(m):
                act.wait_ge(s_ma["o"], 2 * m + 2)
                act.activation(hH[:, m, :], ps[:, 4 + m % 2, :], ACT.Copy).then_inc(s_ma["hi"], 1)

            for u in range(MLA_H * TT):
                n = (u % TT + 1) * P
                act.wait_ge(s_ma["negmax"], u + 1)
                if u >= 2:
                    act.wait_ge(s_ma["trans"], u - 1)
                act.activation(scr[:, u % 2, 0:n], ps[:, u % 2, 0:n], ACT.Exp, bias=stats[:, 1, u:u + 1],
                               scale=MLA_QK ** -0.5, accum_out=stats[:, 2, u:u + 1]).then_inc(s_ma["exp"], 1)
                if u >= 2:
                    mla_pt(u - 2)
            mla_pt(MLA_H * TT - 2)
            mla_pt(MLA_H * TT - 1)
            mla_hi(MLA_H // 2 - 1)
            for k in range(4):
                split_hi_at(act, C_OUT + k + 2)
            norm("norm2", lambda k: xT[:, k, :], KT, lambda k: gain2[:, k:k + 1], lambda k: mod[:, 24 + k:25 + k],
                 dstH=hH, dstL=hL,
                 ready=(s_wo1["added"], 0), mod_at=4)

            def keys_copy(t):
                act.wait_ge(s_q["scores"], t + 1)
                if t >= 2:
                    act.wait_ge(s_q["top"], t - 1)
                act.activation(sc_k[t % 2][:, :, :], ps[:, 2 + t % 2, :].rearrange("p (a n) -> p a n", n=P),
                               ACT.Copy).then_inc(s_q["scopied"], 1)

            for t in range(16):
                if t % 2 == 0 and t // 2 < 7:
                    split_hi_at(act, C_QUERY + t // 2 + 2)
                act.wait_ge(s_q["proj"], t + 1)
                if t >= 2:
                    act.wait_ge(s_q["scores"], t - 1)
                act.activation(qp[t % 2][:, :], ps[:, t % 2, :], ACT.Copy).then_inc(s_q["copied"], 1)
                if t >= 1:
                    keys_copy(t - 1)
            keys_copy(15)
            for tt in range(TT):
                act.wait_ge(s_q["negbest"], tt + 1)
                act.activation(best[:, :, :], best[:, :, :], ACT.Exp).then_inc(s_q["gexp"], 1)
                for n, r in enumerate((2, 0, 1)):
                    act.wait_ge(s_q["trans"], 3 * tt + n + 1)
                    act.activation(fromsel[:, r, tt * P:(tt + 1) * P], ps[:, 4 + r, 0:P],
                                   ACT.Copy).then_inc(s_q["tcopied"], 1)
            with act.Fori(0, NTB // 2) as b:
                for par in range(2):
                    for g in range(TB // 4):
                        if g == 0:
                            act.wait_ge(s_w[f"st{par}"], b * 16)
                        act.wait_ge(s_w["prod"], (2 * b + par) * (TB // 4) + g + 1)
                        act.activation(wst[par][:, :, 4 * g:4 * g + 4],
                                       ps[:, g % 4, :].rearrange("p (t i) -> p i t", t=4),
                                       ACT.Copy).then_inc(s_w["copied"], 1)
            def peer_act(s0, i=0, has_a=True, splits=2):
                for q in range(splits):
                    split_hi(act, C_PEER + 2 * s0 + 1 + q, CHUNK, i, 8)
                if not has_a:
                    return
                for m in range(2):
                    act.wait_ge(s_e["a"], 2 * s0 + m + 1 + 8 * i)
                    if s0 > 0:
                        act.wait_ge(s_e["wa"], 2 * s0 - 2 + m + 1 + 8 * i)
                    act.activation(ga[m][:, :], ps[:, 2 * (s0 % 2) + m, :], ACT.Gelu).then_inc(s_e["gelu"], 1)
                for m in range(2):
                    act.wait_ge(s_e["wa"], 2 * s0 + m + 1 + 8 * i)
                    if s0 >= 2:
                        act.wait_ge(s_e["o"], KT * (s0 - 1) + 8 * KT // 2 * i)
                    act.activation(waH[s0 % 2][m][:, :], wa[m][:, :], ACT.Copy).then_inc(s_e["hi"], 1)

            for par in range(2):
                act.wait_ge(s_w[f"st{par}"], 16 * (NTB // 2))
            peer_act(0)
            peer_act(1)
            with act.Fori(0, PEER_STEPS // 4 - 1) as i:
                for q in range(4):
                    peer_act(2 + q, i)
            for s in range(PEER_STEPS - 2, PEER_STEPS):
                peer_act(s, splits=2 if s < PEER_STEPS - 1 else 1)
            norm("final1", lambda k: xT[:, k, :], KT,
                 ready=(s_e["added"], KT * (PEER_STEPS - 1)))
            act.wait_ge(s_norm["t"], n_at("final1", "t") + KT)
            act.wait_ge(s_p["filled"], 1)
            norm("mix0", lambda k: xT[:, k, :], KT)
            split_hi_at(act, C_POOL)
            for g in (0, 2, 1, 3):
                who = "dve" if g >= 2 else "pool"
                act.wait_ge(s_p["win_" + who], g % 2 + 1)
                act.activation(hH[:, 2 * g:2 * g + 2, :], window(g), ACT.Copy).then_inc(s_p["hi_" + who], 1)
            split_hi_at(act, C_POOL + 1)
            split_hi_at(act, C_POOL + 2)

            def ffn_act(l, c, s0, i=0, has_a=True, splits=2):
                s = s_f[l]
                for q in range(splits):
                    k = c + 2 * s0 + 1 + q
                    split_hi(act, k, CHUNK if is_up(k - c) else D, i, 4)
                if not has_a:
                    return
                act.wait_ge(s["conv"], s0 + 1 + 2 * i)
                if s0 >= 1:
                    act.wait_ge(s["act"], s0 + 2 * i)
                act.activation(gel[s0 % 2][:, :], gcv[s0 % 2][:, :], ACT.Gelu).then_inc(s["gelu"], 1)
                act.wait_ge(s["act"], s0 + 1 + 2 * i)
                if s0 >= 2:
                    act.wait_ge(s["o"], KT * (s0 - 1) + 2 * KT * i)
                act.activation(faH[s0 % 2][:, :], fa[s0 % 2][:, :], ACT.Copy).then_inc(s["hi"], 1)

            def ffn_scalar(l, c):
                ffn_act(l, c, 0, splits=0)
                split_hi(act, c + 2, D)
                ffn_act(l, c, 1)
                with act.Fori(0, FT // 2 - 2) as i:
                    for q in range(2):
                        ffn_act(l, c, 2 + q, i)
                ffn_act(l, c, FT - 2)
                ffn_act(l, c, FT - 1, splits=1)

            norm("ffn0", lambda k: xT[:, k, :], KT, dstH=hH, dstL=hL,
                 ready=(s_p["added"], 0))
            ffn_scalar(0, C_FFN1)
            split_hi_at(act, C_QKV)
            split_hi_at(act, C_QKV + 1)
            norm("mix1", lambda k: xT[:, k, :], KT, dstH=hH, dstL=hL,
                 ready=(s_f[0]["added"], KT * (FT - 1)))
            rope_tables(s_td, lambda q: rope_d[:, q, :])
            for t in range(16):
                if t % 2 == 0:
                    split_hi_at(act, C_QKV + t // 2 + 2)
                act.wait_ge(s_dr["proj"], t + 1)
                act.activation(dqk[:, t, :], ps[:, t % 2, :], ACT.Copy).then_inc(s_dr["copied"], 1)
            for k in range(4):
                split_hi_at(act, C_QKV + 8 + k + 2)
            act.wait_ge(s_da["lam"], 1)
            act.activation(small[:, 2:4], small[:, 0:2], ACT.Exp).then_inc(s_da["lam"], 1)

            def diff_at(u):
                h, qt = u // TT, u % TT
                act.wait_ge(s_da["trans"], u + 1)
                if qt == 0 and h >= 1:
                    act.wait_ge(s_da["o"], h)
                act.activation(scr[:, 5:9, qt * P:(qt + 1) * P],
                               ps[:, 4 + u % 2, :].rearrange("p (k n) -> p k n", n=P),
                               ACT.Copy).then_inc(s_da["at"], 1)
                if qt == 0 and h >= 1:
                    diff_y(h - 1)

            def diff_y(h):
                act.wait_ge(s_da["o"], h + 1)
                act.activation(dqk[:, h, :], ps[:, 6 + h % 2, :], ACT.Copy)
                act.activation(dqk[:, 8 + h, :], ps[:, 6 + h % 2, :], ACT.Square).then_inc(s_dn["sq"], 1)

            for u in range(DIFF_H * TT):
                for c in range(2):
                    act.wait_ge(s_da["negmax"], 2 * u + c + 1)
                    if u >= 2:
                        act.wait_ge(s_da["trans"], u - 1)
                    act.activation(scr[:, 2 * (u % 2) + c, :], ps[:, 2 * (u % 2) + c, :], ACT.Exp,
                                   bias=stats[:, 4 * c + 1, u:u + 1], scale=HD ** -0.5,
                                   accum_out=stats[:, 4 * c + 2, u:u + 1]).then_inc(s_da["exp"], 1)
                if u >= 2:
                    diff_at(u - 2)
            diff_at(DIFF_H * TT - 2)
            diff_at(DIFF_H * TT - 1)
            diff_y(DIFF_H - 1)
            def subln_hi(b):
                act.wait_ge(s_dn["yn"], b + 1)
                act.activation(hH[:, 2 * b:2 * b + 2, :], dqk[:, 2 * b:2 * b + 2, :], ACT.Copy).then_inc(s_dn["hi"], 1)

            for b in range(DIFF_H // 2):
                act.wait_ge(s_dn["rec"], b + 1)
                act.activation(sub_root(b), sub_root(b), ACT.Sqrt).then_inc(s_dn["root"], 1)
                if b >= 1:
                    subln_hi(b - 1)
            subln_hi(DIFF_H // 2 - 1)
            for k in range(4):
                split_hi_at(act, C_WO + k + 2)
            norm("ffn1", lambda k: xT[:, k, :], KT, dstH=hH, dstL=hL,
                 ready=(s_wo2["added"], 0))
            ffn_scalar(1, C_FFN2)
            norm("final2", lambda k: xT[:, k, :], KT,
                 ready=(s_f[1]["added"], KT * (FT - 1)))

        @block.vector
        def _(dve):
            chain = Chain(dve, v_chain)

            def rsqrt(var, root, rec_done, root_done, n):
                dve.reciprocal(scr[:, 4, :], var).then_inc(rec_done, 1)
                dve.wait_ge(root_done, n)
                chain(dve.tensor_tensor(scr[:, 5, :], var, scr[:, 3, :], ALU.mult))
                chain(dve.scalar_tensor_tensor(scr[:, 5, :], scr[:, 5, :], -0.5, scr[:, 3, :], ALU.mult, ALU.mult))
                chain(dve.scalar_tensor_tensor(root, scr[:, 5, :], 1.5, scr[:, 3, :], ALU.add, ALU.mult))

            def norm_root(name, nkt):
                s = s_norm
                dve.wait_ge(s["sum"], n_at(name, "sum") + nkt)
                chain(dve.tensor_scalar(scr[:, 2, :], ps[:, norm_bank(name), :], 1.0 / (nkt * P), EPS, ALU.mult,
                                        ALU.add))
                rsqrt(scr[:, 2, :], scr[:, 6, :], s["rec"], s["root"], n_at(name, "root") + 1)

            def norm(name, src, nkt, dst=None, dstL=None, dstH=None, rooted=False):
                s = s_norm
                if not rooted:
                    norm_root(name, nkt)

                if name in NORM_GAIN:
                    for k in range(nkt):
                        if dst is None and k >= 4:
                            dve.wait_ge(s["lo"], n_at(name, "lo") + k - 3)
                        dve.scalar_tensor_tensor(norm_out(k) if dst is None else dst(k), src(k),
                                                 col(NORM_GAIN[name], k), scr[:, 6, :], ALU.mult,
                                                 ALU.mult).then_inc(s["t"], 1)
                    return

                def low(k):
                    dve.wait_ge(s["hi"], n_at(name, "hi") + k + 1)
                    dve.tensor_tensor(dstL[:, k, :], scr[:, 7 + k % 2, :], dstH[:, k, :],
                                      ALU.subtract).then_inc(s["lo"], 1)

                for k in range(nkt):
                    if k >= 2:
                        dve.wait_ge(s["t"], n_at(name, "t") + k - 1)
                    dve.tensor_tensor(scr[:, k % 2, :], src(k), scr[:, 6, :], ALU.mult).then_inc(s["xr"], 1)
                    if dst is None and k >= 1:
                        low(k - 1)
                if dst is None:
                    low(nkt - 1)

            def rope_tables(s, tabs, positions, inv, sign):
                two_pi = 2.0 * np.pi
                hi = float(np.float32(6.28125))
                mid = float(np.float32(two_pi - hi))
                mid = float((np.float32(mid).view(np.uint32) & np.uint32(0xFFFFF000)).view(np.float32))
                lo = float(np.float32(two_pi - hi - mid))
                ang, turn = scr[:, 5, :], scr[:, 6, :]
                chain(dve.tensor_copy(ang, positions))
                chain(dve.tensor_scalar(ang, ang, inv, None, ALU.mult))
                for q in range(2):
                    chain(dve.tensor_scalar(turn, ang, 1.0 / two_pi, 0.25 if q == 0 else 0.0, ALU.mult, ALU.add))
                    chain(dve.tensor_scalar(turn, turn, 12582912.0, None, ALU.add))
                    chain(dve.tensor_scalar(turn, turn, -12582912.0, None, ALU.add))
                    chain(dve.scalar_tensor_tensor(tabs(q), turn, -hi, ang, ALU.mult, ALU.add))
                    chain(dve.scalar_tensor_tensor(tabs(q), turn, -mid, tabs(q), ALU.mult, ALU.add))
                    chain(dve.scalar_tensor_tensor(tabs(q), turn, -lo, tabs(q), ALU.mult, ALU.add))
                    if q == 0:
                        chain(dve.tensor_scalar(tabs(q), tabs(q), float(np.pi / 2), None, ALU.add))
                    dve.tensor_scalar(tabs(q), tabs(q), 3.1415925, -3.1415925, ALU.min, ALU.max).then_inc(s["arg"], 1)
                dve.wait_ge(s["sin"], 2)
                chain(dve.tensor_scalar(tabs(1), tabs(1), sign, None, ALU.mult))

            def rope(x, swapped, tabs, n, done):
                tmp = scr[0:n, 0, :]
                chain(dve.tensor_tensor(tmp, swapped, tabs(1)[0:n], ALU.mult))
                chain(dve.tensor_tensor(x, x, tabs(0)[0:n], ALU.mult))
                dve.tensor_tensor(x, x, tmp, ALU.add).then_inc(done, 1)

            dve.wait_ge(ld_const, 64)
            dve.wait_ge(s_ada["exp"], 1)
            chain(dve.tensor_scalar(sc1[:, :], sc1[:, :], 1.0, None, ALU.add))
            chain(dve.reciprocal(sc1[:, :], sc1[:, :]))
            dve.tensor_tensor(sc[:, :], sc1[:, :], col("c", 0, 8), ALU.mult).then_inc(s_ada["silu"], 1)
            dve.wait_ge(s_ada["silu"], 1)
            for k in range(KT):
                if k == KT - 2:
                    norm_root("norm1", KT)
                dve.wait_ge(ld_ada[k % 4], 16 * (k // 4 + 1))
                if k == 0:
                    op = dve.tensor_scalar(ada_sum1[:, :], ada[0][:, :], sc[:, 0:1], None, ALU.mult)
                else:
                    op = dve.scalar_tensor_tensor(ada_sum1[:, :], ada[k % 4][:, :], sc[:, k:k + 1], ada_sum1[:, :],
                                                  ALU.mult, ALU.add)
                op.then_inc(s_ada["summed"], 1)
                dve.wait_ge(s_ada["summed"], k + 1)
            dve.wait_ge(s_ada["cols"], 1)
            dve.tensor_tensor(mod[:, 0:16], ps[:, 0, 0:16], col("b_ada", 0, 16), ALU.add).then_inc(s_ada["mod"], 1)
            dve.wait_ge(s_ada["mod"], 1)

            def gain(g, scale, name):
                chain(dve.tensor_scalar(g[:, :], scale, 1.0, None, ALU.add))
                dve.tensor_tensor(g[:, :], g[:, :], col(name, 0, 8), ALU.mult).then_inc(s_ada["mod"], 1)

            gain(gain1, mod[:, 8:16], "g_norm1")
            norm("norm1", lambda k: xT[:, k, :], KT, dstL=hL, dstH=hH, rooted=True)
            split_lo_at(dve, 0)
            split_lo_at(dve, 1)
            dve.wait_ge(s_norm["lo"], n_at("norm1", "lo") + KT)
            rope_tables(s_tr, lambda q: rope_r[:, q, :], posi[:, :], col("inv64"), col("sign64"))
            split_lo_at(dve, 2)
            split_lo_at(dve, 3)
            for t in range(8):
                if t % 2 == 0:
                    split_lo_at(dve, C_RQK + t // 2 + 2)
                dve.wait_ge(s_rr["perm"], t + 1)
                rope(qk[:, t, :], ps[:, 2 + t % 2, :], lambda q: rope_r[:, q, :], P, s_rr["roped"])
                dve.wait_ge(s_rr["roped"], t + 1)
            norm("normq", lambda k: lat[:, k, :], 2, dst=lambda k: lat[:, k, :])
            split_lo_at(dve, C_RG + 2)
            split_lo_at(dve, C_RG + 3)
            norm("normkv", lambda k: lat[:, 2, :], 1, dst=lambda k: lat[:, 2, :])
            for j in range(8):
                c, tt = j // TT, j % TT
                dve.wait_ge(s_rp["proj"], 4 + j + 1)
                dve.tensor_copy(rv[:, tt, c * 256:(c + 1) * 256], ps[:, 4 + j % 2, 0:256]).then_inc(s_rp["value"], 1)
            split_lo_at(dve, C_RV + 2)
            split_lo_at(dve, C_RV + 3)
            def ada_chunk(r):
                dve.wait_ge(s_ada[f"ld{r % 2}"], 16 * (r // 2 + 1))
                if r % 4 == 0 and r:
                    dve.wait_ge(s_ada["cols"], 1 + r // 4)
                for j in range(2):
                    k = 2 * (r % 4) + j
                    w = stage[r % 2][:, j * D:(j + 1) * D]
                    if k == 0:
                        op = dve.tensor_scalar(ada_sum[:, :], w, sc[:, 0:1], None, ALU.mult)
                    else:
                        op = dve.scalar_tensor_tensor(ada_sum[:, :], w, sc[:, k:k + 1], ada_sum[:, :], ALU.mult,
                                                      ALU.add)
                    op.then_inc(s_ada["summed"], 1)
                    dve.wait_ge(s_ada["summed"], KT + 2 * r + j + 1)

            for u in range(RET_H * TT):
                h, J = u // TT, u % TT
                n = T - P * J
                dve.wait_ge(s_rt["scores"], u + 1)
                dve.wait_ge(s_rt[f"ld{h % 2}"], 16 * (h // 2 + 1))
                if u >= 2:
                    dve.wait_ge(s_rt["y"], u - 1)
                dve.tensor_tensor(scr[:, 1 + u % 2, 0:n], ps[:, u % 2, 0:n], decay[h % 2][:, 0:n],
                                  ALU.mult).then_inc(s_rt["decayed"], 1)
                if u % 2 == 1:
                    ada_chunk(u // 2)
                if u == 2 * TT:
                    dve.wait_ge(s_rn["gexp"], 1)
                    g4 = scr[:, 5:9, :]
                    chain(dve.tensor_scalar(g4, g4, 1.0, None, ALU.add))
                    chain(dve.reciprocal(g4, g4))
                    chain(dve.tensor_tensor(g4, g4, rg[:, :, :], ALU.mult))
            dve.wait_ge(s_ada["cols"], 5)
            dve.tensor_tensor(mod[:, 16:48], ps[:, 3, 16:48], col("b_ada", 16, 32), ALU.add).then_inc(s_ada["mod"], 1)
            dve.wait_ge(s_ada["mod"], 3)
            gain(gain2, mod[:, 32:40], "g_norm2")
            for b in range(2):
                y = qk[:, 2 * b:2 * b + 2, :]
                dve.wait_ge(s_rn["mean"], 2 * b + 2)
                dve.tensor_tensor(y, y, ps[:, 6 * b:6 * b + 2, :], ALU.subtract).then_inc(s_rn["cent"], 1)
            for b in range(2):
                dve.wait_ge(s_rn["var"], 2 * b + 2)
                chain(dve.tensor_scalar(rv[:, 2 * b:2 * b + 2, :], ps[:, 4 - 2 * b:6 - 2 * b, :], EPS, None, ALU.add))
                dve.reciprocal(qk[:, 4 + 2 * b:6 + 2 * b, :], rv[:, 2 * b:2 * b + 2, :]).then_inc(s_rn["rec"], 1)
            for b in range(2):
                var, root = rv[:, 2 * b:2 * b + 2, :], qk[:, 4 + 2 * b:6 + 2 * b, :]
                tmp = scr[:, 1 + 2 * b:3 + 2 * b, :]
                dve.wait_ge(s_rn["root"], b + 1)
                chain(dve.tensor_tensor(tmp, var, root, ALU.mult))
                chain(dve.scalar_tensor_tensor(tmp, tmp, -0.5, root, ALU.mult, ALU.mult))
                chain(dve.scalar_tensor_tensor(tmp, tmp, 1.5, root, ALU.add, ALU.mult))
                chain(dve.tensor_tensor(tmp, tmp, scr[:, 5 + 2 * b:7 + 2 * b, :], ALU.mult))
                for m in (2 * b, 2 * b + 1):
                    op = dve.scalar_tensor_tensor(qk[:, m, :], qk[:, m, :], col("g_ret", m), tmp[:, m - 2 * b, :],
                                                  ALU.mult, ALU.mult)
                op.then_inc(s_rn["yn"], 1)
            rope_tables(s_tm, lambda q: scr[:, 7 + q, :], posi[:, :], col("inv96"), col("sign96"))
            mla_tabs = lambda q: scr[:, 7 + q, :]
            dve.wait_ge(s_mr["perm"], 1)
            rope(lat[0:MLA_QK, 3, :], ps[0:MLA_QK, 2, :], mla_tabs, MLA_QK, s_mr["kr"])
            dve.wait_ge(s_mr["kr"], 1)
            for h in range(MLA_H):
                dve.tensor_copy(kh[NOPE:MLA_QK, h, :], lat[NOPE:MLA_QK, 3, :]).then_inc(s_mr["kr"], 1)
            for h in range(MLA_H):
                dve.wait_ge(s_mr["perm"], h + 2)
                rope(qh[0:MLA_QK, h, :], ps[0:MLA_QK, 2 + (h + 1) % 2, :], mla_tabs, MLA_QK, s_mr["roped"])
                dve.wait_ge(s_mr["roped"], h + 1)
            split_lo_at(dve, C_OUT)
            for tt in range(TT):
                dve.wait_ge(s_mk["v"], tt + 1)
                dve.wait_ge(s_mr["kr"], MLA_H + 1)
                dve.tensor_copy(lat[:, tt, :], ps[:, 4 + tt % 2, :]).then_inc(s_mk["vcopied"], 1)
            split_lo_at(dve, C_OUT + 1)

            def mla_probs(u):
                n = (u % TT + 1) * P
                dve.wait_ge(s_ma["exp"], u + 1)
                chain(dve.reciprocal(stats[:, 3, u:u + 1], stats[:, 2, u:u + 1]))
                dve.tensor_scalar(scr[:, u % 2, 0:n], scr[:, u % 2, 0:n], stats[:, 3, u:u + 1], None,
                                  ALU.mult).then_inc(s_ma["probs"], 1)
                if u % (2 * TT) == 2 * TT - 1 and u >= 2 * TT:
                    mla_low(u // (2 * TT) - 1)

            def mla_low(m):
                dve.wait_ge(s_ma["hi"], m + 1)
                dve.tensor_tensor(hL[:, m, :], ps[:, 4 + m % 2, :], hH[:, m, :], ALU.subtract).then_inc(s_ma["lo"], 1)

            for u in range(MLA_H * TT):
                qt = u % TT
                n = (qt + 1) * P
                dve.wait_ge(s_ma["scores"], u + 1)
                diag = ps[:, u % 2, qt * P:(qt + 1) * P]
                chain(dve.tensor_tensor(diag, diag, tab[:, CAUSAL, :], ALU.add))
                chain(dve.reduce_max(stats[:, 0, u:u + 1], ps[:, u % 2, 0:n], AX))
                dve.tensor_scalar(stats[:, 1, u:u + 1], stats[:, 0, u:u + 1], -(MLA_QK ** -0.5), None,
                                  ALU.mult).then_inc(s_ma["negmax"], 1)
                if u >= 1:
                    mla_probs(u - 1)
            mla_probs(MLA_H * TT - 1)
            mla_low(3)
            for k in range(4):
                split_lo_at(dve, C_OUT + k + 2)
                for j in range(2):
                    t = 2 * k + j
                    dve.wait_ge(s_wo1["proj"], t + 1)
                    dve.scalar_tensor_tensor(xT[:, t, :], ps[:, t % 4, :], mod[:, 16 + t:17 + t], xT[:, t, :],
                                             ALU.mult, ALU.add).then_inc(s_wo1["added"], 1)
            dve.wait_ge(s_wo1["added"], KT)
            norm("norm2", lambda k: xT[:, k, :], KT, dstL=hL, dstH=hH)

            def top16(rows):
                for q, step in enumerate((
                        lambda vals, masked, v, i: dve.max(v[:, 0:8], vals),
                        lambda vals, masked, v, i: dve.max_index(i[:, 0:8], v[:, 0:8], vals),
                        lambda vals, masked, v, i: dve.match_replace(masked, v[:, 0:8], vals, FAR_BELOW),
                        lambda vals, masked, v, i: dve.max(v[:, 8:16], masked),
                        lambda vals, masked, v, i: dve.max_index(i[:, 8:16], v[:, 8:16], masked))):
                    for row in rows:
                        op = step(*row)
                    if q != 1:
                        chain(op)

            for t in range(16):
                if t % 2 == 0 and t // 2 < 7:
                    split_lo_at(dve, C_QUERY + t // 2 + 2)
                dve.wait_ge(s_q["scopied"], t + 1)
                top16([(sc_k[t % 2][:, tt, :], sc_m[:, tt, :], topv[:, tt, t, :], topi[:, tt, t, :])
                       for tt in range(TT)])
                dve.tensor_copy(topf[:, :, t, :], topi[:, :, t, :]).then_inc(s_q["top"], 1)
            dve.wait_ge(s_q["top"], 16)
            picks = pick_buffers()

            def key_indices(tt):
                for half in range(2):
                    dve.wait_ge(s_q["spread"], 2 * tt + half + 1)
                    if half == 0 and tt >= 1:
                        dve.wait_ge(s_q["trans"], 3 * tt)
                    dve.tensor_reduce(chosen[:, half, :], picks[half], AX, ALU.add).then_inc(s_q["chosen"], 1)

            for tt in range(TT):
                v = topv[:, tt, :, :].rearrange("p (h two) a -> p h two a", two=2)
                dve.tensor_tensor(cand[:, :, 0:16], v[:, :, 0, 0:1].broadcast_to([P, PEER_H, 16]), v[:, :, 1, :],
                                  ALU.add)
                dve.tensor_tensor(cand[:, :, 16:72].rearrange("p h (a b) -> p h a b", a=7),
                                  v[:, :, 0, 1:8].unsqueeze(3).broadcast_to([P, PEER_H, 7, 8]),
                                  v[:, :, 1, 0:8].unsqueeze(2).broadcast_to([P, PEER_H, 7, 8]), ALU.add)
                chain(dve.tensor_tensor(cand[:, :, 72:80], v[:, :, 0, 8:16],
                                        v[:, :, 1, 0:1].broadcast_to([P, PEER_H, 8]), ALU.add))
                top16([(cand[:, h, :], cand2[:, h, :], best[:, h, :], pos[:, h, :]) for h in range(PEER_H)])
                chain(dve.tensor_copy(gsum[:, 0, :], best[:, :, 0]))
                dve.tensor_tensor(best[:, :, :], best[:, :, :], gsum[:, 0, :].unsqueeze(2).broadcast_to(
                    [P, PEER_H, TOPK]), ALU.subtract).then_inc(s_q["negbest"], 1)
                dve.tensor_scalar(posu[:, 0], pos[:, :, :], 3, None, ALU.logical_shift_right)
                chain(dve.tensor_scalar(posu[:, 1], pos[:, :, :], 7, None, ALU.bitwise_and))
                chain(dve.tensor_copy(posf[:, :, :, :], posu[:, :, :, :]))
                dve.tensor_scalar(second[:, :, :], posf[:, 0], 1.0, 8.0, ALU.is_equal, ALU.mult)
                chain(dve.scalar_tensor_tensor(last[:, :, :], posf[:, 0], 9.0, posf[:, 1], ALU.is_equal, ALU.mult))
                dve.tensor_scalar(posf[:, 0], posf[:, 0], -1.0, 0.0, ALU.add, ALU.max)
                chain(dve.tensor_tensor(posf[:, 1], posf[:, 1], last[:, :, :], ALU.subtract))
                dve.tensor_tensor(posf[:, 0], posf[:, 0], last[:, :, :], ALU.add)
                chain(dve.tensor_tensor(posf[:, 1], posf[:, 1], second[:, :, :], ALU.add))
                if tt >= 1:
                    key_indices(tt - 1)
                    dve.wait_ge(s_q["chosen"], 3 * tt)
                iota = tab[:, IOTA, 0:TOPK].unsqueeze(1).broadcast_to([P, PEER_H * TOPK, TOPK])
                for half in range(2):
                    dve.tensor_tensor(picks[half], iota, posf[:, half].rearrange("p h k -> p (h k)").unsqueeze(2)
                                      .broadcast_to([P, PEER_H * TOPK, TOPK]), ALU.is_equal).then_inc(s_q["hits"], 1)
                dve.wait_ge(s_q["gexp"], tt + 1)
                chain(dve.tensor_reduce(gsum[:, 0, :], best[:, :, :], AX, ALU.add))
                chain(dve.reciprocal(gsum[:, 1, :], gsum[:, 0, :]))
                if tt >= 1:
                    dve.wait_ge(s_q["trans"], 3 * tt - 2)
                dve.tensor_tensor(chosen[:, 2, :].rearrange("p (h k) -> p h k", k=TOPK), best[:, :, :],
                                  gsum[:, 1, :].unsqueeze(2).broadcast_to([P, PEER_H, TOPK]),
                                  ALU.mult).then_inc(s_q["chosen"], 1)
                dve.wait_ge(s_q["chosen"], 3 * tt + 1)
            key_indices(TT - 1)
            dve.wait_ge(s_q["tcopied"], 3 * TT)

            iota4 = tab[:, IOTA, :].unsqueeze(1).broadcast_to([P, 4, P])

            def hits(par, tok):
                for half, ones in ((1, oneJ[par]), (0, oneI[par])):
                    ins = dve.tensor_tensor(ones[:, :, :], iota4, fromsel[:, half, bass.ds(tok, 4)].unsqueeze(2)
                                            .broadcast_to([P, 4, P]), ALU.is_equal)
                ins.then_inc(s_w["hits"], 1)

            for par in range(4):
                hits(par, 4 * par)
            with dve.Fori(1, T // 16) as i:
                for par in range(4):
                    dve.wait_ge(s_w["prod"], 4 * i + par - 3)
                    hits(par, i * 16 + 4 * par)

            def peer_dve(s0, i=0, has_a=True, splits=2, has_o=True):
                for q in range(splits):
                    split_lo(dve, C_PEER + 2 * s0 + 1 + q, CHUNK, i, 8)
                if has_a:
                    par = (s0 // 2) % 2
                    dve.wait_ge(s_e[f"ld{par}"], 16 * (s0 // 4 + 1) + 16 * i)
                    for m in range(2):
                        dve.wait_ge(s_e["gelu"], 2 * s0 + m + 1 + 8 * i)
                        if s0 >= 1:
                            dve.wait_ge(s_e["lo"], 2 * s0 + m - 1 + 8 * i)
                        dve.tensor_tensor(wa[m][:, :].rearrange("p (b t) -> p b t", b=NTB),
                                          ga[m][:, :].rearrange("p (b t) -> p b t", b=NTB),
                                          wg[par][:, :, 2 * (s0 % 2) + m, :], ALU.mult).then_inc(s_e["wa"], 1)
                    for m in range(2):
                        dve.wait_ge(s_e["hi"], 2 * s0 + m + 1 + 8 * i)
                        dve.tensor_tensor(waL[s0 % 2][m][:, :], wa[m][:, :], waH[s0 % 2][m][:, :],
                                          ALU.subtract).then_inc(s_e["lo"], 1)
                if has_o:
                    for d in range(KT):
                        dve.wait_ge(s_e["o"], KT * (s0 - 1) + d + 1 + 4 * KT * i)
                        if s0 >= 2:
                            dve.wait_ge(s_e["added"], KT * (s0 - 2) + d + 1 + 4 * KT * i)
                        dve.scalar_tensor_tensor(xT[:, d, :], ps[:, 4 + d % 4, :], mod[:, 40 + d:41 + d],
                                                 xT[:, d, :], ALU.mult, ALU.add).then_inc(s_e["added"], 1)

            peer_dve(0, has_o=False)
            peer_dve(1)
            with dve.Fori(0, PEER_STEPS // 4 - 1) as i:
                for q in range(4):
                    peer_dve(2 + q, i)
            for s in range(PEER_STEPS - 2, PEER_STEPS):
                peer_dve(s, splits=2 if s < PEER_STEPS - 1 else 1)
            peer_dve(PEER_STEPS, has_a=False, splits=0)
            norm("final1", lambda k: xT[:, k, :], KT, dst=lambda k: xT[:, k, :])
            dve.wait_ge(s_norm["t"], n_at("final1", "t") + KT)
            chain(dve.memset(hp[:, :, 0:PAD], 0.0))
            dve.memset(hp[:, :, PAD + T:2 * PAD + T], 0.0).then_inc(s_p["filled"], 1)
            norm("mix0", lambda k: xT[:, k, :], KT, dst=lambda k: hp[:, k, PAD:PAD + T])
            split_lo_at(dve, C_POOL)
            pool_windows(dve, (2, 3), lambda op: chain(op), wbuf, "dve")
            split_lo_at(dve, C_POOL + 1)
            split_lo_at(dve, C_POOL + 2)
            for t in range(KT):
                dve.wait_ge(s_p["proj"], t + 1)
                dve.scalar_tensor_tensor(xT[:, t, :], ps[:, t % 4, :], col("pool_scale", t), xT[:, t, :],
                                         ALU.mult, ALU.add).then_inc(s_p["added"], 1)
            dve.wait_ge(s_p["added"], KT)

            def ffn_dve(l, c, s0, i=0, has_a=True, splits=2, has_o=True):
                s = s_f[l]

                def add(d):
                    dve.wait_ge(s["o"], KT * (s0 - 1) + d + 1 + 2 * KT * i)
                    if s0 >= 2:
                        dve.wait_ge(s["added"], KT * (s0 - 2) + d + 1 + 2 * KT * i)
                    dve.tensor_tensor(xT[:, d, :], xT[:, d, :], ps[:, 4 + d % 4, :], ALU.add).then_inc(s["added"], 1)

                for q in range(2):
                    k = c + 2 * s0 + 1 + q
                    if q < splits:
                        split_lo(dve, k, CHUNK if is_up(k - c) else D, i, 4)
                    if has_o:
                        for d in range(4 * q, 4 * q + 4):
                            add(d)
                if has_a:
                    b0 = VEC[f"conv{l}"][0]

                    def cv(j):
                        if isinstance(i, int):
                            return vec[:, b0 + 4 * s0 + j:b0 + 4 * s0 + j + 1]
                        return vec[:, bass.ds(b0 + 4 * s0 + j + 8 * i, 1)]

                    g, u = ps[:, 2 * (s0 % 2), :], ps[:, 2 * (s0 % 2) + 1, :]
                    y = gcv[s0 % 2]
                    dve.wait_ge(s["proj"], 2 * s0 + 2 + 4 * i)
                    chain(dve.tensor_scalar(y[:, :], g, cv(1), cv(3), ALU.mult, ALU.add))
                    chain(dve.scalar_tensor_tensor(y[:, 1:T], g[:, 0:T - 1], cv(0), y[:, 1:T], ALU.mult, ALU.add))
                    dve.scalar_tensor_tensor(y[:, 0:T - 1], g[:, 1:T], cv(2), y[:, 0:T - 1], ALU.mult,
                                             ALU.add).then_inc(s["conv"], 1)
                    dve.wait_ge(s["gelu"], s0 + 1 + 2 * i)
                    if s0 >= 2:
                        dve.wait_ge(s["lo"], s0 - 1 + 2 * i)
                    dve.tensor_tensor(fa[s0 % 2][:, :], gel[s0 % 2][:, :], u, ALU.mult).then_inc(s["act"], 1)
                    dve.wait_ge(s["hi"], s0 + 1 + 2 * i)
                    dve.tensor_tensor(faL[s0 % 2][:, :], fa[s0 % 2][:, :], faH[s0 % 2][:, :],
                                      ALU.subtract).then_inc(s["lo"], 1)

            def ffn_vector(l, c):
                ffn_dve(l, c, 0, splits=0, has_o=False)
                split_lo(dve, c + 2, D)
                ffn_dve(l, c, 1)
                n0 = chain.n
                with dve.Fori(0, FT // 2 - 2) as i:
                    chain.n = n0 + 4 * i
                    for q in range(2):
                        ffn_dve(l, c, 2 + q, i)
                chain.n = n0 + 4 * (FT // 2 - 2)
                ffn_dve(l, c, FT - 2)
                ffn_dve(l, c, FT - 1, splits=1)
                ffn_dve(l, c, FT, has_a=False, splits=0)

            norm("ffn0", lambda k: xT[:, k, :], KT, dstL=hL, dstH=hH)
            ffn_vector(0, C_FFN1)
            split_lo_at(dve, C_QKV)
            split_lo_at(dve, C_QKV + 1)
            dve.wait_ge(s_f[0]["added"], KT * FT)
            norm("mix1", lambda k: xT[:, k, :], KT, dstL=hL, dstH=hH)
            dve.wait_ge(ld_const, 80)
            rope_tables(s_td, lambda q: rope_d[:, q, :], posi[:, :], col("inv64"), col("sign64"))
            for t in range(16):
                if t % 2 == 0:
                    split_lo_at(dve, C_QKV + t // 2 + 2)
                dve.wait_ge(s_dr["perm"], t + 1)
                rope(dqk[:, t, :], ps[:, 2 + t % 2, :], lambda q: rope_d[:, q, :], P, s_dr["roped"])
                dve.wait_ge(s_dr["roped"], t + 1)
            for j in range(16):
                c, tt = j // TT, j % TT
                if tt == 0:
                    split_lo_at(dve, C_QKV + 8 + c + 2)
                dve.wait_ge(s_dv["v"], j + 1)
                dve.tensor_copy(dv[:, tt, c * 256:(c + 1) * 256], ps[:, 4 + j % 2, 0:256]).then_inc(s_dv["copied"], 1)
            for q in range(2):
                op = dve.tensor_tensor_reduce(out=sinkv[:, 0:HD], in0=lams[:, 2 * q, :], in1=lams[:, 2 * q + 1, :],
                                              scale=1.0, scalar=0.0, op0=ALU.mult, op1=ALU.add,
                                              accum_out=small[:, q:q + 1])
                if q == 0:
                    chain(op)
                else:
                    op.then_inc(s_da["lam"], 1)
            dve.wait_ge(s_da["lam"], 2)
            chain(dve.tensor_tensor(small[:, 4:5], small[:, 3:4], small[:, 2:3], ALU.subtract))
            chain(dve.tensor_scalar(small[:, 5:6], small[:, 4:5], -LAM_INIT, None, ALU.add))

            def diff_probs(u):
                p0, p1 = scr[:, 2 * (u % 2), :], scr[:, 2 * (u % 2) + 1, :]
                dve.wait_ge(s_da["exp"], 2 * u + 2)
                for c in range(2):
                    chain(dve.reciprocal(stats[:, 4 * c + 3, u:u + 1], stats[:, 4 * c + 2, u:u + 1]))
                chain(dve.tensor_tensor(stats[:, 7, u:u + 1], stats[:, 7, u:u + 1], small[:, 5:6], ALU.mult))
                chain(dve.tensor_scalar(p1, p1, stats[:, 7, u:u + 1], None, ALU.mult))
                dve.scalar_tensor_tensor(p0, p0, stats[:, 3, u:u + 1], p1, ALU.mult,
                                         ALU.add).then_inc(s_da["probs"], 1)

            for u in range(DIFF_H * TT):
                for c in range(2):
                    dve.wait_ge(s_da["scores"], 2 * u + c + 1)
                    chain(dve.reduce_max(stats[:, 4 * c, u:u + 1], ps[:, 2 * (u % 2) + c, :], AX))
                    dve.tensor_scalar(stats[:, 4 * c + 1, u:u + 1], stats[:, 4 * c, u:u + 1], -(HD ** -0.5), None,
                                      ALU.mult).then_inc(s_da["negmax"], 1)
                if u >= 1:
                    diff_probs(u - 1)
            diff_probs(DIFF_H * TT - 1)
            def subln_var(b):
                dve.wait_ge(s_dn["sum"], 2 * b + 2)
                chain(dve.tensor_scalar(dqk[:, 8 + 2 * b:10 + 2 * b, :], ps[:, 2 * (b % 2):2 * (b % 2) + 2, :], 1.0 / P,
                                        SUBLN_EPS, ALU.mult, ALU.add))
                dve.reciprocal(sub_root(b), dqk[:, 8 + 2 * b:10 + 2 * b, :]).then_inc(s_dn["rec"], 1)

            subln_var(0)
            for b in range(DIFF_H // 2):
                if b + 1 < DIFF_H // 2:
                    subln_var(b + 1)
                var, tmp = dqk[:, 8 + 2 * b:10 + 2 * b, :], scr[:, 2 * (b % 2):2 * (b % 2) + 2, :]
                y = dqk[:, 2 * b:2 * b + 2, :]
                dve.wait_ge(s_dn["root"], b + 1)
                chain(dve.tensor_tensor(tmp, var, sub_root(b), ALU.mult))
                chain(dve.scalar_tensor_tensor(tmp, tmp, -0.5 * (1.0 - LAM_INIT), sub_root(b), ALU.mult, ALU.mult))
                chain(dve.scalar_tensor_tensor(tmp, tmp, 1.5 * (1.0 - LAM_INIT), sub_root(b), ALU.add, ALU.mult))
                dve.scalar_tensor_tensor(y, y, col("subln"), tmp, ALU.mult, ALU.mult).then_inc(s_dn["yn"], 1)
            for k in range(4):
                split_lo_at(dve, C_WO + k + 2)
                for j in range(2):
                    t = 2 * k + j
                    dve.wait_ge(s_wo2["proj"], t + 1)
                    dve.tensor_tensor(xT[:, t, :], xT[:, t, :], ps[:, 4 + t % 4, :], ALU.add).then_inc(s_wo2["added"], 1)
            dve.wait_ge(s_wo2["added"], KT)
            norm("ffn1", lambda k: xT[:, k, :], KT, dstL=hL, dstH=hH)
            ffn_vector(1, C_FFN2)
            dve.wait_ge(s_f[1]["added"], KT * FT)
            norm("final2", lambda k: xT[:, k, :], KT, dst=lambda k: xT[:, k, :])

        @block.gpsimd
        def _(pool):
            pool_chain = Chain(pool, g_chain)

            def norm_low(name, nkt, dstH, dstL, src=None):
                for k in range(nkt):
                    pool.wait_ge(s_norm["hi"], n_at(name, "hi") + k + 1)
                    pool.tensor_tensor(dstL[:, k, :], norm_out(k) if src is None else src(k), dstH[:, k, :],
                                       ALU.subtract).then_inc(s_norm["lo"], 1)

            for b in range(2):
                pool.wait_ge(s_rn["hi"], b + 1)
                pool.tensor_tensor(hL[:, 4 + 2 * b:6 + 2 * b, :], qk[:, 2 * b:2 * b + 2, :],
                                   hH[:, 4 + 2 * b:6 + 2 * b, :], ALU.subtract).then_inc(s_rn["lo"], 1)
            norm_low("normq", 2, qnH, qnL, lambda k: lat[:, k, :])
            norm_low("normkv", 1, kvH, kvL, lambda k: lat[:, 2, :])
            picks = pick_buffers()
            for tt in range(TT):
                f = topf[:, tt, :, :].rearrange("p (h two) a -> p h two a", two=2)
                for half in range(2):
                    pool.wait_ge(s_q["hits"], 2 * tt + half + 1)
                    e4 = picks[half].rearrange("p (h k) a -> p h k a", h=PEER_H)
                    pool.tensor_tensor(e4, e4, f[:, :, half, :].unsqueeze(2).broadcast_to([P, PEER_H, TOPK, TOPK]),
                                       ALU.mult).then_inc(s_q["spread"], 1)
            pool.wait_ge(s_q["tcopied"], 3 * TT)
            with pool.Fori(0, T // 16) as i:
                for par in range(4):
                    pool.wait_ge(s_w["hits"], 4 * i + par + 1)
                    pool.tensor_tensor(oneI[par][:, :, :], oneI[par][:, :, :],
                                       fromsel[:, 2, bass.ds(i * 16 + 4 * par, 4)].unsqueeze(2)
                                       .broadcast_to([P, 4, P]), ALU.mult).then_inc(s_w["ones"], 1)
            pool_windows(pool, (0, 1), lambda op: pool_chain(op), wbuf2, "pool")
            norm_low("ffn0", KT, hH, hL)
            norm_low("mix1", KT, hH, hL)
            for b in range(DIFF_H // 2):
                pool.wait_ge(s_dn["hi"], b + 1)
                pool.tensor_tensor(hL[:, 2 * b:2 * b + 2, :], dqk[:, 2 * b:2 * b + 2, :], hH[:, 2 * b:2 * b + 2, :],
                                   ALU.subtract).then_inc(s_dn["lo"], 1)
            norm_low("ffn1", KT, hH, hL)

        @block.tensor
        def _(pe):
            def norm(name, nkt):
                s = s_norm
                for k in range(nkt):
                    pe.wait_ge(s["sq"], n_at(name, "sq") + k + 1)
                    pe.matmul(ps[:, norm_bank(name), :], tab[:, ONES, :], scr[:, k % 2, :], start=k == 0,
                              stop=k == nkt - 1).then_inc(s["sum"], 1)

            def chunk(k, i=0, per=0):
                pe.wait_ge(w_split, k + 1 + i * per)

            def tile(k, j, dst, done, arriving=None):
                product(pe, k, dst, slice(j * P, (j + 1) * P), KT, 256, hH, hL, done, j == 0, arriving)

            def halves_of(name):
                return lambda q: (s_norm["lo"], n_at(name, "lo") + q + 1)

            def mod_cols(bank, first, weights, n):
                for f in range(n):
                    m = pe.matmul(ps[:, bank, first + f:first + f + 1], weights[:, f * P:(f + 1) * P],
                                  tab[:, ONES, 0:1], start=True, stop=True)
                m.then_inc(s_ada["cols"], 1)

            pe.wait_ge(ld_const, 64)
            norm("norm1", KT)
            pe.wait_ge(s_ada["summed"], KT)
            mod_cols(0, 0, ada_sum1, 16)
            pe.wait_ge(s_ada["mod"], 1)
            for t in range(4):
                if t % 2 == 0:
                    chunk(C_LAT + t // 2)
                if t >= 2:
                    pe.wait_ge(s_lat["copied"], t - 1)
                if t < 2:
                    tile(C_LAT, t, ps[:, t % 2, :], s_lat["proj"], halves_of("norm1") if t == 0 else None)
                else:
                    n = P if t == 2 else MLA_QK
                    product(pe, C_KV, ps[0:n, t % 2, :], slice((t - 2) * P, (t - 2) * P + n), KT, 224, hH, hL,
                            s_lat["proj"], t == 2)
            for t in range(9):
                if t < 8:
                    if t % 2 == 0:
                        chunk(C_RQK + t // 2)
                    if t >= 2:
                        pe.wait_ge(s_rr["copied"], t - 1)
                    else:
                        pe.wait_ge(s_lat["copied"], t + 3)
                    tile(C_RQK + t // 2, t % 2, ps[:, t % 2, :], s_rr["proj"])
                if t >= 1:
                    pe.wait_ge(s_rr["copied"], t)
                    if t >= 3:
                        pe.wait_ge(s_rr["roped"], t - 2)
                    pe.matmul(ps[:, 2 + (t - 1) % 2, :], tab[:, SWAP64, :], qk[:, t - 1, :], start=True,
                              stop=True).then_inc(s_rr["perm"], 1)
            norm("normq", 2)
            for t in range(4):
                if t % 2 == 0:
                    chunk(C_RG + t // 2)
                if t >= 2:
                    pe.wait_ge(s_rp["gate"], t - 1)
                tile(C_RG + t // 2, t % 2, ps[:, t % 2, :], s_rp["proj"])
            norm("normkv", 1)
            for j in range(8):
                c, tt = C_RV + j // TT, j % TT
                if tt == 0:
                    chunk(c)
                if j >= 2:
                    pe.wait_ge(s_rp["value"], j - 1)
                wh = wH[c % SLOTS][:, :].rearrange("p (k n) -> p k n", k=KT)
                wl = wL[c % SLOTS][:, :].rearrange("p (k n) -> p k n", k=KT)
                rows = slice(tt * P, (tt + 1) * P)
                for k in range(KT):
                    m = three(pe, ps[:, 4 + j % 2, 0:256], hH[:, k, rows], hL[:, k, rows], wh[:, k, :], wl[:, k, :],
                              k == 0, k == KT - 1, tt == 0 and k == 0)
                m.then_inc(s_rp["proj"], 1)
            pe.wait_ge(s_rr["roped"], 8)
            pe.wait_ge(s_rp["gate"], 4)
            pe.wait_ge(s_rp["value"], 8)

            def ret_y(u):
                h, J = u // TT, u % TT
                m, half = h // 2, (h % 2) * RET_D
                pe.wait_ge(s_rt["decayed"], u + 1)
                if m >= 2 and u % (2 * TT) == 0:
                    pe.wait_ge(s_rt["ycopied"], m - 1)
                pe.matmul(ps[half:half + RET_D, 4 + m % 2, J * P:T], rv[:, J, h * RET_D:(h + 1) * RET_D],
                          scr[:, 1 + u % 2, 0:T - J * P], start=J == 0, stop=J == TT - 1).then_inc(s_rt["y"], 1)

            def late_mod(g):
                pe.wait_ge(s_ada["summed"], KT + 8 * (g + 1))
                mod_cols(3, 16 + 8 * g, ada_sum, 8)

            for u in range(RET_H * TT):
                h, J = u // TT, u % TT
                half = (h % 2) * RET_D
                if u > 8 and u % 8 == 1:
                    late_mod(u // 8 - 1)
                if u >= 2:
                    pe.wait_ge(s_rt["decayed"], u - 1)
                pe.matmul(ps[:, u % 2, 0:T - J * P], qk[half:half + RET_D, 4 + h // 2, J * P:(J + 1) * P],
                          qk[half:half + RET_D, h // 2, J * P:T], start=True, stop=True).then_inc(s_rt["scores"], 1)
                if u >= 1:
                    ret_y(u - 1)
            ret_y(RET_H * TT - 1)
            late_mod(3)
            for m in range(4):
                pe.wait_ge(s_rt["ycopied"], m + 1)
                pe.matmul(ps[:, (0, 1, 6, 7)[m], :], tab[:, BLOCKMEAN, :], qk[:, m, :], start=True,
                          stop=True).then_inc(s_rn["mean"], 1)
            for m in range(4):
                pe.wait_ge(s_rn["sq"], m // 2 + 1)
                pe.matmul(ps[:, (4, 5, 2, 3)[m], :], tab[:, BLOCKMEAN, :], qk[:, 4 + m, :], start=True,
                          stop=True).then_inc(s_rn["var"], 1)
            pe.wait_ge(s_lat["copied"], 4)
            pe.wait_ge(s_rn["rec"], 2)
            pe.matmul(ps[0:MLA_QK, 2, :], tab[0:MLA_QK, SWAP96, 0:MLA_QK], lat[0:MLA_QK, 3, :], start=True,
                      stop=True).then_inc(s_mr["perm"], 1)
            pe.wait_ge(s_norm["lo"], n_at("normkv", "lo") + 1)
            chunk(C_UQ)
            for h in range(MLA_H + 1):
                if h < MLA_H:
                    if h >= 2:
                        pe.wait_ge(s_mr["copied"], h - 1)
                    product(pe, C_UQ, ps[0:MLA_QK, h % 2, :], slice(h * MLA_QK, (h + 1) * MLA_QK), 2,
                            MLA_H * MLA_QK, qnH, qnL, s_mr["proj"], h == 0)
                if h >= 1:
                    pe.wait_ge(s_mr["copied"], h)
                    if h == 2:
                        pe.wait_ge(s_mr["kr"], 1)
                    if h >= 3:
                        pe.wait_ge(s_mr["roped"], h - 2)
                    pe.matmul(ps[0:MLA_QK, 2 + h % 2, :], tab[0:MLA_QK, SWAP96, 0:MLA_QK], qh[0:MLA_QK, h - 1, :],
                              start=True, stop=True).then_inc(s_mr["perm"], 1)
            chunk(C_UKV)
            for h in range(MLA_H):
                if h >= 2:
                    pe.wait_ge(s_mk["kcopied"], h - 1)
                product(pe, C_UKV, ps[:, h % 2, :], slice(h * P, (h + 1) * P), 1, MLA_H * P, kvH, kvL, s_mk["k"],
                        h == 0)
            vh = wH[C_UKV % SLOTS][:, 0:MLA_H * P].rearrange("p (h n) -> p h n", n=P)[:, :, NOPE:P]
            vl = wL[C_UKV % SLOTS][:, 0:MLA_H * P].rearrange("p (h n) -> p h n", n=P)[:, :, NOPE:P]
            for tt in range(TT):
                if tt >= 2:
                    pe.wait_ge(s_mk["vcopied"], tt - 1)
                rows = slice(tt * P, (tt + 1) * P)
                dst = ps[:, 4 + tt % 2, :].rearrange("p (h n) -> p h n", n=MLA_V)
                three(pe, dst, kvH[:, 0, rows], kvL[:, 0, rows], vh, vl, True, True).then_inc(s_mk["v"], 1)
            pe.wait_ge(s_mr["roped"], MLA_H)
            pe.wait_ge(s_mr["kr"], MLA_H + 1)
            pe.wait_ge(s_mk["kcopied"], MLA_H)
            pe.wait_ge(s_mk["vcopied"], TT)

            def mla_rest(u):
                h, qt = u // TT, u % TT
                pe.wait_ge(s_ma["probs"], u + 1)
                if u >= 2:
                    pe.wait_ge(s_ma["pt"], u - 1)
                for k in range(qt + 1):
                    m = pe.transpose(ps[:, 2 + u % 2, k * P:(k + 1) * P], scr[:, u % 2, k * P:(k + 1) * P],
                                     tab[:, IDENT, :])
                m.then_inc(s_ma["trans"], 1)
                if qt == 0 and h >= 1:
                    mla_out(h - 1)

            def mla_out(h):
                pe.wait_ge(s_ma["pt"], TT * (h + 1))
                mm, half = h // 2, (h % 2) * MLA_V
                if mm >= 2 and h % 2 == 0:
                    pe.wait_ge(s_ma["lo"], mm - 1)
                for k in range(TT):
                    m = pe.matmul(ps[half:half + MLA_V, 4 + mm % 2, k * P:T], lat[:, k, h * MLA_V:(h + 1) * MLA_V],
                                  scr[:, 2 + k, k * P:T], start=k == 0, stop=k == TT - 1)
                m.then_inc(s_ma["o"], 1)

            for u in range(MLA_H * TT):
                h, qt = u // TT, u % TT
                n = (qt + 1) * P
                if u >= 2:
                    pe.wait_ge(s_ma["exp"], u - 1)
                pe.matmul(ps[:, u % 2, 0:n], qh[0:MLA_QK, h, qt * P:n], kh[0:MLA_QK, h, 0:n], start=True,
                          stop=True).then_inc(s_ma["scores"], 1)
                if u >= 2:
                    mla_rest(u - 2)
            mla_rest(MLA_H * TT - 2)
            mla_rest(MLA_H * TT - 1)
            mla_out(MLA_H - 1)
            pe.wait_ge(s_ma["lo"], 4)
            pe.wait_ge(s_rn["lo"], 2)
            for t in range(KT):
                if t % 2 == 0:
                    chunk(C_OUT + t // 2)
                if t >= 4:
                    pe.wait_ge(s_wo1["added"], t - 3)
                tile(C_OUT + t // 2, t % 2, ps[:, t % 4, :], s_wo1["proj"])
            norm("norm2", KT)
            pe.wait_ge(s_q["keys"], 16)

            def key_scores(t):
                pe.wait_ge(s_q["copied"], t + 1)
                if t >= 2:
                    pe.wait_ge(s_q["scopied"], t - 1)
                for tt in range(TT):
                    m = pe.matmul(ps[:, 2 + t % 2, tt * P:(tt + 1) * P], qp[t % 2][:, tt * P:(tt + 1) * P],
                                  keysT[:, t % 2, :], start=True, stop=True)
                m.then_inc(s_q["scores"], 1)

            for t in range(16):
                if t % 2 == 0:
                    chunk(C_QUERY + t // 2)
                if t >= 2:
                    pe.wait_ge(s_q["copied"], t - 1)
                tile(C_QUERY + t // 2, t % 2, ps[:, t % 2, :], s_q["proj"], halves_of("norm2") if t == 0 else None)
                if t >= 1:
                    key_scores(t - 1)
            key_scores(15)
            for tt in range(TT):
                for n, r in enumerate((2, 0, 1)):
                    pe.wait_ge(s_q["chosen"], 3 * tt + n + 1)
                    if tt >= 1:
                        pe.wait_ge(s_q["tcopied"], 3 * tt - 2 + n)
                    pe.transpose(ps[:, 4 + r, 0:P], chosen[:, r, :], tab[:, IDENT, :]).then_inc(s_q["trans"], 1)

            def spread_four(par):
                for q in range(4):
                    m = pe.matmul(ps[:, par, q * P:(q + 1) * P], oneJ[par][:, q, :], oneI[par][:, q, :], start=True,
                                  stop=True)
                m.then_inc(s_w["prod"], 1)

            for par in range(4):
                pe.wait_ge(s_w["ones"], par + 1)
                spread_four(par)
            with pe.Fori(1, T // 16) as i:
                for par in range(4):
                    pe.wait_ge(s_w["ones"], 4 * i + par + 1)
                    pe.wait_ge(s_w["copied"], 4 * i + par - 3)
                    spread_four(par)
            pe.wait_ge(s_w["copied"], T // 4)

            def peer_pe(s0, i=0, has_a=True, has_o=True):
                if has_a:
                    k = C_PEER + max(0, 2 * s0 - 1)
                    chunk(k, i, 8)
                    for m in range(2):
                        if s0 >= 2:
                            pe.wait_ge(s_e["gelu"], 2 * (s0 - 2) + m + 1 + 8 * i)
                        tile(k, m, ps[:, 2 * (s0 % 2) + m, :], s_e["a"])
                if has_o:
                    k = C_PEER + (2 * s0 if has_a else 2 * s0 - 1)
                    chunk(k, i, 8)
                    pe.wait_ge(s_e["lo"], 2 * s0 + 8 * i)
                    wh = wH[k % SLOTS][:, :].rearrange("p (m d) -> p m d", m=2)
                    wl = wL[k % SLOTS][:, :].rearrange("p (m d) -> p m d", m=2)
                    par = (s0 - 1) % 2
                    for d in range(KT):
                        if s0 > 1 or d >= 4:
                            pe.wait_ge(s_e["added"], KT * (s0 - 1) + d - 3 + 4 * KT * i)
                        for m in range(2):
                            ins = three(pe, ps[:, 4 + d % 4, :], wh[:, m, d * P:(d + 1) * P],
                                        wl[:, m, d * P:(d + 1) * P], waH[par][m][:, :], waL[par][m][:, :],
                                        m == 0, m == 1, d == 0 and m == 0)
                        ins.then_inc(s_e["o"], 1)

            peer_pe(0, has_o=False)
            peer_pe(1)
            with pe.Fori(0, PEER_STEPS // 4 - 1) as i:
                for q in range(4):
                    peer_pe(2 + q, i)
            for s in range(PEER_STEPS - 2, PEER_STEPS):
                peer_pe(s)
            peer_pe(PEER_STEPS, has_a=False)
            norm("final1", KT)
            norm("mix0", KT)
            chunk(C_POOL)
            wph = wH[C_POOL % SLOTS][:, :].rearrange("p (g k n) -> p g k n", g=4, k=2)
            wpl = wL[C_POOL % SLOTS][:, :].rearrange("p (g k n) -> p g k n", g=4, k=2)
            for t in range(KT):
                g, e = t // 2, slice((t % 2) * P, (t % 2 + 1) * P)
                pe.wait_ge(s_p["lo_dve" if g >= 2 else "lo_pool"], g % 2 + 1)
                if t >= 4:
                    pe.wait_ge(s_p["added"], t - 3)
                for k in range(2):
                    m = three(pe, ps[:, t % 4, :], wph[:, g, k, e], wpl[:, g, k, e], hH[:, 2 * g + k, :],
                              hL[:, 2 * g + k, :], k == 0, k == 1, t == 0 and k == 0)
                m.then_inc(s_p["proj"], 1)

            def ffn_pe(l, c, s0, i=0, has_a=True, has_o=True):
                s = s_f[l]
                if has_a:
                    k = c + max(0, 2 * s0 - 1)
                    chunk(k, i, 4)
                    if s0 >= 2:
                        pe.wait_ge(s["act"], s0 - 1 + 2 * i)
                    for m in range(2):
                        tile(k, m, ps[:, 2 * (s0 % 2) + m, :], s["proj"],
                             halves_of(f"ffn{l}") if c == k and m == 0 else None)
                if has_o:
                    k = c + (2 * s0 if has_a else 2 * s0 - 1)
                    chunk(k, i, 4)
                    pe.wait_ge(s["lo"], s0 + 2 * i)
                    par = (s0 - 1) % 2
                    for d in range(KT):
                        if s0 > 1 or d >= 4:
                            pe.wait_ge(s["added"], KT * (s0 - 1) + d - 3 + 2 * KT * i)
                        cols = slice(d * P, (d + 1) * P)
                        three(pe, ps[:, 4 + d % 4, :], wH[k % SLOTS][:, cols], wL[k % SLOTS][:, cols], faH[par][:, :],
                              faL[par][:, :], True, True, d == 0).then_inc(s["o"], 1)

            def ffn_tensor(l, c):
                ffn_pe(l, c, 0, has_o=False)
                ffn_pe(l, c, 1)
                with pe.Fori(0, FT // 2 - 2) as i:
                    for q in range(2):
                        ffn_pe(l, c, 2 + q, i)
                ffn_pe(l, c, FT - 2)
                ffn_pe(l, c, FT - 1)
                ffn_pe(l, c, FT, has_a=False)

            norm("ffn0", KT)
            ffn_tensor(0, C_FFN1)
            norm("mix1", KT)
            for t in range(17):
                if t < 16:
                    if t % 2 == 0:
                        chunk(C_QKV + t // 2)
                    if t >= 2:
                        pe.wait_ge(s_dr["copied"], t - 1)
                    tile(C_QKV + t // 2, t % 2, ps[:, t % 2, :], s_dr["proj"], halves_of("mix1") if t == 0 else None)
                if t >= 1:
                    pe.wait_ge(s_dr["copied"], t)
                    if t >= 3:
                        pe.wait_ge(s_dr["roped"], t - 2)
                    pe.matmul(ps[:, 2 + (t - 1) % 2, :], tab[:, SWAP64, :], dqk[:, t - 1, :], start=True,
                              stop=True).then_inc(s_dr["perm"], 1)
            for j in range(16):
                c, tt = C_QKV + 8 + j // TT, j % TT
                if tt == 0:
                    chunk(c)
                if j >= 2:
                    pe.wait_ge(s_dv["copied"], j - 1)
                wh = wH[c % SLOTS][:, :].rearrange("p (k n) -> p k n", k=KT)
                wl = wL[c % SLOTS][:, :].rearrange("p (k n) -> p k n", k=KT)
                rows = slice(tt * P, (tt + 1) * P)
                for k in range(KT):
                    m = three(pe, ps[:, 4 + j % 2, 0:256], hH[:, k, rows], hL[:, k, rows], wh[:, k, :], wl[:, k, :],
                              k == 0, k == KT - 1, tt == 0 and k == 0)
                m.then_inc(s_dv["v"], 1)
            pe.wait_ge(s_dr["roped"], 16)
            pe.wait_ge(s_dv["copied"], 16)

            def diff_rest(u):
                h, qt = u // TT, u % TT
                pe.wait_ge(s_da["probs"], u + 1)
                if u >= 2:
                    pe.wait_ge(s_da["at"], u - 1)
                for k in range(TT):
                    m = pe.transpose(ps[:, 4 + u % 2, k * P:(k + 1) * P], scr[:, 2 * (u % 2), k * P:(k + 1) * P],
                                     tab[:, IDENT, :])
                m.then_inc(s_da["trans"], 1)
                if qt == 0 and h >= 1:
                    diff_out(h - 1)

            def diff_out(h):
                pe.wait_ge(s_da["at"], TT * (h + 1))
                if h >= 2:
                    pe.wait_ge(s_dn["sq"], h - 1)
                for k in range(TT):
                    m = pe.matmul(ps[:, 6 + h % 2, :], dv[:, k, h * P:(h + 1) * P], scr[:, 5 + k, :],
                                  start=k == 0, stop=k == TT - 1)
                m.then_inc(s_da["o"], 1)

            for u in range(DIFF_H * TT):
                h, qt = u // TT, u % TT
                for c in range(2):
                    if u >= 2:
                        pe.wait_ge(s_da["exp"], 2 * (u - 2) + c + 1)
                    half = slice(c * HD, (c + 1) * HD)
                    pe.matmul(ps[:, 2 * (u % 2) + c, :], dqk[half, h, qt * P:(qt + 1) * P], dqk[half, 8 + h, :],
                              start=True, stop=True).then_inc(s_da["scores"], 1)
                if u >= 2:
                    diff_rest(u - 2)
            diff_rest(DIFF_H * TT - 2)
            diff_rest(DIFF_H * TT - 1)
            diff_out(DIFF_H - 1)
            for h in range(DIFF_H):
                pe.wait_ge(s_dn["sq"], h + 1)
                if h >= 4:
                    pe.wait_ge(s_dn["rec"], h // 2 - 1)
                pe.matmul(ps[:, h % 4, :], tab[:, ONES, :], dqk[:, 8 + h, :], start=True,
                          stop=True).then_inc(s_dn["sum"], 1)
            for t in range(KT):
                if t % 2 == 0:
                    chunk(C_WO + t // 2)
                if t >= 4:
                    pe.wait_ge(s_wo2["added"], t - 3)
                tile(C_WO + t // 2, t % 2, ps[:, 4 + t % 4, :], s_wo2["proj"],
                     (lambda q: (s_dn["lo"], q // 2 + 1)) if t == 0 else None)
            norm("ffn1", KT)
            ffn_tensor(1, C_FFN2)
            norm("final2", KT)


def ada_chunks(w):
    a = w[:, 0:2 * D].reshape(KT, P, 2 * D)
    b = w[:, 2 * D:].reshape(KT // 2, 2, P, 4, D).transpose(3, 0, 2, 1, 4).reshape(2 * KT, P, 2 * D)
    return np.concatenate([a, b], axis=0)


def constants():
    inv64 = np.float32(ROPE_THETA) ** (-np.arange(0, 64, 2, dtype=np.float32) / np.float32(64))
    inv32 = np.float32(ROPE_THETA) ** (-np.arange(0, 32, 2, dtype=np.float32) / np.float32(32))
    p = np.arange(P)
    f64 = inv64[p % 32].astype(np.float32)
    f96 = np.where((p >= NOPE) & (p < MLA_QK), inv32[(p - NOPE) % 16], 0).astype(np.float32)
    sign64 = np.where(p % 64 < 32, -1, 1).astype(np.float32)
    sign96 = np.where((p - NOPE) % 32 < 16, -1, 1).astype(np.float32)
    tables = np.zeros((P, NTAB, P), np.float32)
    tables[:, ONES] = 1
    tables[:, IDENT] = np.eye(P)
    for a in p:
        tables[a, SWAP64, a ^ 32] = 1
        if NOPE <= a < MLA_QK:
            tables[a, SWAP96, NOPE + ((a - NOPE) ^ 16)] = 1
    tables[:, BLOCKMEAN] = (p[:, None] // RET_D == p[None, :] // RET_D) / RET_D
    tables[:, CAUSAL] = np.where(p[None, :] <= p[:, None], 0, NEG)
    tables[:, IOTA] = p[None, :]
    gamma = 1.0 - 2.0 ** (-5.0 - np.arange(RET_H, dtype=np.float64))
    diff = np.arange(T)[None, :] - p[:, None]
    decays = np.where(diff >= 0, gamma[:, None, None] ** np.maximum(diff, 0), 0) * RET_D ** -0.5
    t = np.arange(T)
    recips = np.stack([1.0 / (np.clip(t + w - w // 2, 0, T) - np.clip(t - w // 2, 0, T)) for w in WINDOWS])
    return {
        "freq": [("inv64", f64), ("inv96", f96), ("sign64", sign64), ("sign96", sign96)],
        "tables": tables,
        "decays": decays.astype(np.float32),
        "recips": np.broadcast_to(recips[None].astype(np.float32), (P, len(WINDOWS), T)),
    }


def layout(inputs):
    g = {k: np.asarray(v) for k, v in inputs.items()}

    def cols(v):
        return v.reshape(-1, P).T

    def chunks(w, n=256):
        k, m = w.shape
        return w.reshape(k // P, P, m // n, n).transpose(2, 1, 0, 3).reshape(m // n, P, (k // P) * n)

    con = constants()
    vec = np.zeros((P, NVEC), np.float32)

    def put(name, v):
        o, n = VEC[name]
        vec[:, o:o + n] = v.reshape(P, n)

    for name, v in (("c", g["c"][0]), ("b_ada", g["b_ada"][0]), ("g_norm1", g["g_norm1"][0]), ("g_q", g["g_q_norm"][0]),
                    ("g_kv", g["g_kv_norm"][0]), ("g_ret", g["g_ret_norm"][0]), ("g_norm2", g["g_norm2"][0]),
                    ("g_final", g["g_final"]), ("mix0", g["mix_norm_2"][0]), ("mix1", g["mix_norm_2"][1]),
                    ("pool_scale", g["pool_scale_2"][0]), ("subln", g["diff_subln_2"][0]),
                    ("ffn0", g["ffn_norm_2"][0]), ("ffn1", g["ffn_norm_2"][1]), ("final", g["final_norm_2"])):
        put(name, cols(v))
    for l in range(2):
        cv = np.concatenate([g["ffn_conv_w_2"][l], g["ffn_conv_b_2"][l][None]])
        put(f"conv{l}", cv.reshape(4, FT, P).transpose(2, 1, 0))
    for name, v in con["freq"]:
        put(name, v)
    w_in = g["w_in"][0]
    o = Q_RANK + P + ROPE
    w_kv = np.concatenate([w_in[:, Q_RANK:Q_RANK + P], w_in[:, Q_RANK:Q_RANK + NOPE], w_in[:, Q_RANK + P:o]], 1)
    rw = RET_H * RET_D
    ret = np.concatenate([w_in[:, o:o + 2 * rw], w_in[:, o + 3 * rw:], w_in[:, o + 2 * rw:o + 3 * rw]], 1)
    up = g["ffn_w_up_2"].reshape(2, KT, P, 2, FT, P).transpose(0, 4, 2, 1, 3, 5).reshape(2, FT, P, CHUNK)
    a = {
        "vectors": vec,
        "tables": con["tables"],
        "decays": con["decays"],
        "recips": con["recips"],
        "positions_l": np.concatenate([g["positions"].reshape(1, T), g["positions_2"].reshape(1, T)], 1),
        "lams": np.concatenate([g[f"diff_lam_{n}_2"].reshape(1, HD) for n in ("q1", "k1", "q2", "k2")], 1),
        "x_l": g["x"][0].T.reshape(KT, P, T).transpose(1, 0, 2),
        "w_ada_l": ada_chunks(g["w_ada"][0]),
        "w_lat0": chunks(w_in[:, 0:Q_RANK])[0],
        "w_lat1": chunks(w_kv, 224)[0],
        "w_ret_l": chunks(ret),
        "w_uq_l": chunks(g["w_uq"][0], MLA_H * MLA_QK)[0],
        "w_ukv_l": g["w_ukv"][0],
        "w_out_l": chunks(g["w_out"][0]),
        "w_query_l": chunks(g["w_query"][0]),
        "keys_l": g["sub_keys"][0].transpose(2, 0, 1),
        "u_l": chunks(g["expert_u"][0].T),
        "v_l": g["expert_v"][0].reshape(PEER_STEPS, 2, P, D).transpose(0, 2, 1, 3).reshape(PEER_STEPS, P, CHUNK),
        "pool_l": g["pool_w_2"][0].reshape(4, 2, P, 256).transpose(2, 0, 1, 3).reshape(P, CHUNK),
        "up_l": up,
        "down_l": g["ffn_w_down_2"].reshape(2, FT, P, D),
        "w_qkv_l": chunks(g["diff_w_qkv_2"][0]),
        "w_o_l": chunks(g["diff_w_o_2"][0]),
    }
    return {k: np.ascontiguousarray(v) for k, v in a.items()}


def kernel(**inputs):
    import concourse.bacc as bacc
    from concourse.bass_utils import run_bass_kernel_spmd

    arrays = layout(inputs)
    nc = bacc.Bacc("TRN2", target_bir_lowering=False, num_devices=1)
    args = {n: nc.dram_tensor(n, a.shape, mybir.dt.from_np(a.dtype), kind="ExternalInput").ap()
            for n, a in arrays.items()}
    args["w_scratch"] = nc.dram_tensor("w_scratch", (NTB, P, P, TB), F32).ap()
    outs = {"out": nc.dram_tensor("out", (P, KT, T), F32, kind="ExternalOutput").ap()}
    build(nc, args, outs)
    r = run_bass_kernel_spmd(nc, [arrays], core_ids=[0])
    y = r.results[0]["out"]
    return np.ascontiguousarray(y.transpose(2, 1, 0).reshape(1, T, D))
```
